# Optimizing a Trainium2 kernel written in Bass

```python
import math
import jax, jax.numpy as jnp
from jax import lax
import numpy as np

D_MODEL = 1024
BATCH = 1
SEQ = 512
DEPTH = 2

SB_HEADS = 8
SB_HEAD_DIM = 64
D_SB = SB_HEADS * SB_HEAD_DIM
MLA_HEADS = 8
MLA_NOPE_DIM = 64
MLA_ROPE_DIM = 32
MLA_QK_DIM = MLA_NOPE_DIM + MLA_ROPE_DIM
MLA_V_DIM = 64
MLA_Q_RANK = 256
MLA_KV_RANK = 128
D_MLA_OUT = MLA_HEADS * MLA_V_DIM
ROPE_THETA = 10000.0
D_MIX = D_SB + D_MLA_OUT
D_IN = 3 * D_SB + MLA_Q_RANK + MLA_KV_RANK + MLA_ROPE_DIM
Q_BLOCK = 128
PEER_HEADS = 8
PEER_N_KEYS = 128
PEER_N_EXPERTS = PEER_N_KEYS * PEER_N_KEYS
PEER_KEY_DIM = 256
PEER_HALF = PEER_KEY_DIM // 2
PEER_TOPK = 16
TOKEN_CHUNK = 128
DEEPNORM_ALPHA = (2.0 * DEPTH) ** 0.25
DEEPNORM_BETA = (8.0 * DEPTH) ** -0.25
LN_EPS = 1e-5
RMS_EPS = 1e-6

kernel_name = "hymba_sb_mla_peer_deepnorm"

def layer_norm(x, g, b):
    xf = x.astype(jnp.float32)
    mu = jnp.mean(xf, axis=-1, keepdims=True)
    var = jnp.mean(jnp.square(xf - mu), axis=-1, keepdims=True)
    return ((xf - mu) * lax.rsqrt(var + LN_EPS) * g + b).astype(x.dtype)

def rms_norm(x, g):
    xf = x.astype(jnp.float32)
    return (xf * lax.rsqrt(jnp.mean(jnp.square(xf), axis=-1, keepdims=True) + RMS_EPS) * g).astype(x.dtype)

def apply_rope(x, cos, sin):
    half = x.shape[-1] // 2
    x1, x2 = x[..., :half], x[..., half:]
    return jnp.concatenate([x1 * cos - x2 * sin, x2 * cos + x1 * sin], axis=-1).astype(x.dtype)

def stick_breaking_attention(q, k, v):
    S, d = q.shape[2], q.shape[3]
    scale = 1.0 / math.sqrt(d)
    outs = []
    for i in range(S // Q_BLOCK):
        q0, end = i * Q_BLOCK, (i + 1) * Q_BLOCK
        z = jnp.einsum('bhqd,bhkd->bhqk', q[:, :, q0:end], k[:, :, :end]).astype(jnp.float32) * scale
        t_idx = q0 + jnp.arange(Q_BLOCK)[:, None]
        s_idx = jnp.arange(end)[None, :]
        causal = s_idx < t_idx
        log_1m = jnp.where(causal, jax.nn.log_sigmoid(-z), 0.0)
        tail = lax.cumsum(log_1m, axis=3, reverse=True) - log_1m
        w = jnp.where(causal, jnp.exp(jax.nn.log_sigmoid(z) + tail), 0.0)
        outs.append(jnp.einsum('bhqk,bhkd->bhqd', w.astype(v.dtype), v[:, :, :end]))
    return jnp.concatenate(outs, axis=2)

def causal_softmax_attention(q, k, v):
    S, d = q.shape[2], q.shape[3]
    scale = 1.0 / math.sqrt(d)
    outs = []
    for i in range(S // Q_BLOCK):
        q0, end = i * Q_BLOCK, (i + 1) * Q_BLOCK
        s = jnp.einsum('bhqd,bhkd->bhqk', q[:, :, q0:end], k[:, :, :end]).astype(jnp.float32) * scale
        causal = jnp.arange(end)[None, :] <= (q0 + jnp.arange(Q_BLOCK)[:, None])
        p = jax.nn.softmax(jnp.where(causal, s, -jnp.inf), axis=-1)
        outs.append(jnp.einsum('bhqk,bhkd->bhqd', p.astype(v.dtype), v[:, :, :end]))
    return jnp.concatenate(outs, axis=2)

def hybrid_mixer(x, w_in, g_cq, w_uq, g_ckv, w_ukv, w_o, cos, sin):
    B, S, _ = x.shape
    h = x @ w_in
    cuts = [D_SB, 2 * D_SB, 3 * D_SB, 3 * D_SB + MLA_Q_RANK, 3 * D_SB + MLA_Q_RANK + MLA_KV_RANK]
    sb_q, sb_k, sb_v, c_q, c_kv, k_r = jnp.split(h, cuts, axis=-1)

    def heads(t, n):
        return t.reshape(B, S, n, -1).transpose(0, 2, 1, 3)

    o_sb = stick_breaking_attention(heads(sb_q, SB_HEADS), heads(sb_k, SB_HEADS), heads(sb_v, SB_HEADS))
    o_sb = o_sb.transpose(0, 2, 1, 3).reshape(B, S, D_SB)

    q = (rms_norm(c_q, g_cq) @ w_uq).reshape(B, S, MLA_HEADS, MLA_QK_DIM)
    q_nope, q_rope = q[..., :MLA_NOPE_DIM], q[..., MLA_NOPE_DIM:]
    q_rope = apply_rope(q_rope, cos[:, None, :], sin[:, None, :])
    k_rope = apply_rope(k_r, cos, sin)
    kv = (rms_norm(c_kv, g_ckv) @ w_ukv).reshape(B, S, MLA_HEADS, MLA_NOPE_DIM + MLA_V_DIM)
    k_nope, v_mla = kv[..., :MLA_NOPE_DIM], kv[..., MLA_NOPE_DIM:]
    q_full = jnp.concatenate([q_nope, q_rope], axis=-1)
    k_full = jnp.concatenate([k_nope, jnp.broadcast_to(k_rope[:, :, None, :], (B, S, MLA_HEADS, MLA_ROPE_DIM))], axis=-1)
    o_mla = causal_softmax_attention(q_full.transpose(0, 2, 1, 3), k_full.transpose(0, 2, 1, 3), v_mla.transpose(0, 2, 1, 3))
    o_mla = o_mla.transpose(0, 2, 1, 3).reshape(B, S, D_MLA_OUT)

    return jnp.concatenate([o_sb, o_mla], axis=-1) @ w_o

def peer_ffn(x, w_q, sub_keys, u_tab, v_tab):
    B, S, D = x.shape
    K = PEER_TOPK
    q = (x @ w_q).reshape(B, S, PEER_HEADS, 2, PEER_HALF)
    scores = jnp.einsum('bshcd,hcnd->bshcn', q, sub_keys).astype(jnp.float32)
    s_half, i_half = lax.top_k(scores, K)
    cand = (s_half[..., 0, :, None] + s_half[..., 1, None, :]).reshape(B, S, PEER_HEADS, K * K)
    s_top, c_idx = lax.top_k(cand, K)
    e_idx = (jnp.take_along_axis(i_half[..., 0, :], c_idx // K, axis=-1) * PEER_N_KEYS
             + jnp.take_along_axis(i_half[..., 1, :], c_idx % K, axis=-1))
    gate = jax.nn.softmax(s_top, axis=-1)
    n_chunks = (B * S) // TOKEN_CHUNK
    xs = x.reshape(n_chunks, TOKEN_CHUNK, D)
    idx = e_idx.reshape(n_chunks, TOKEN_CHUNK, PEER_HEADS * K)
    gs = gate.reshape(n_chunks, TOKEN_CHUNK, PEER_HEADS * K).astype(x.dtype)

    def chunk(args):
        xc, ic, gc = args
        u = jnp.take(u_tab, ic, axis=0)
        a = gc * jax.nn.gelu(jnp.einsum('td,tkd->tk', xc, u), approximate=False)
        v = jnp.take(v_tab, ic, axis=0)
        return jnp.einsum('tk,tkd->td', a, v)

    return lax.map(chunk, (xs, idx, gs)).reshape(B, S, D)

def setup_inputs(seed: int = 0) -> dict:
    key = jax.random.key(seed)
    ks = jax.random.split(key, 16)
    f32 = jnp.float32
    nrm = lambda k, shape: jax.random.normal(k, shape, f32)
    x = nrm(ks[0], (BATCH, SEQ, D_MODEL))
    col_scale = jnp.concatenate([jnp.ones((2 * D_SB,), f32), jnp.full((D_SB,), DEEPNORM_BETA, f32),
                                 jnp.ones((D_IN - 3 * D_SB,), f32)])
    w_in = nrm(ks[1], (DEPTH, D_MODEL, D_IN)) * D_MODEL ** -0.5 * col_scale
    g_cq = 1.0 + 0.02 * nrm(ks[2], (DEPTH, MLA_Q_RANK))
    w_uq = nrm(ks[3], (DEPTH, MLA_Q_RANK, MLA_HEADS * MLA_QK_DIM)) * MLA_Q_RANK ** -0.5
    g_ckv = 1.0 + 0.02 * nrm(ks[4], (DEPTH, MLA_KV_RANK))
    kv_scale = jnp.concatenate([jnp.ones((MLA_NOPE_DIM,), f32), jnp.full((MLA_V_DIM,), DEEPNORM_BETA, f32)])
    w_ukv = (nrm(ks[5], (DEPTH, MLA_KV_RANK, MLA_HEADS, MLA_NOPE_DIM + MLA_V_DIM)) * MLA_KV_RANK ** -0.5
             * kv_scale).reshape(DEPTH, MLA_KV_RANK, MLA_HEADS * (MLA_NOPE_DIM + MLA_V_DIM))
    w_o = nrm(ks[6], (DEPTH, D_MIX, D_MODEL)) * D_MIX ** -0.5 * DEEPNORM_BETA
    ln1_g = 1.0 + 0.02 * nrm(ks[7], (DEPTH, D_MODEL))
    ln1_b = 0.02 * nrm(ks[8], (DEPTH, D_MODEL))
    peer_wq = nrm(ks[9], (DEPTH, D_MODEL, PEER_HEADS * PEER_KEY_DIM)) * D_MODEL ** -0.5
    peer_keys = nrm(ks[10], (DEPTH, PEER_HEADS, 2, PEER_N_KEYS, PEER_HALF)) * PEER_HALF ** -0.5
    peer_u = nrm(ks[11], (DEPTH, PEER_N_EXPERTS, D_MODEL)) * D_MODEL ** -0.5
    peer_v = nrm(ks[12], (DEPTH, PEER_N_EXPERTS, D_MODEL)) * DEEPNORM_BETA
    ln2_g = 1.0 + 0.02 * nrm(ks[13], (DEPTH, D_MODEL))
    ln2_b = 0.02 * nrm(ks[14], (DEPTH, D_MODEL))
    return {"x": x, "w_in": w_in, "g_cq": g_cq, "w_uq": w_uq, "g_ckv": g_ckv, "w_ukv": w_ukv,
            "w_o": w_o, "ln1_g": ln1_g, "ln1_b": ln1_b, "peer_wq": peer_wq, "peer_keys": peer_keys,
            "peer_u": peer_u, "peer_v": peer_v, "ln2_g": ln2_g, "ln2_b": ln2_b}

def reference(x, w_in, g_cq, w_uq, g_ckv, w_ukv, w_o, ln1_g, ln1_b, peer_wq, peer_keys,
              peer_u, peer_v, ln2_g, ln2_b):
    S = x.shape[1]
    pos = jnp.arange(S, dtype=jnp.float32)
    inv_freq = ROPE_THETA ** (-jnp.arange(0, MLA_ROPE_DIM, 2, dtype=jnp.float32) / MLA_ROPE_DIM)
    ang = pos[:, None] * inv_freq[None, :]
    cos, sin = jnp.cos(ang), jnp.sin(ang)
    for l in range(DEPTH):
        mix = hybrid_mixer(x, w_in[l], g_cq[l], w_uq[l], g_ckv[l], w_ukv[l], w_o[l], cos, sin)
        x = layer_norm(DEEPNORM_ALPHA * x + mix, ln1_g[l], ln1_b[l])
        ffn = peer_ffn(x, peer_wq[l], peer_keys[l], peer_u[l], peer_v[l])
        x = layer_norm(DEEPNORM_ALPHA * x + ffn, ln2_g[l], ln2_b[l])
    return x


_drawn_inputs = setup_inputs


def setup_inputs(seed=0):
    import zlib

    import numpy as np

    out = dict(_drawn_inputs(seed))
    spreads = {}
    factors = {'g_cq': 7.889, 'g_ckv': 5.46}
    for name, (base, spread) in spreads.items():
        noise = np.random.default_rng([zlib.crc32(name.encode()), seed]).standard_normal(out[name].shape)
        drawn = base * np.exp(spread * noise) if base else spread * noise
        out[name] = __import__('jax').numpy.asarray(drawn.astype(out[name].dtype))
    for name, factor in factors.items():
        out[name] = (out[name] * factor).astype(out[name].dtype)
    return out
```

```python
import math
from contextlib import ExitStack, contextmanager

import numpy as np

import concourse.bass as bass
from concourse import mybir

F32 = mybir.dt.float32
F32R = mybir.dt.float32r
U32 = mybir.dt.uint32
ALU = mybir.AluOpType
ACT = mybir.ActivationFunctionType
AX_X = mybir.AxisListType.X

P = 128
DEPTH = 2
S = 512
D = 1024
NT = S // P
ND = D // P
HALF = D // 2
HD = 64
PAIRS = 4
D_SB = 512
Q_RANK = 256
KV_RANK = 128
ROPE = 32
QK = HD + ROPE
LATENT0 = 3 * D_SB
LATENT = Q_RANK + KV_RANK
N_KEYS = 128
P_HEADS = 8
TOPK = 16
ALPHA = (2.0 * DEPTH) ** 0.25
LN_EPS = 1e-5
RMS_EPS = 1e-6
NEG = -3.0e38

PACK = {4: 0, 3: 512, 1: 896, 2: 1024}
PACKED = 1280
SB_AT = {s: PACK[NT - s] for s in range(NT)}
LA_AT = {t: PACK[t + 1] for t in range(NT)}


class Chain:

    def __init__(self, eng, sem, credit=0, passed=None):
        self.passed = passed
        self.eng, self.sem, self.credit, self.base, self.n = eng, sem, credit, credit, 0

    def link(self, instruction):
        instruction.then_inc(self.sem, 1)
        self.n += 1
        self.eng.wait_ge(self.sem, self.base + self.n)

    def link_plain(self, instruction):
        self.link(instruction)
        self.eng.sem_inc(self.passed, 1)

    def turn(self, i, per):
        self.base, self.n, self.per = i * per + self.credit, 0, per

    def turned(self, count):
        assert self.n == self.per, (self.n, self.per)
        self.base, self.n = count * self.per + self.credit, 0


@contextmanager
def phase(nc, names):
    with ExitStack() as ctx:
        sems = [ctx.enter_context(nc.semaphore(n)) for n in names]
        with nc.Block(no_gpsimd_drain=True) as block:
            yield (block, *sems)
        nums = sorted(s.num for s in sems)
        assert nums == list(range(nums[0], nums[0] + len(nums)))
        nc.all_engine_barrier(sems_to_clear=range(nums[0], nums[-1] + 1))


CREDIT = 1


def give_credit(block, sems):
    @block.gpsimd
    def _(pool):
        for sem in sems:
            pool.sem_inc(sem, CREDIT)


def cols(ap, start, n):
    return ap[:, start:start + n]


def make_constants(nc, c, rope_cos, rope_sin):
    with phase(nc, ["filled", "selected", "tables_in"]) as (block, filled, selected, tables_in):
        @block.gpsimd
        def _(pool):
            nc.gpsimd.memset(c.ident[:], 0.0).then_inc(filled, 1)
            nc.gpsimd.memset(c.neg_ones[:], -1.0).then_inc(filled, 1)
            nc.gpsimd.memset(c.neg_mask[:], 0.0).then_inc(filled, 1)
            nc.gpsimd.iota(c.count_keys[:], [[1, N_KEYS]], base=0, channel_multiplier=0,
                           allow_small_or_imprecise_dtypes=True)
            nc.gpsimd.iota(c.count_top[:], [[1, TOPK]], base=0, channel_multiplier=0,
                           allow_small_or_imprecise_dtypes=True)
            nc.gpsimd.memset(c.ones[:], 1.0)
            pool.wait_ge(filled, 3)
            nc.gpsimd.affine_select(out=c.ident[:], in_=c.ident[:], compare_op=ALU.not_equal, fill=1.0,
                                    base=0, pattern=[[-1, P]], channel_multiplier=1)
            nc.gpsimd.affine_select(out=c.neg_tri[:], in_=c.neg_ones[:], compare_op=ALU.is_ge, fill=0.0,
                                    base=0, pattern=[[-1, P]], channel_multiplier=1)
            nc.gpsimd.affine_select(out=c.neg_mask[:], in_=c.neg_mask[:], compare_op=ALU.is_ge, fill=NEG,
                                    base=0, pattern=[[-1, P]], channel_multiplier=1).then_inc(selected, 1)

        @block.sync
        def _(sp):
            sp.dma_start(c.cos[HD:QK, :], rope_cos).then_inc(tables_in, 16)
            sp.dma_start(c.sin[HD:QK, :], rope_sin).then_inc(tables_in, 16)
            sp.wait_ge(tables_in, 32)


def load_x(nc, c, x):
    with phase(nc, ["x_in"]) as (block, x_in):
        @block.sync
        def _(sp):
            sp.dma_start(c.x[:], x[0].rearrange("(t p) d -> p t d", p=P)).then_inc(x_in, 16)
            sp.wait_ge(x_in, 16)


def store_x(nc, c, out):
    with phase(nc, ["x_out"]) as (block, x_out):
        @block.sync
        def _(sp):
            sp.dma_start(out[0].rearrange("(t p) d -> p t d", p=P), c.x[:]).then_inc(x_out, 16)
            sp.wait_ge(x_out, 16)


def transpose_x(nc, c):
    with phase(nc, ["turned", "copied"]) as (block, turned, copied):
        @block.tensor
        def _(pe):
            for k in range(ND):
                if k >= 4:
                    pe.wait_ge(copied, k - 3)
                for t in range(NT):
                    mm = nc.tensor.transpose(c.psum[:, k % 4, t * P:(t + 1) * P],
                                             c.x[:, t, k * P:(k + 1) * P], c.ident[:])
                mm.then_inc(turned, 1)

        @block.scalar
        def _(act):
            for k in range(ND):
                act.wait_ge(turned, k + 1)
                nc.scalar.copy(c.xt[:, k, :], c.psum[:, k % 4, :]).then_inc(copied, 1)


def split_x(nc, c, x_hi, x_lo):
    with phase(nc, ["high_done", "low_done"]) as (block, high_done, low_done):
        @block.scalar
        def _(act):
            for k in range(ND):
                nc.scalar.copy(x_hi[:, k, :], c.xt[:, k, :]).then_inc(high_done, 1)

        @block.vector
        def _(dve):
            for k in range(ND):
                dve.wait_ge(high_done, k + 1)
                nc.vector.tensor_tensor(x_lo[:, k, :], c.xt[:, k, :], x_hi[:, k, :].bitcast(F32),
                                        ALU.subtract).then_inc(low_done, 1)


def latents(nc, c, m, l, w_in, g_cq, g_ckv):
    with ExitStack() as ctx:
        w = ctx.enter_context(nc.sbuf_tensor("w_lat", [P, ND, LATENT + ROPE], F32))
        w_swap = ctx.enter_context(nc.sbuf_tensor("w_lat_swap", [P, ND, ROPE], F32))
        g = ctx.enter_context(nc.sbuf_tensor("g_lat", [P, 3], F32))
        squares = ctx.enter_context(nc.sbuf_tensor("lat_squares", [P, NT, Q_RANK], F32))
        stat = ctx.enter_context(nc.sbuf_tensor("lat_stat", [P, 2, 2 * NT], F32))
        normed = ctx.enter_context(nc.sbuf_tensor("lat_normed", [P, NT, LATENT], F32))
        rot = ctx.enter_context(nc.sbuf_tensor("lat_rot", [P, S], F32))
        names = ["w_in_", "projected", "roped", "squared", "rooted", "dve_chain", "norm_done", "turned"]
        with phase(nc, names) as (block, loaded, projected, roped, squared, rooted, chain, norm_done, turned):
            wl = w_in[bass.ds(l, 1)].rearrange("o (c p) n -> p (o c) n", p=P)
            rope0 = LATENT0 + LATENT

            @block.sync
            def _(sp):
                sp.dma_start(w[:], wl[:, :, LATENT0:]).then_inc(loaded, 16)
                sp.dma_start(w_swap[:, :, 0:ROPE // 2], wl[:, :, rope0 + ROPE // 2:]).then_inc(loaded, 16)
                sp.dma_start(w_swap[:, :, ROPE // 2:], wl[:, :, rope0:rope0 + ROPE // 2]).then_inc(loaded, 16)
                sp.dma_start(g[:, 0:2], g_cq[bass.ds(l, 1)].rearrange("o (c p) -> p (o c)", p=P),
                             allow_slow_non_contiguous=True).then_inc(loaded, 16)
                sp.dma_start(g[:, 2:3], g_ckv[bass.ds(l, 1)].rearrange("o (c p) -> p (o c)", p=P),
                             allow_slow_non_contiguous=True).then_inc(loaded, 16)

            @block.tensor
            def _(pe):
                pe.wait_ge(loaded, 80)
                for t in range(NT):
                    for k in range(ND):
                        mm = nc.tensor.matmul(c.psum[:, t, 0:LATENT], c.xt[:, k, t * P:(t + 1) * P],
                                              w[:, k, 0:LATENT], start=k == 0, stop=k == ND - 1)
                    mm.then_inc(projected, 1)
                for bank, wr in ((4, w[:, :, LATENT:]), (5, w_swap[:])):
                    for k in range(ND):
                        mm = nc.tensor.matmul(c.psum[HD:QK, bank, :], wr[:, k, :], c.xt[:, k, :],
                                              start=k == 0, stop=k == ND - 1)
                    mm.then_inc(roped, 1)
                pe.wait_ge(norm_done, NT)
                for k in range(3):
                    for t in range(NT):
                        mm = nc.tensor.transpose(c.psum[:, k, t * P:(t + 1) * P],
                                                 normed[:, t, k * P:(k + 1) * P], c.ident[:])
                    mm.then_inc(turned, 1)

            @block.scalar
            def _(act):
                for t in range(NT):
                    act.wait_ge(projected, t + 1)
                    nc.scalar.activation(squares[:, t, :], c.psum[:, t, 0:Q_RANK], ACT.Square,
                                         accum_out=stat[:, 0, t:t + 1]).then_inc(squared, 1)
                    act.wait_ge(squared, 2 * t + 1)
                    nc.scalar.activation(squares[:, t, 0:KV_RANK], c.psum[:, t, Q_RANK:LATENT], ACT.Square,
                                         accum_out=stat[:, 0, NT + t:NT + t + 1]).then_inc(squared, 1)
                act.wait_ge(chain, 2)
                nc.scalar.activation(stat[:, 0, :], stat[:, 1, :], ACT.Sqrt).then_inc(rooted, 1)

            @block.vector
            def _(dve):
                ch = Chain(dve, chain)
                dve.wait_ge(squared, 2 * NT)
                ch.link(nc.vector.tensor_scalar(stat[:, 1, 0:NT], stat[:, 0, 0:NT], 1.0 / Q_RANK, RMS_EPS,
                                                ALU.mult, ALU.add))
                ch.link(nc.vector.tensor_scalar(stat[:, 1, NT:], stat[:, 0, NT:], 1.0 / KV_RANK, RMS_EPS,
                                                ALU.mult, ALU.add))
                dve.wait_ge(rooted, 1)
                ch.link(nc.vector.reciprocal(stat[:, 1, :], stat[:, 0, :]))
                for t in range(NT):
                    nc.vector.tensor_scalar(normed[:, t, 0:Q_RANK], c.psum[:, t, 0:Q_RANK],
                                            stat[:, 1, t:t + 1], None, ALU.mult)
                    nc.vector.tensor_scalar(normed[:, t, Q_RANK:], c.psum[:, t, Q_RANK:LATENT],
                                            stat[:, 1, NT + t:NT + t + 1], None, ALU.mult).then_inc(norm_done, 1)
                dve.wait_ge(roped, 2)
                nc.vector.tensor_tensor(rot[HD:QK, :], c.psum[HD:QK, 4, :], c.cos[HD:QK, :], ALU.mult)
                ch.link(nc.vector.tensor_tensor(m.k_rope[HD:QK, :], c.psum[HD:QK, 5, :], c.sin[HD:QK, :], ALU.mult))
                ch.link(nc.vector.tensor_tensor(m.k_rope[HD:QK, :], m.k_rope[HD:QK, :], rot[HD:QK, :], ALU.add))
                for e in range(2):
                    nc.vector.tensor_copy(m.k_full[HD:QK, e, :], m.k_rope[HD:QK, :])
                for k in range(3):
                    dve.wait_ge(turned, k + 1)
                    ins = nc.vector.tensor_scalar(m.lat_t[:, k, :], c.psum[:, k, :], g[:, k:k + 1], None, ALU.mult)
                ch.link(ins)


def stick_breaking(nc, c, m, l, w_in):
    with ExitStack() as ctx:
        def sb(name, shape):
            return ctx.enter_context(nc.sbuf_tensor(name, shape, F32))
        w = sb("sb_w", [P, 3, ND, P])
        q, k_ = sb("sb_q", [P, S]), sb("sb_k", [P, S])
        v = sb("sb_v", [P, NT, P])
        size = sb("sb_size", [P, 2, PACKED])
        soft = sb("sb_soft", [P, 2, PACKED])
        wts = sb("sb_wts", [P, 2, PACKED])
        names = ["w_here", "projected", "evacuated", "scored", "sized", "logged", "soft_done", "masked",
                 "summed", "weighed", "ready", "mixed", "stored", "act_chain", "passed"]
        with phase(nc, names) as (block, w_here, projected, evacuated, scored, sized, logged, soft_done,
                                  masked, summed, weighed, ready, mixed, stored, act_chain, passed):
            z = [c.flat[:, 1536 * e:1536 * e + PACKED] for e in range(2)]

            @block.sync
            def _(sp):
                with sp.Fori(0, PAIRS) as p:
                    sp.wait_ge(projected, p * 3 + CREDIT)
                    for n in range(3):
                        sp.dma_start(w[:, n], w_in[bass.ds(l, 1), :, bass.ds(p * P + n * D_SB, P)]
                                     .rearrange("o (c p) n -> p (o c) n", p=P)).then_inc(w_here, 16)

            @block.tensor
            def _(pe):
                with pe.Fori(0, PAIRS) as p:
                    pe.wait_ge(w_here, p * 48 + 48)
                    for n in range(2):
                        if n == 0:
                            pe.wait_ge(stored, p + CREDIT)
                        for k in range(ND):
                            mm = nc.tensor.matmul(c.psum[:, 6 + n, :], w[:, n, k, :], c.xt[:, k, :],
                                                  start=k == 0, stop=k == ND - 1)
                        mm.then_inc(projected, 1)
                    pe.wait_ge(evacuated, p * 3 + 1)
                    for t in range(NT):
                        for k in range(ND):
                            mm = nc.tensor.matmul(c.psum[:, 6, t * P:(t + 1) * P],
                                                  c.xt[:, k, t * P:(t + 1) * P], w[:, 2, k, :],
                                                  start=k == 0, stop=k == ND - 1)
                    mm.then_inc(projected, 1)
                    pe.wait_ge(evacuated, p * 3 + 2)
                    for e in range(2):
                        for s in (0, 1, 3, 2):
                            mm = nc.tensor.matmul(cols(z[e], SB_AT[s], S - s * P),
                                                  k_[HD * e:HD * (e + 1), s * P:(s + 1) * P],
                                                  q[HD * e:HD * (e + 1), s * P:], start=s != 3, stop=False,
                                                  skip_group_check=True)
                        mm.then_inc(scored, 1)
                    for e in range(2):
                        pe.wait_ge(masked, p * 2 + e + 1)
                        for j in range(NT):
                            for s in range(j + 1):
                                out = cols(z[e], SB_AT[s] + (j - s) * P, S - j * P)
                                mm = nc.tensor.matmul(out, (c.neg_tri if s == j else c.neg_ones)[:],
                                                      cols(soft[:, e], SB_AT[j], S - j * P),
                                                      start=False, stop=s == j, skip_group_check=True)
                        mm.then_inc(summed, 1)
                    pe.wait_ge(evacuated, p * 3 + 3)
                    for e in range(2):
                        pe.wait_ge(ready, p * 2 + e + 1)
                        for s in range(NT):
                            mm = nc.tensor.matmul(c.psum[HD * e:HD * (e + 1), 7, s * P:],
                                                  v[:, s, HD * e:HD * (e + 1)],
                                                  cols(wts[:, e], SB_AT[s], S - s * P),
                                                  start=s == 0, stop=s == NT - 1, skip_group_check=True)
                    mm.then_inc(mixed, 1)

            @block.scalar
            def _(act):
                with act.Fori(0, PAIRS) as p:
                    act.wait_ge(projected, p * 3 + 1 + CREDIT)
                    nc.scalar.mul(q[:], c.psum[:, 6, :], HD ** -0.5).then_inc(evacuated, 1)
                    act.wait_ge(projected, p * 3 + 2 + CREDIT)
                    nc.scalar.copy(k_[:], c.psum[:, 7, :]).then_inc(evacuated, 1)
                    act.wait_ge(projected, p * 3 + 3 + CREDIT)
                    nc.scalar.copy(v[:].rearrange("p t n -> p (t n)"), c.psum[:, 6, :]).then_inc(evacuated, 1)
                    for e in range(2):
                        act.wait_ge(scored, p * 2 + e + 1)
                        nc.scalar.activation(size[:, e], z[e], ACT.Abs).then_inc(sized, 1)
                        act.wait_ge(sized, p * 2 + e + 1)
                        nc.scalar.activation(size[:, e], size[:, e], ACT.Exp, scale=-1.0).then_inc(act_chain, 1)
                        act.wait_ge(act_chain, p * 2 + e + 1)
                        nc.scalar.activation(size[:, e], size[:, e], ACT.Ln, bias=c.ones[:, 0:1]).then_inc(logged, 1)
                    for e in range(2):
                        act.wait_ge(summed, p * 2 + e + 1)
                        nc.scalar.activation(wts[:, e], z[e], ACT.Exp).then_inc(weighed, 1)
                    act.wait_ge(mixed, p + 1)
                    nc.scalar.copy(m.mixed_t[:, bass.ds(p, 1), :].rearrange("p o t -> p (o t)"),
                                   c.psum[:, 7, :]).then_inc(stored, 1)

            @block.vector
            def _(dve):
                with dve.Fori(0, PAIRS) as p:
                    for e in range(2):
                        dve.wait_ge(logged, p * 2 + e + 1)
                        nc.vector.scalar_tensor_tensor(out=soft[:, e], in0=z[e], scalar=0.0, in1=size[:, e],
                                                       op0=ALU.max, op1=ALU.add).then_inc(soft_done, 1)

            @block.gpsimd
            def _(pool):
                for sem in (projected, stored):
                    pool.sem_inc(sem, CREDIT)
                with pool.Fori(0, PAIRS) as p:
                    for sem, done, tile in ((soft_done, masked, soft), (weighed, ready, wts)):
                        for e in range(2):
                            pool.wait_ge(sem, p * 2 + e + 1)
                            pool.sem_inc(passed, 1)
                            for s in range(NT):
                                diag = cols(tile[:, e], SB_AT[s], P)
                                ins = nc.gpsimd.affine_select(out=diag, in_=diag, compare_op=ALU.is_gt, fill=0.0,
                                                              base=0, pattern=[[1, P]], channel_multiplier=-1)
                            ins.then_inc(done, 1)


def latent_attention(nc, c, m, l, w_uq, w_ukv):
    with ExitStack() as ctx:
        def sb(name, shape):
            return ctx.enter_context(nc.sbuf_tensor(name, shape, F32))
        wq = sb("la_wq", [P, 2, 2, QK])
        wq_swap = sb("la_wq_swap", [P, 2, 2, ROPE])
        wkv = sb("la_wkv", [P, 2, 2, HD])
        q = sb("la_q", [P, 2, S])
        rot = sb("la_rot", [P, 2, 2, S])
        v = sb("la_v", [P, NT, P])
        probs = sb("la_probs", [P, 2, PACKED])
        probs_t = sb("la_probs_t", [P, 2, PACKED])
        peak = sb("la_peak", [P, 2, NT])
        bias = sb("la_bias", [P, 2, NT])
        total = sb("la_total", [P, 2, NT])
        share = sb("la_share", [P, 2, NT])
        scale = QK ** -0.5
        names = ["w_here", "q_made", "k_made", "v_made", "q_out", "k_out", "v_out", "scored", "biased",
                 "exped", "scaled", "turned", "turned_out", "mixed", "stored", "dve_chain"]
        with phase(nc, names) as (block, w_here, q_made, k_made, v_made, q_out, k_out, v_out, scored, biased,
                                  exped, scaled, turned, turned_out, mixed, stored, chain):
            sc = [c.flat[:, 1536 * e:1536 * e + PACKED] for e in range(2)]
            give_credit(block, (v_made, stored, turned_out))

            @block.sync
            def _(sp):
                with sp.Fori(0, PAIRS) as p:
                    sp.wait_ge(v_made, p + CREDIT)
                    uq = w_uq[bass.ds(l, 1), :, bass.ds(p * 2 * QK, 2 * QK)].rearrange(
                        "o (c p) (e n) -> p (o c) e n", p=P, e=2)
                    for k in range(2):
                        sp.dma_start(wq[:, k], uq[:, k]).then_inc(w_here, 16)
                        sp.dma_start(wq_swap[:, k, :, 0:ROPE // 2], uq[:, k, :, HD + ROPE // 2:]).then_inc(w_here, 16)
                        sp.dma_start(wq_swap[:, k, :, ROPE // 2:], uq[:, k, :, HD:HD + ROPE // 2]).then_inc(w_here, 16)
                    sp.dma_start(wkv[:].rearrange("p e h n -> p (e h n)"),
                                 w_ukv[bass.ds(l, 1), :, bass.ds(p * 4 * HD, 4 * HD)]
                                 .rearrange("o p n -> p (o n)")).then_inc(w_here, 16)

            @block.tensor
            def _(pe):
                with pe.Fori(0, PAIRS) as p:
                    pe.wait_ge(w_here, p * 112 + 112)
                    pe.wait_ge(stored, p + CREDIT)
                    pe.wait_ge(turned_out, p * 2 + CREDIT)
                    for e in range(2):
                        for k in range(2):
                            nc.tensor.matmul(c.psum[0:QK, 6, :], wq[:, k, e, :], m.lat_t[:, k, :],
                                             start=k == 0, stop=k == 1)
                        for k in range(2):
                            mm = nc.tensor.matmul(c.psum[HD:QK, 7, :], wq_swap[:, k, e, :], m.lat_t[:, k, :],
                                                  start=k == 0, stop=k == 1)
                        mm.then_inc(q_made, 1)
                        mm = nc.tensor.matmul(c.psum[0:HD, 3 * e, :], wkv[:, e, 0, :], m.lat_t[:, 2, :],
                                              start=True, stop=True)
                        mm.then_inc(k_made, 1)
                        pe.wait_ge(q_out, p * 4 + 2 * e + 2)
                    for t in range(NT):
                        mm = nc.tensor.matmul(c.psum[:, 6, t * P:(t + 1) * P], m.lat_t[:, 2, t * P:(t + 1) * P],
                                              wkv[:, :, 1, :], start=True, stop=True)
                    mm.then_inc(v_made, 1)
                    for e in range(2):
                        pe.wait_ge(k_out, p * 2 + e + 1)
                        for t in (3, 2, 0, 1):
                            mm = nc.tensor.matmul(cols(sc[e], LA_AT[t], (t + 1) * P),
                                                  q[0:QK, e, t * P:(t + 1) * P], m.k_full[0:QK, e, 0:(t + 1) * P],
                                                  start=True, stop=True)
                        mm.then_inc(scored, 1)
                    for e in range(2):
                        pe.wait_ge(scaled, p * 2 + e + 1)
                        for s in range(NT):
                            for t in range(s, NT):
                                mm = nc.tensor.transpose(cols(sc[e], SB_AT[s] + (t - s) * P, P),
                                                         cols(probs[:, e], LA_AT[t] + s * P, P), c.ident[:])
                        mm.then_inc(turned, 1)
                    pe.wait_ge(v_out, p + 1)
                    for e in range(2):
                        pe.wait_ge(turned_out, p * 2 + e + 1 + CREDIT)
                        for s in range(NT):
                            mm = nc.tensor.matmul(c.psum[HD * e:HD * (e + 1), 7, s * P:],
                                                  v[:, s, HD * e:HD * (e + 1)],
                                                  cols(probs_t[:, e], SB_AT[s], S - s * P),
                                                  start=s == 0, stop=s == NT - 1, skip_group_check=True)
                    mm.then_inc(mixed, 1)

            @block.scalar
            def _(act):
                with act.Fori(0, PAIRS) as p:
                    for e in range(2):
                        act.wait_ge(q_made, p * 2 + e + 1)
                        nc.scalar.copy(q[0:HD, e, :], c.psum[0:HD, 6, :]).then_inc(q_out, 1)
                        act.wait_ge(k_made, p * 2 + e + 1)
                        nc.scalar.copy(m.k_full[0:HD, e, :], c.psum[0:HD, 3 * e, :]).then_inc(k_out, 1)
                    act.wait_ge(v_made, p + 1 + CREDIT)
                    nc.scalar.copy(v[:].rearrange("p t n -> p (t n)"), c.psum[:, 6, :]).then_inc(v_out, 1)
                    for e in range(2):
                        act.wait_ge(biased, p * 2 + e + 1)
                        for t in range(NT):
                            at = cols(probs[:, e], LA_AT[t], (t + 1) * P)
                            ins = nc.scalar.activation(at, cols(sc[e], LA_AT[t], (t + 1) * P), ACT.Exp,
                                                       bias=bias[:, e, t:t + 1], scale=scale,
                                                       accum_out=total[:, e, t:t + 1])
                        ins.then_inc(exped, 1)
                    for e in range(2):
                        act.wait_ge(turned, p * 2 + e + 1)
                        nc.scalar.copy(probs_t[:, e], sc[e]).then_inc(turned_out, 1)
                    act.wait_ge(mixed, p + 1)
                    nc.scalar.copy(m.mixed_t[:, bass.ds(p + PAIRS, 1), :].rearrange("p o t -> p (o t)"),
                                   c.psum[:, 7, :]).then_inc(stored, 1)

            @block.vector
            def _(dve):
                ch = Chain(dve, chain)
                with dve.Fori(0, PAIRS) as p:
                    ch.turn(p, 8)
                    for e in range(2):
                        dve.wait_ge(q_made, p * 2 + e + 1)
                        nc.vector.tensor_tensor(rot[HD:QK, e, 0, :], c.psum[HD:QK, 6, :], c.cos[HD:QK, :], ALU.mult)
                        ins = nc.vector.tensor_tensor(rot[HD:QK, e, 1, :], c.psum[HD:QK, 7, :], c.sin[HD:QK, :],
                                                      ALU.mult)
                        ch.link(ins)
                        nc.vector.tensor_tensor(q[HD:QK, e, :], rot[HD:QK, e, 0, :], rot[HD:QK, e, 1, :],
                                                ALU.add).then_inc(q_out, 1)
                    for e in range(2):
                        dve.wait_ge(scored, p * 2 + e + 1)
                        for t in range(NT):
                            diag = cols(sc[e], LA_AT[t] + t * P, P)
                            ins = nc.vector.tensor_tensor(diag, diag, c.neg_mask[:], ALU.add)
                        ch.link(ins)
                        for t in range(NT):
                            ins = nc.vector.reduce_max(peak[:, e, t:t + 1], cols(sc[e], LA_AT[t], (t + 1) * P), AX_X)
                        ch.link(ins)
                        nc.vector.tensor_scalar(bias[:, e, :], peak[:, e, :], -scale, None,
                                                ALU.mult).then_inc(biased, 1)
                    for e in range(2):
                        dve.wait_ge(exped, p * 2 + e + 1)
                        ch.link(nc.vector.reciprocal(share[:, e, :], total[:, e, :]))
                        for t in range(NT):
                            at = cols(probs[:, e], LA_AT[t], (t + 1) * P)
                            ins = nc.vector.tensor_scalar(at, at, share[:, e, t:t + 1], None, ALU.mult)
                        ins.then_inc(scaled, 1)
                ch.turned(PAIRS)


def layer_norm_steps(nc, dve, ch, c, ln, t, act_wait):
    for h in range(2):
        ins = nc.vector.bn_stats(ln.stats[:, t, h, :], c.x[:, t, h * HALF:(h + 1) * HALF])
    ch.link(ins)
    ch.link(nc.vector.bn_aggr(ln.mv[:, t, :], ln.stats[:, t].rearrange("p h s -> p (h s)")))
    nc.vector.tensor_scalar(ln.var[:, t:t + 1], ln.mv[:, t, 1:2], LN_EPS, None, ALU.add).then_inc(ln.var_done, 1)
    dve.wait_ge(ln.rooted, t + 1)
    ch.link(nc.vector.reciprocal(ln.rstd[:, t:t + 1], ln.root[:, t:t + 1]))
    ch.link(nc.vector.tensor_scalar(c.x[:, t, :], c.x[:, t, :], ln.mv[:, t, 0:1], ln.rstd[:, t:t + 1],
                                    ALU.subtract, ALU.mult))
    ch.link(nc.vector.tensor_tensor(c.x[:, t, :], c.x[:, t, :], ln.g[:], ALU.mult))
    ch.link(nc.vector.tensor_tensor(c.x[:, t, :], c.x[:, t, :], ln.b[:], ALU.add))


class Norm:

    def __init__(self, nc, ctx, name):
        def sb(part, shape):
            return ctx.enter_context(nc.sbuf_tensor(f"{name}_{part}", shape, F32))
        self.g, self.b = sb("g", [P, D]), sb("b", [P, D])
        self.stats, self.mv = sb("stats", [P, NT, 2, 6]), sb("mv", [P, NT, 2])
        self.var, self.root, self.rstd = sb("var", [P, NT]), sb("root", [P, NT]), sb("rstd", [P, NT])


def project_out(nc, c, m, l, w_o, ln_g, ln_b):
    with ExitStack() as ctx:
        w = ctx.enter_context(nc.sbuf_tensor("w_out", [P, ND, D], F32))
        ln = Norm(nc, ctx, "ln1")
        with phase(nc, ["w_here", "params_here", "projected", "dve_chain", "var_done", "rooted"]) as (
                block, w_here, params_here, projected, chain, ln.var_done, ln.rooted):
            @block.sync
            def _(sp):
                sp.dma_start(w[:], w_o[bass.ds(l, 1)].rearrange("o (c p) n -> p (o c) n", p=P)).then_inc(w_here, 16)
                sp.dma_start(ln.g[:], ln_g[bass.ds(l, 1)].broadcast_to([P, D])).then_inc(params_here, 16)
                sp.dma_start(ln.b[:], ln_b[bass.ds(l, 1)].broadcast_to([P, D])).then_inc(params_here, 16)

            @block.tensor
            def _(pe):
                pe.wait_ge(w_here, 16)
                for t in range(NT):
                    for h in range(2):
                        for k in range(ND):
                            mm = nc.tensor.matmul(c.psum[:, 2 * t + h, :], m.mixed_t[:, k, t * P:(t + 1) * P],
                                                  w[:, k, h * HALF:(h + 1) * HALF], start=k == 0, stop=k == ND - 1)
                        mm.then_inc(projected, 1)

            @block.vector
            def _(dve):
                ch = Chain(dve, chain)
                dve.wait_ge(params_here, 32)
                for t in range(NT):
                    for h in range(2):
                        dve.wait_ge(projected, 2 * t + h + 1)
                        half = c.x[:, t, h * HALF:(h + 1) * HALF]
                        ins = nc.vector.scalar_tensor_tensor(out=half, in0=half, scalar=ALPHA,
                                                             in1=c.psum[:, 2 * t + h, :], op0=ALU.mult, op1=ALU.add)
                    ch.link(ins)
                    layer_norm_steps(nc, dve, ch, c, ln, t, None)

            @block.scalar
            def _(act):
                for t in range(NT):
                    act.wait_ge(ln.var_done, t + 1)
                    nc.scalar.activation(ln.root[:, t:t + 1], ln.var[:, t:t + 1], ACT.Sqrt).then_inc(ln.rooted, 1)


def residual_norm(nc, c, l, ffn, ln_g, ln_b):
    with ExitStack() as ctx:
        ln = Norm(nc, ctx, "ln2")
        with phase(nc, ["params_here", "dve_chain", "var_done", "rooted"]) as (
                block, params_here, chain, ln.var_done, ln.rooted):
            @block.sync
            def _(sp):
                sp.dma_start(ln.g[:], ln_g[bass.ds(l, 1)].broadcast_to([P, D])).then_inc(params_here, 16)
                sp.dma_start(ln.b[:], ln_b[bass.ds(l, 1)].broadcast_to([P, D])).then_inc(params_here, 16)

            @block.vector
            def _(dve):
                ch = Chain(dve, chain)
                dve.wait_ge(params_here, 32)
                for t in range(NT):
                    ch.link(nc.vector.scalar_tensor_tensor(out=c.x[:, t, :], in0=c.x[:, t, :], scalar=ALPHA,
                                                           in1=ffn[:, t, :], op0=ALU.mult, op1=ALU.add))
                    layer_norm_steps(nc, dve, ch, c, ln, t, None)

            @block.scalar
            def _(act):
                for t in range(NT):
                    act.wait_ge(ln.var_done, t + 1)
                    nc.scalar.activation(ln.root[:, t:t + 1], ln.var[:, t:t + 1], ACT.Sqrt).then_inc(ln.rooted, 1)


def route(nc, c, r, l, w_q, keys):
    with ExitStack() as ctx:
        def sb(name, shape, dt=F32):
            return ctx.enter_context(nc.sbuf_tensor(name, shape, dt))
        w = sb("rt_w", [P, 2, ND, P])
        key = sb("rt_key", [P, 2, P])
        key_t = sb("rt_key_t", [P, 2, P])
        q = sb("rt_q", [P, 2, S])
        score = sb("rt_score", [P, NT, 2, N_KEYS])
        score2 = sb("rt_score2", [P, NT, 2, N_KEYS])
        best = sb("rt_best", [P, NT, 2, TOPK])
        best_at = sb("rt_best_at", [P, NT, 2, TOPK], U32)
        best_key = sb("rt_best_key", [P, NT, 2, TOPK])
        cand = sb("rt_cand", [P, NT, TOPK, TOPK])
        cand2 = sb("rt_cand2", [P, NT, TOPK, TOPK])
        top = sb("rt_top", [P, NT, TOPK])
        top_at = sb("rt_top_at", [P, NT, TOPK], U32)
        part = sb("rt_part", [P, 2, NT, TOPK], U32)
        part_f = sb("rt_part_f", [P, 2, NT, TOPK])
        hit = sb("rt_hit", [P, 2, NT, TOPK, TOPK])
        names = ["w_here0", "w_here1", "key_here", "keys_turned", "q_made", "keys_out", "q_out", "scored",
                 "score_out", "hit_made", "looked_up", "dve_chain", "passed"]
        PER = 11
        with phase(nc, names) as (block, w_here0, w_here1, key_here, keys_turned, q_made, keys_out, q_out, scored,
                                  score_out, hit_made, looked_up, chain, passed):
            w_here = (w_here0, w_here1)

            @block.sync
            def _(sp):
                with sp.Fori(0, P_HEADS) as h:
                    sp.wait_ge(keys_turned, h + CREDIT)
                    sp.dma_start(key[:], keys[bass.ds(l, 1), bass.ds(h, 1)]
                                 .rearrange("o h c n k -> n (o h c) k")).then_inc(key_here, 16)
                    for half in range(2):
                        sp.wait_ge(q_made, h * 2 + half + 1)
                        sp.dma_start(w[:, half], w_q[bass.ds(l, 1), :, bass.ds(h * (2 * P) + half * P, P)]
                                     .rearrange("o (c p) n -> p (o c) n", p=P)).then_inc(w_here[half], 16)

            @block.gpsimd
            def _(pool):
                nc.gpsimd.memset(hit[:], 0.0).then_inc(looked_up, 2)
                for sem, n in ((keys_turned, CREDIT), (q_made, 2), (keys_out, CREDIT), (score_out, CREDIT),
                               (chain, PER)):
                    pool.sem_inc(sem, n)
                with pool.Fori(0, P_HEADS) as h:
                    for half in range(2):
                        pool.wait_ge(hit_made, h * 2 + half + 1)
                        nc.gpsimd.tensor_tensor(
                            hit[:, half], hit[:, half],
                            best_key[:, :, half, :].unsqueeze(2).broadcast_to([P, NT, TOPK, TOPK]),
                            ALU.mult).then_inc(looked_up, 1)

            @block.tensor
            def _(pe):
                with pe.Fori(0, P_HEADS) as h:
                    pe.wait_ge(key_here, h * 16 + 16)
                    pe.wait_ge(keys_out, h + CREDIT)
                    for half in range(2):
                        mm = nc.tensor.transpose(c.psum[:, 0, half * P:(half + 1) * P], key[:, half, :], c.ident[:])
                    mm.then_inc(keys_turned, 1)
                    for half in range(2):
                        pe.wait_ge(w_here[half], h * 16 + 16)
                        for k in range(ND):
                            mm = nc.tensor.matmul(c.psum[:, 1 + half, :], w[:, half, k, :],
                                                  c.xt[:, k, :], start=k == 0, stop=k == ND - 1)
                        mm.then_inc(q_made, 1)
                    pe.wait_ge(keys_out, h + 1 + CREDIT)
                    pe.wait_ge(q_out, h * 2 + 2)
                    pe.wait_ge(score_out, h + CREDIT)
                    for t in range(NT):
                        for half in range(2):
                            mm = nc.tensor.matmul(c.flat[:, 2048 + (2 * t + half) * P:2048 + (2 * t + half + 1) * P],
                                                  q[:, half, t * P:(t + 1) * P], key_t[:, half, :],
                                                  start=True, stop=True)
                    mm.then_inc(scored, 1)

            @block.scalar
            def _(act):
                with act.Fori(0, P_HEADS) as h:
                    act.wait_ge(keys_turned, h + 1 + CREDIT)
                    nc.scalar.copy(key_t[:].rearrange("p c k -> p (c k)"), c.psum[:, 0, 0:2 * P]).then_inc(keys_out, 1)
                    for half in range(2):
                        act.wait_ge(q_made, h * 2 + half + 1 + 2)
                        nc.scalar.copy(q[:, half, :], c.psum[:, 1 + half, :]).then_inc(q_out, 1)
                    act.wait_ge(scored, h + 1)
                    act.wait_ge(chain, h * PER + 2)
                    nc.scalar.copy(score[:].rearrange("p t c n -> p (t c n)"),
                                   c.flat[:, 2048:2048 + NT * 2 * N_KEYS]).then_inc(score_out, 1)

            @block.vector
            def _(dve):
                ch = Chain(dve, chain, PER, passed)

                def top16(pairs):
                    for values, spare, out, at in pairs:
                        ins = nc.vector.max(out[:, 0:8], values)
                    ch.link_plain(ins)
                    for values, spare, out, at in pairs:
                        nc.vector.max_index(at[:, 0:8], out[:, 0:8], values)
                    for values, spare, out, at in pairs:
                        ins = nc.vector.match_replace(spare, out[:, 0:8], values, NEG)
                    ch.link_plain(ins)
                    for values, spare, out, at in pairs:
                        ins = nc.vector.max(out[:, 8:16], spare)
                    ch.link_plain(ins)
                    for values, spare, out, at in pairs:
                        ins = nc.vector.max_index(at[:, 8:16], out[:, 8:16], spare)
                    ch.link_plain(ins)

                with dve.Fori(0, P_HEADS) as h:
                    ch.turn(h, PER)
                    dve.wait_ge(score_out, h + 1 + CREDIT)
                    dve.sem_inc(passed, 1)
                    top16([(score[:, t, half, :], score2[:, t, half, :], best[:, t, half, :], best_at[:, t, half, :])
                           for t in range(NT) for half in range(2)])
                    for half in range(2):
                        dve.wait_ge(looked_up, h * 2 + half + 1)
                        nc.vector.tensor_reduce(
                            r.index[:, half, :, bass.ds(h, 1), :].rearrange("p t o k -> p t (o k)"),
                            hit[:, half], AX_X, ALU.add)
                    nc.vector.tensor_copy(best_key[:], best_at[:])
                    ch.link_plain(nc.vector.tensor_tensor(
                        cand[:], best[:, :, 0, :].unsqueeze(3).broadcast_to([P, NT, TOPK, TOPK]),
                        best[:, :, 1, :].unsqueeze(2).broadcast_to([P, NT, TOPK, TOPK]), ALU.add))
                    top16([(cand[:, t].rearrange("p a b -> p (a b)"), cand2[:, t].rearrange("p a b -> p (a b)"),
                            top[:, t, :], top_at[:, t, :]) for t in range(NT)])
                    at_h = bass.ds(h, 1)
                    nc.vector.tensor_copy(r.top[:, :, at_h, :].rearrange("p t o k -> p t (o k)"), top[:])
                    nc.vector.tensor_scalar(part[:, 0], top_at[:], 4, None, ALU.logical_shift_right)
                    ch.link(nc.vector.tensor_scalar(part[:, 1], top_at[:], TOPK - 1, None, ALU.bitwise_and))
                    ch.link(nc.vector.tensor_copy(part_f[:], part[:]))
                    for half in range(2):
                        ins = nc.vector.tensor_tensor(
                            hit[:, half].rearrange("p t k a -> p (t k) a"),
                            part_f[:, half].rearrange("p t k -> p (t k)").unsqueeze(2).broadcast_to(
                                [P, NT * TOPK, TOPK]),
                            c.count_top[:].unsqueeze(1).broadcast_to([P, NT * TOPK, TOPK]),
                            ALU.is_equal).then_inc(hit_made, 1)
                ch.turned(P_HEADS)
                for half in range(2):
                    dve.wait_ge(looked_up, P_HEADS * 2 + half + 1)
                    nc.vector.tensor_reduce(r.index[:, half, :, P_HEADS, :], hit[:, half], AX_X, ALU.add)


def gates(nc, c, r):
    with ExitStack() as ctx:
        def sb(name, shape):
            return ctx.enter_context(nc.sbuf_tensor(name, shape, F32))
        e = sb("gt_exp", [P, NT, P_HEADS, TOPK])
        total = sb("gt_total", [P, NT * P_HEADS])
        share = sb("gt_share", [P, NT * P_HEADS])
        with phase(nc, ["dve_chain", "exped", "turned", "evacuated"]) as (block, chain, exped, turned, evacuated):
            ef = e[:].rearrange("p t h k -> p (t h) k")
            shape = [P, NT * P_HEADS, TOPK]

            @block.vector
            def _(dve):
                ch = Chain(dve, chain)
                top = r.top[:].rearrange("p t h k -> p (t h) k")
                ch.link(nc.vector.tensor_tensor(ef, top, top[:, :, 0:1].broadcast_to(shape), ALU.subtract))
                dve.wait_ge(exped, 1)
                ch.link(nc.vector.tensor_reduce(total[:], ef, AX_X, ALU.add))
                ch.link(nc.vector.reciprocal(share[:], total[:]))
                ch.link(nc.vector.tensor_tensor(ef, ef, share[:].unsqueeze(2).broadcast_to(shape), ALU.mult))

            @block.scalar
            def _(act):
                act.wait_ge(chain, 1)
                nc.scalar.activation(e[:], e[:], ACT.Exp).then_inc(exped, 1)
                for n in range(3):
                    act.wait_ge(turned, n + 1)
                    nc.scalar.copy(r.turned[:, n, :], c.psum[:, n, :]).then_inc(evacuated, 1)

            @block.tensor
            def _(pe):
                for n, tile in enumerate((r.index[:, 0, :, 1:], r.index[:, 1, :, 1:], e)):
                    if n == 2:
                        pe.wait_ge(chain, 4)
                    for t in range(NT):
                        mm = nc.tensor.transpose(c.psum[:, n, t * P:(t + 1) * P],
                                                 tile[:, t].rearrange("p h k -> p (h k)"), c.ident[:])
                    mm.then_inc(turned, 1)


def spread_gates(nc, c, r, gate_dram):
    RING = 8
    GATE_RING = 4
    GROUPS = P // 4
    BODY = 8
    TILE_TURNS = GROUPS // BODY
    TURNS = NT * TILE_TURNS
    LAG = 3
    ONE_HOT_BY = "PADPAPAD"
    with ExitStack() as ctx:
        hot_j = ctx.enter_context(nc.sbuf_tensor("sg_hot_j", [P, RING, 4, N_KEYS], F32))
        gate_i = ctx.enter_context(nc.sbuf_tensor("sg_gate_i", [P, GATE_RING, 4, N_KEYS], F32))
        apart = ctx.enter_context(nc.sbuf_tensor("sg_apart", [P, 4, N_KEYS], F32))
        pool_j = ctx.enter_context(nc.sbuf_tensor("sg_pool_j", [P, BODY, 4], F32))
        out = [ctx.enter_context(nc.sbuf_tensor(f"sg_out{b}", [P, N_KEYS, P], F32)) for b in range(2)]
        by = {e: ONE_HOT_BY.count(e) for e in "PAD"}
        names = ["made", "hot_pool", "hot_act", "hot_dve", "staged", "apart_done", "passed", "multiplied", "evacuated",
                 "written0", "written1"]
        with phase(nc, names) as (block, made, hot_pool, hot_act, hot_dve, staged, apart_done, passed, multiplied,
                                  evacuated, *written):
            hot = {"P": hot_pool, "A": hot_act, "D": hot_dve}

            def nth(g):
                return ONE_HOT_BY[:g + 1].count(ONE_HOT_BY[g])

            @block.gpsimd
            def _(pool):
                pool.sem_inc(multiplied, RING)
                pool.sem_inc(evacuated, RING)
                pool.sem_inc(hot_pool, by["P"])
                pool.sem_inc(hot_act, by["A"])
                with pool.Fori(0, TURNS) as i:
                    for g in range(BODY):
                        if ONE_HOT_BY[g] != "P":
                            continue
                        pool.wait_ge(staged, i * by["P"] + nth(g))
                        pool.wait_ge(multiplied, i * BODY + (g + 1))
                        pool.sem_inc(passed, 1)
                        for n in range(4):
                            ins = nc.gpsimd.tensor_scalar(hot_j[:, g % RING, n, :], c.count_keys[:],
                                                          pool_j[:, g, n:n + 1], None, ALU.is_equal)
                        ins.then_inc(hot_pool, 1)

            @block.vector
            def _(dve):
                with dve.Fori(0, TURNS) as i:
                    for g in range(BODY):
                        at4 = bass.ds(i * (4 * BODY) + 4 * g, 4)
                        if ONE_HOT_BY[g] == "P":
                            dve.wait_ge(hot_pool, i * by["P"] + nth(g))
                            nc.vector.tensor_copy(pool_j[:, g, :], r.turned[:, 1, at4]).then_inc(staged, 1)
                        dve.wait_ge(multiplied, i * BODY + (g + 1 + RING - GATE_RING))
                        for n in range(4):
                            at = bass.ds(i * (4 * BODY) + (4 * g + n), 1)
                            ins = nc.vector.tensor_scalar(gate_i[:, g % GATE_RING, n, :], c.count_keys[:],
                                                          r.turned[:, 0, at], r.turned[:, 2, at],
                                                          ALU.is_equal, ALU.mult)
                        ins.then_inc(made, 1)
                        if ONE_HOT_BY[g] == "D":
                            nc.vector.tensor_tensor(
                                hot_j[:, g % RING], c.count_keys[:].unsqueeze(1).broadcast_to([P, 4, N_KEYS]),
                                r.turned[:, 1, at4].unsqueeze(2).broadcast_to([P, 4, N_KEYS]),
                                ALU.is_equal).then_inc(hot_dve, 1)

            @block.tensor
            def _(pe):
                with pe.Fori(0, TURNS) as i:
                    for g in range(BODY):
                        e = ONE_HOT_BY[g]
                        pe.wait_ge(made, i * BODY + (g + 1))
                        pe.wait_ge(hot[e], i * by[e] + (nth(g) + (0 if e == "D" else by[e])))
                        pe.wait_ge(evacuated, i * BODY + (g + 1))
                        for n in range(4):
                            mm = nc.tensor.matmul(c.psum[:, g % RING, n * P:(n + 1) * P], hot_j[:, g % RING, n, :],
                                                  gate_i[:, g % GATE_RING, n, :], start=True, stop=True)
                        mm.then_inc(multiplied, 1)

            @block.scalar
            def _(act):
                def one_hot(i, t, g):
                    done = t * by["A"] * TILE_TURNS + nth(g)
                    act.wait_ge(multiplied, i * BODY + (t * GROUPS + g + 1))
                    act.wait_ge(hot_act, i * by["A"] + (done - 1 + by["A"]))
                    for n in range(4):
                        at = bass.ds(i * (4 * BODY) + (t * P + 4 * g + n), 1)
                        ins = nc.scalar.activation(apart[:, n, :], c.count_keys[:], ACT.Abs,
                                                   bias=r.turned[:, 1, at], scale=-1.0)
                    ins.then_inc(apart_done, 1)
                    act.wait_ge(apart_done, i * by["A"] + done)
                    nc.scalar.activation(hot_j[:, g % RING], apart[:], ACT.Relu, bias=c.ones[:, 0:1],
                                         scale=-1.0).then_inc(hot_act, 1)

                def empty(i, t, g):
                    evacuate(nc, c, act, out[t % 2], i, t, g, multiplied, evacuated, GROUPS, BODY, RING)

                def turn(i, t, first):
                    for g in range(BODY):
                        if ONE_HOT_BY[g] == "A":
                            one_hot(i, t, g)
                        if g >= LAG or not first:
                            empty(i, t, g - LAG)

                for t in range(NT):
                    if t >= 2:
                        act.wait_ge(written[t % 2], 64 * (t // 2))
                    turn(0, t, True)
                    with act.Fori(1, TILE_TURNS) as i:
                        turn(i, t, False)
                    for g in range(BODY - LAG, BODY):
                        empty(TILE_TURNS - 1, t, g)

            @block.sync
            def _(sp):
                for t in range(NT):
                    sp.wait_ge(evacuated, (t + 1) * GROUPS + RING)
                    for q in range(4):
                        n = N_KEYS // 4
                        sp.dma_start(gate_dram[q * n:(q + 1) * n, :, t * P:(t + 1) * P].rearrange("i j t -> j i t"),
                                     out[t % 2][:, q * n:(q + 1) * n, :]).then_inc(written[t % 2], 16)
                for sem in written:
                    sp.wait_ge(sem, 64 * NT // 2)


def evacuate(nc, c, act, out, i, t, g, multiplied, evacuated, groups, body, ring):
    act.wait_ge(multiplied, i * body + (t * groups + g + 1 + ring))
    nc.scalar.copy(out[:, :, bass.ds(i * (4 * body) + 4 * g, 4)],
                   c.psum[:, g % ring, :].rearrange("p (n i) -> p i n", n=4)).then_inc(evacuated, 1)


def experts(nc, c, l, x_hi, x_lo, ffn, peer_u, peer_v, gate_dram):
    GB = 2
    BODY = 2 * GB
    TURNS = N_KEYS // BODY
    with ExitStack() as ctx:
        def sb(name, shape, dt=F32):
            return ctx.enter_context(nc.sbuf_tensor(name, shape, dt))
        u = sb("ex_u", [P, BODY, D])
        v = sb("ex_v", [P, BODY, D])
        gate = sb("ex_gate", [P, BODY, S])
        ut_hi, ut_lo = (sb(f"ex_ut_{n}", [P, 2, D], F32R) for n in ("hi", "lo"))
        v_hi, v_lo = (sb(f"ex_v_{n}", [P, 2, GB, D], F32R) for n in ("hi", "lo"))
        a_hi, a_lo = (sb(f"ex_a_{n}", [P, 2, GB, S], F32R) for n in ("hi", "lo"))
        act_out = sb("ex_act", [P, 2, S])
        a_full = sb("ex_a", [P, 2, S])
        names = ([f"u_here{s}" for s in range(BODY)] + [f"v_here{s}" for s in range(BODY)]
                 + [f"gate_here{s}" for s in range(BODY)]
                 + ["u_turned", "u_high", "u_low", "hidden", "gelued", "gated", "a_high", "a_low", "v_high", "v_low",
                    "summed", "added", "zeroed"])
        with phase(nc, names) as (block, *sems):
            u_here, v_here, gate_here = sems[0:BODY], sems[BODY:2 * BODY], sems[2 * BODY:3 * BODY]
            (u_turned, u_high, u_low, hidden, gelued, gated, a_high, a_low, v_high, v_low,
             summed, added, zeroed) = sems[3 * BODY:]


            @block.sync
            def _(sp):
                def load(i, s, first):
                    at = bass.ds(i * (BODY * P) + s * P, P) if not first else slice(s * P, (s + 1) * P)
                    key = bass.ds(i * BODY + s, 1) if not first else slice(s, s + 1)
                    if not first:
                        sp.wait_ge(u_turned, i * (2 * BODY) + (2 * (s + 1) - 2 * BODY))
                    sp.dma_start(u[:, s, :], peer_u[bass.ds(l, 1), at].rearrange("o p d -> (o p) d")
                                 ).then_inc(u_here[s], 16)
                    if not first:
                        sp.wait_ge(gated, i * BODY + (s + 1 - BODY))
                        sp.wait_ge(a_low, i * BODY + (s + 1 - BODY))
                    sp.dma_start(gate[:, s, :], gate_dram[key].rearrange("o j t -> (o j) t")
                                 ).then_inc(gate_here[s], 16)
                    if not first:
                        sp.wait_ge(v_low, i * BODY + (s + 1 - BODY))
                    sp.dma_start(v[:, s, :], peer_v[bass.ds(l, 1), at].rearrange("o p d -> (o p) d")
                                 ).then_inc(v_here[s], 16)

                for s in range(BODY):
                    load(0, s, True)
                with sp.Fori(1, TURNS) as i:
                    for s in range(BODY):
                        load(i, s, False)

            @block.tensor
            def _(pe):
                def turn_u(i, s):
                    pe.wait_ge(u_here[s], i * 16 + 16)
                    for h in range(2):
                        if not (isinstance(i, int) and s == 0):
                            pe.wait_ge(u_low, i * (2 * BODY) + (2 * s + h - 1))
                        for k in range(4):
                            mm = nc.tensor.transpose(c.psum[:, h, k * P:(k + 1) * P],
                                                     u[:, s, (4 * h + k) * P:(4 * h + k + 1) * P], c.ident[:])
                        mm.then_inc(u_turned, 1)

                def hide(i, s):
                    pe.wait_ge(u_low, i * (2 * BODY) + (2 * s + 2))
                    if not (isinstance(i, int) and s < 2):
                        pe.wait_ge(gelued, i * BODY + (s - 1))
                    for k in range(ND):
                        at = slice(k * P, (k + 1) * P)
                        for n, (left, right) in enumerate(((ut_hi, x_hi), (ut_hi, x_lo), (ut_lo, x_hi))):
                            mm = nc.tensor.matmul(c.psum[:, 2 + s % 2, :], left[:, s % 2, at], right[:, k, :],
                                                  start=k + n == 0, stop=k == ND - 1 and n == 2)
                    mm.then_inc(hidden, 1)

                def add_up(i, par, part):
                    if part == 0:
                        pe.wait_ge(a_low, i * BODY + GB * (par + 1))
                        pe.wait_ge(v_low, i * BODY + GB * (par + 1))
                    for t in (2 * part, 2 * part + 1):
                        tok = slice(t * P, (t + 1) * P)
                        for h in range(2):
                            n = 2 * t + h
                            if not (isinstance(i, int) and par == 0 and n < 4):
                                pe.wait_ge(added, i * 16 + (8 * par + n - 3))
                            half = slice(h * HALF, (h + 1) * HALF)
                            for b in range(GB):
                                for m, (left, right) in enumerate(((a_hi, v_hi), (a_hi, v_lo), (a_lo, v_hi))):
                                    mm = nc.tensor.matmul(c.psum[:, 4 + n % 4, :], left[:, par, b, tok],
                                                          right[:, par, b, half], start=b + m == 0,
                                                          stop=b == GB - 1 and m == 2)
                            mm.then_inc(summed, 1)

                def turn(i, first):
                    for s, (di, par, part) in enumerate(((-1, 0, 1), (-1, 1, 0), (-1, 1, 1), (0, 0, 0))):
                        turn_u(i, s)
                        if not first or di == 0:
                            add_up(i + di, par, part)
                        hide(i, s)

                turn(0, True)
                with pe.Fori(1, TURNS) as i:
                    turn(i, False)
                add_up(TURNS - 1, 0, 1)
                add_up(TURNS - 1, 1, 0)
                add_up(TURNS - 1, 1, 1)

            def free_group(eng, i, s, first):
                if not first:
                    eng.wait_ge(summed, i * 16 + (8 * (s // GB) - 8))

            @block.scalar
            def _(act):
                def turn(i, first):
                    for s in range(BODY):
                        for h in range(2):
                            act.wait_ge(u_turned, i * (2 * BODY) + (2 * s + h + 1))
                            nc.scalar.copy(ut_hi[:, s % 2, h * HALF:(h + 1) * HALF],
                                           c.psum[:, h, :]).then_inc(u_high, 1)
                        act.wait_ge(v_here[s], i * 16 + 16)
                        free_group(act, i, s, first)
                        nc.scalar.copy(v_hi[:, s // GB, s % GB, :], v[:, s, :]).then_inc(v_high, 1)
                        act.wait_ge(hidden, i * BODY + (s + 1))
                        if not (first and s < 2):
                            act.wait_ge(gated, i * BODY + (s - 1))
                            act.wait_ge(a_high, i * BODY + (s - 1))
                        nc.scalar.activation(act_out[:, s % 2, :], c.psum[:, 2 + s % 2, :],
                                             ACT.Gelu).then_inc(gelued, 1)

                turn(0, True)
                with act.Fori(1, TURNS) as i:
                    turn(i, False)

            @block.gpsimd
            def _(pool):
                nc.gpsimd.memset(ffn[:], 0.0).then_inc(zeroed, 1)

                def turn(i, first):
                    for s in range(BODY):
                        pool.wait_ge(gate_here[s], i * 16 + 16)
                        pool.wait_ge(gelued, i * BODY + (s + 1))
                        if not (first and s < 2):
                            pool.wait_ge(a_low, i * BODY + (s - 1))
                        nc.gpsimd.tensor_tensor(a_full[:, s % 2, :], act_out[:, s % 2, :], gate[:, s, :],
                                                ALU.mult).then_inc(gated, 1)

                turn(0, True)
                with pool.Fori(1, TURNS) as i:
                    turn(i, False)

            @block.vector
            def _(dve):
                def add(i, first_sum):
                    for n in range(first_sum, first_sum + 4):
                        dve.wait_ge(summed, i * 16 + (n + 1))
                        at = ffn[:, (n % 8) // 2, (n % 2) * HALF:(n % 2 + 1) * HALF]
                        nc.vector.tensor_tensor(at, at, c.psum[:, 4 + n % 4, :], ALU.add).then_inc(added, 1)

                def turn(i, first):
                    for s in range(BODY):
                        for h in range(2):
                            dve.wait_ge(u_high, i * (2 * BODY) + (2 * s + h + 1))
                            at = slice(h * HALF, (h + 1) * HALF)
                            nc.vector.tensor_tensor(ut_lo[:, s % 2, at], c.psum[:, h, :],
                                                    ut_hi[:, s % 2, at].bitcast(F32), ALU.subtract).then_inc(u_low, 1)
                        if not first or s == 3:
                            add(i, 4 * s - 12)
                        dve.wait_ge(v_high, i * BODY + (s + 1))
                        nc.vector.tensor_tensor(v_lo[:, s // GB, s % GB, :], v[:, s, :],
                                                v_hi[:, s // GB, s % GB, :].bitcast(F32),
                                                ALU.subtract).then_inc(v_low, 1)
                        dve.wait_ge(gate_here[s], i * 16 + 16)
                        dve.wait_ge(gelued, i * BODY + (s + 1))
                        nc.vector.tensor_tensor(a_hi[:, s // GB, s % GB, :], act_out[:, s % 2, :], gate[:, s, :],
                                                ALU.mult).then_inc(a_high, 1)
                        dve.wait_ge(a_high, i * BODY + (s + 1))
                        dve.wait_ge(gated, i * BODY + (s + 1))
                        nc.vector.tensor_tensor(a_lo[:, s // GB, s % GB, :], a_full[:, s % 2, :],
                                                a_hi[:, s // GB, s % GB, :].bitcast(F32),
                                                ALU.subtract).then_inc(a_low, 1)

                dve.wait_ge(zeroed, 1)
                turn(0, True)
                with dve.Fori(1, TURNS) as i:
                    turn(i, False)
                for first_sum in (4, 8, 12):
                    add(TURNS - 1, first_sum)


class Tiles:
    pass


def build(nc, x, w_in, g_cq, w_uq, g_ckv, w_ukv, w_o, ln1_g, ln1_b, peer_wq, peer_keys, peer_u, peer_v,
          ln2_g, ln2_b, rope_cos, rope_sin, out, gate_dram):
    with ExitStack() as whole:
        def tile(ctx, name, shape, dt=F32):
            return ctx.enter_context(nc.sbuf_tensor(name, shape, dt))

        c = Tiles()
        c.x = tile(whole, "x", [P, NT, D])
        c.xt = tile(whole, "xt", [P, ND, S])
        c.ident = tile(whole, "ident", [P, P])
        c.neg_ones = tile(whole, "neg_ones", [P, P])
        c.neg_tri = tile(whole, "neg_tri", [P, P])
        c.neg_mask = tile(whole, "neg_mask", [P, P])
        c.count_keys = tile(whole, "count_keys", [P, N_KEYS])
        c.count_top = tile(whole, "count_top", [P, TOPK])
        c.ones = tile(whole, "ones", [P, 1])
        c.cos = tile(whole, "cos", [P, S])
        c.sin = tile(whole, "sin", [P, S])
        c.psum = whole.enter_context(nc.psum_tensor("banks", [P, 8, 512], F32))
        c.flat = c.psum[:].rearrange("p b n -> p (b n)")

        make_constants(nc, c, rope_cos, rope_sin)
        load_x(nc, c, x)
        with nc.Fori(0, DEPTH) as l:
            transpose_x(nc, c)
            with ExitStack() as ctx:
                m = Tiles()
                m.mixed_t = tile(ctx, "mixed_t", [P, ND, S])
                m.lat_t = tile(ctx, "lat_t", [P, 3, S])
                m.k_rope = tile(ctx, "k_rope", [P, S])
                m.k_full = tile(ctx, "k_full", [P, 2, S])
                latents(nc, c, m, l, w_in, g_cq, g_ckv)
                stick_breaking(nc, c, m, l, w_in)
                latent_attention(nc, c, m, l, w_uq, w_ukv)
                project_out(nc, c, m, l, w_o, ln1_g, ln1_b)
            transpose_x(nc, c)
            with ExitStack() as ctx:
                r = Tiles()
                r.top = tile(ctx, "top", [P, NT, P_HEADS, TOPK])
                r.index = tile(ctx, "index", [P, 2, NT, 1 + P_HEADS, TOPK])
                r.turned = tile(ctx, "picks_t", [P, 3, S])
                route(nc, c, r, l, peer_wq, peer_keys)
                gates(nc, c, r)
                spread_gates(nc, c, r, gate_dram)
            with ExitStack() as ctx:
                ffn = tile(ctx, "ffn", [P, NT, D])
                x_hi, x_lo = (tile(ctx, f"x_{n}", [P, ND, S], F32R) for n in ("hi", "lo"))
                split_x(nc, c, x_hi, x_lo)
                experts(nc, c, l, x_hi, x_lo, ffn, peer_u, peer_v, gate_dram)
                residual_norm(nc, c, l, ffn, ln2_g, ln2_b)
        store_x(nc, c, out)


_INS = ["x", "w_in", "g_cq", "w_uq", "g_ckv", "w_ukv", "w_o", "ln1_g", "ln1_b", "peer_wq", "peer_keys",
        "peer_u", "peer_v", "ln2_g", "ln2_b"]


def rope_tables():
    inv = (np.float32(10000.0) ** (-np.arange(0, ROPE, 2, dtype=np.float32) / np.float32(ROPE))).astype(np.float32)
    angle = inv[:, None] * np.arange(S, dtype=np.float32)[None, :]
    cos, sin = np.cos(angle, dtype=np.float32), np.sin(angle, dtype=np.float32)
    return np.concatenate([cos, cos]), np.concatenate([-sin, sin])


def kernel(**inputs):
    import concourse.bacc as bacc
    from concourse.bass_utils import run_bass_kernel_spmd

    nc = bacc.Bacc("TRN2", target_bir_lowering=False, num_devices=1)
    arrays, args = {}, []
    for name in _INS:
        arrays[f"in_{name}_dram"] = np.ascontiguousarray(inputs[name])
    arrays["rope_cos_dram"], arrays["rope_sin_dram"] = rope_tables()
    for name, a in arrays.items():
        args.append(nc.dram_tensor(name, a.shape, mybir.dt.from_np(a.dtype), kind="ExternalInput").ap())
    args.append(nc.dram_tensor("out_0_dram", (1, S, D), F32, kind="ExternalOutput").ap())
    args.append(nc.dram_tensor("gates_dram", (N_KEYS, N_KEYS, S), F32).ap())
    build(nc, *args)
    return run_bass_kernel_spmd(nc, [arrays], core_ids=[0]).results[0]["out_0_dram"]
```

```python
from contextlib import ExitStack, contextmanager

import numpy as np

import concourse.bass as bass
from concourse import mybir

F32 = mybir.dt.float32
BF16 = mybir.dt.bfloat16
F32R = mybir.dt.float32r
U32 = mybir.dt.uint32
ALU = mybir.AluOpType
ACT = mybir.ActivationFunctionType
AX_X = mybir.AxisListType.X

P = 128
DEPTH = 2
S = 512
D = 1024
NT = S // P
ND = D // P
HALF = D // 2
HD = 64
PAIRS = 4
D_SB = 512
Q_RANK = 256
KV_RANK = 128
ROPE = 32
QK = HD + ROPE
LATENT0 = 3 * D_SB
LATENT = Q_RANK + KV_RANK
N_KEYS = 128
P_HEADS = 8
TOPK = 16
ALPHA = (2.0 * DEPTH) ** 0.25
LN_EPS = 1e-5
RMS_EPS = 1e-6
NEG = -3.0e38

PACK = {4: 0, 3: 512, 1: 896, 2: 1024}
PACKED = 1280
SB_AT = {s: PACK[NT - s] for s in range(NT)}
LA_AT = {t: PACK[t + 1] for t in range(NT)}


class Chain:

    def __init__(self, eng, sem, credit=0, passed=None):
        self.passed = passed
        self.eng, self.sem, self.credit, self.base, self.n = eng, sem, credit, credit, 0

    def link(self, instruction):
        instruction.then_inc(self.sem, 1)
        self.n += 1
        self.eng.wait_ge(self.sem, self.base + self.n)

    def link_plain(self, instruction):
        self.link(instruction)
        self.eng.sem_inc(self.passed, 1)

    def turn(self, i, per):
        self.base, self.n, self.per = i * per + self.credit, 0, per

    def turned(self, count):
        assert self.n == self.per, (self.n, self.per)
        self.base, self.n = count * self.per + self.credit, 0


@contextmanager
def phase(nc, names):
    with ExitStack() as ctx:
        sems = [ctx.enter_context(nc.semaphore(n)) for n in names]
        with nc.Block(no_gpsimd_drain=True) as block:
            yield (block, *sems)
        nums = sorted(s.num for s in sems)
        assert nums == list(range(nums[0], nums[0] + len(nums)))
        nc.all_engine_barrier(sems_to_clear=range(nums[0], nums[-1] + 1))


CREDIT = 1


def give_credit(block, sems):
    @block.gpsimd
    def _(pool):
        for sem in sems:
            pool.sem_inc(sem, CREDIT)


def cols(ap, start, n):
    return ap[:, start:start + n]


def make_constants(nc, c, x, rope_cos, rope_sin):
    with phase(nc, ["filled", "selected", "tables_in"]) as (block, filled, selected, tables_in):
        @block.vector
        def _(dve):
            dve.wait_ge(selected, 1)
            nc.vector.tensor_copy(c.neg_tri_r[:], c.neg_tri[:])
            nc.vector.tensor_copy(c.neg_ones_r[:], c.neg_ones[:])

        @block.gpsimd
        def _(pool):
            nc.gpsimd.memset(c.ident[:], 0.0).then_inc(filled, 1)
            nc.gpsimd.memset(c.neg_ones[:], -1.0).then_inc(filled, 1)
            nc.gpsimd.memset(c.neg_mask[:], 0.0).then_inc(filled, 1)
            nc.gpsimd.iota(c.count_keys[:], [[1, N_KEYS]], base=0, channel_multiplier=0,
                           allow_small_or_imprecise_dtypes=True)
            nc.gpsimd.iota(c.count_rows[:], [[1, TOPK], [0, TOPK]], base=0, channel_multiplier=0,
                           allow_small_or_imprecise_dtypes=True)
            nc.gpsimd.memset(c.ones[:], 1.0)
            pool.wait_ge(filled, 3)
            nc.gpsimd.affine_select(out=c.ident[:], in_=c.ident[:], compare_op=ALU.not_equal, fill=1.0,
                                    base=0, pattern=[[-1, P]], channel_multiplier=1)
            nc.gpsimd.affine_select(out=c.neg_tri[:], in_=c.neg_ones[:], compare_op=ALU.is_ge, fill=0.0,
                                    base=0, pattern=[[-1, P]], channel_multiplier=1)
            nc.gpsimd.affine_select(out=c.neg_mask[:], in_=c.neg_mask[:], compare_op=ALU.is_ge, fill=NEG,
                                    base=0, pattern=[[-1, P]], channel_multiplier=1).then_inc(selected, 1)

        @block.sync
        def _(sp):
            sp.dma_start(c.x[:], x[0].rearrange("(t p) d -> p t d", p=P)).then_inc(tables_in, 16)
            sp.dma_start(c.cos[HD:QK, :], rope_cos).then_inc(tables_in, 16)
            sp.dma_start(c.sin[HD:QK, :], rope_sin).then_inc(tables_in, 16)
            sp.wait_ge(tables_in, 48)


def store_x(nc, c, out):
    with phase(nc, ["x_out"]) as (block, x_out):
        @block.sync
        def _(sp):
            sp.dma_start(out[0].rearrange("(t p) d -> p t d", p=P), c.x[:]).then_inc(x_out, 16)
            sp.wait_ge(x_out, 16)


def split(nc, ch, full, high, low):
    ch.link(nc.vector.tensor_copy(high, full))
    return nc.vector.tensor_tensor(low, full, high.bitcast(F32), ALU.subtract)


PARTS = ((0, 0), (0, 1), (1, 0))


def turn_x(nc, c, pe, x_turned, x_copied):
    for k in range(ND):
        if k >= 4:
            pe.wait_ge(x_copied, k - 3)
        for t in range(NT):
            mm = nc.tensor.transpose(c.psum[:, k % 4, t * P:(t + 1) * P], c.x[:, t, k * P:(k + 1) * P], c.ident[:])
        mm.then_inc(x_turned, 1)
    pe.wait_ge(x_copied, ND)


def take_x(nc, c, act, x_turned, x_copied):
    for k in range(ND):
        act.wait_ge(x_turned, k + 1)
        nc.scalar.copy(c.xt[:, k, :], c.psum[:, k % 4, :]).then_inc(x_copied, 1)


def latents(nc, c, m, l, w_in, g_cq, g_ckv):
    with ExitStack() as ctx:
        w = ctx.enter_context(nc.sbuf_tensor("w_lat", [P, ND, LATENT + ROPE], F32))
        w_swap = ctx.enter_context(nc.sbuf_tensor("w_lat_swap", [P, ND, ROPE], F32))
        g = ctx.enter_context(nc.sbuf_tensor("g_lat", [P, 3], F32))
        squares = ctx.enter_context(nc.sbuf_tensor("lat_squares", [P, NT, Q_RANK], F32))
        stat = ctx.enter_context(nc.sbuf_tensor("lat_stat", [P, 2, 2 * NT], F32))
        normed = ctx.enter_context(nc.sbuf_tensor("lat_normed", [P, NT, LATENT], F32))
        rot = ctx.enter_context(nc.sbuf_tensor("lat_rot", [P, 2, S], F32))
        names = ["w_here", "g_here", "first_pair_here", "x_turned", "x_copied", "projected", "roped", "squared",
                 "rooted", "dve_chain", "norm_done", "turned"]
        with phase(nc, names) as (block, loaded, g_here, first_pair_here, x_turned, x_copied, projected, roped,
                                  squared, rooted, chain, norm_done, turned):
            wl = w_in[bass.ds(l, 1)].rearrange("o (c p) n -> p (o c) n", p=P)
            rope0 = LATENT0 + LATENT

            @block.sync
            def _(sp):
                sp.dma_start(w[:], wl[:, :, LATENT0:]).then_inc(loaded, 16)
                sp.dma_start(w_swap[:, :, 0:ROPE // 2], wl[:, :, rope0 + ROPE // 2:]).then_inc(loaded, 16)
                sp.dma_start(w_swap[:, :, ROPE // 2:], wl[:, :, rope0:rope0 + ROPE // 2]).then_inc(loaded, 16)
                sp.dma_start(g[:, 0:2], g_cq[bass.ds(l, 1)].rearrange("o (c p) -> p (o c)", p=P),
                             allow_slow_non_contiguous=True).then_inc(g_here, 16)
                sp.dma_start(g[:, 2:3], g_ckv[bass.ds(l, 1)].rearrange("o (c p) -> p (o c)", p=P),
                             allow_slow_non_contiguous=True).then_inc(g_here, 16)

                for n in range(3):
                    load_sb_weights(sp, m, l, w_in, 0, n, first_pair_here)
                sp.wait_ge(first_pair_here, 48)

            @block.tensor
            def _(pe):
                turn_x(nc, c, pe, x_turned, x_copied)
                pe.wait_ge(loaded, 48)
                for t in range(NT):
                    for k in range(ND):
                        mm = nc.tensor.matmul(c.psum[:, t, 0:LATENT], c.xt[:, k, t * P:(t + 1) * P],
                                              w[:, k, 0:LATENT], start=k == 0, stop=k == ND - 1)
                    mm.then_inc(projected, 1)
                for bank, wr in ((4, w[:, :, LATENT:]), (5, w_swap[:])):
                    for k in range(ND):
                        mm = nc.tensor.matmul(c.psum[HD:QK, bank, :], wr[:, k, :], c.xt[:, k, :],
                                              start=k == 0, stop=k == ND - 1)
                    mm.then_inc(roped, 1)
                pe.wait_ge(norm_done, NT)
                for k in range(3):
                    for t in range(NT):
                        mm = nc.tensor.transpose(c.psum[:, k, t * P:(t + 1) * P],
                                                 normed[:, t, k * P:(k + 1) * P], c.ident[:])
                    mm.then_inc(turned, 1)

            @block.scalar
            def _(act):
                take_x(nc, c, act, x_turned, x_copied)
                for t in range(NT):
                    act.wait_ge(projected, t + 1)
                    nc.scalar.activation(squares[:, t, :], c.psum[:, t, 0:Q_RANK], ACT.Square,
                                         accum_out=stat[:, 0, t:t + 1]).then_inc(squared, 1)
                    act.wait_ge(squared, 2 * t + 1)
                    nc.scalar.activation(squares[:, t, 0:KV_RANK], c.psum[:, t, Q_RANK:LATENT], ACT.Square,
                                         accum_out=stat[:, 0, NT + t:NT + t + 1]).then_inc(squared, 1)
                act.wait_ge(chain, ND + 2)
                nc.scalar.activation(stat[:, 0, :], stat[:, 1, :], ACT.Sqrt).then_inc(rooted, 1)

            @block.vector
            def _(dve):
                ch = Chain(dve, chain)
                for k in range(ND):
                    dve.wait_ge(x_copied, k + 1)
                    split(nc, ch, c.xt[:, k, :], m.x_hi[:, k, :], m.x_lo[:, k, :])
                dve.wait_ge(squared, 2 * NT)
                ch.link(nc.vector.tensor_scalar(stat[:, 1, 0:NT], stat[:, 0, 0:NT], 1.0 / Q_RANK, RMS_EPS,
                                                ALU.mult, ALU.add))
                ch.link(nc.vector.tensor_scalar(stat[:, 1, NT:], stat[:, 0, NT:], 1.0 / KV_RANK, RMS_EPS,
                                                ALU.mult, ALU.add))
                dve.wait_ge(rooted, 1)
                ch.link(nc.vector.reciprocal(stat[:, 1, :], stat[:, 0, :]))
                for t in range(NT):
                    nc.vector.tensor_scalar(normed[:, t, 0:Q_RANK], c.psum[:, t, 0:Q_RANK],
                                            stat[:, 1, t:t + 1], None, ALU.mult)
                    nc.vector.tensor_scalar(normed[:, t, Q_RANK:], c.psum[:, t, Q_RANK:LATENT],
                                            stat[:, 1, NT + t:NT + t + 1], None, ALU.mult).then_inc(norm_done, 1)
                dve.wait_ge(roped, 2)
                nc.vector.tensor_tensor(rot[HD:QK, 0, :], c.psum[HD:QK, 4, :], c.cos[HD:QK, :], ALU.mult)
                ch.link(nc.vector.tensor_tensor(rot[HD:QK, 1, :], c.psum[HD:QK, 5, :], c.sin[HD:QK, :], ALU.mult))
                for e in range(2):
                    nc.vector.tensor_tensor(m.k_full[HD:QK, e, :], rot[HD:QK, 0, :], rot[HD:QK, 1, :], ALU.add)
                dve.wait_ge(g_here, 32)
                for k in range(3):
                    dve.wait_ge(turned, k + 1)
                    ins = nc.vector.tensor_scalar(m.lat_t[:, k, :], c.psum[:, k, :], g[:, k:k + 1], None, ALU.mult)
                ch.link(ins)


def load_sb_weights(sp, m, l, w_in, p, n, here):
    sp.dma_start(m.sb_w[:, n], w_in[bass.ds(l, 1), :, bass.ds(p * P + n * D_SB, P)]
                 .rearrange("o (c p) n -> p (o c) n", p=P)).then_inc(here, 16)


def stick_breaking(nc, c, m, l, w_in, w_uq, w_ukv):
    with ExitStack() as ctx:
        def sb(name, shape, dt=F32):
            return ctx.enter_context(nc.sbuf_tensor(name, shape, dt))
        w = m.sb_w
        w_parts = [sb(f"sb_w_{n}", [P, 2, ND, P], F32R) for n in ("hi", "lo")]
        q, k_ = sb("sb_q", [P, S]), sb("sb_k", [P, S])
        v = sb("sb_v", [P, NT, P])
        soft = sb("sb_soft", [P, 2, PACKED])
        soft_parts = [sb(f"sb_soft_{n}", [P, 2, PACKED], F32R) for n in ("hi", "lo")]
        wts = sb("sb_wts", [P, 2, PACKED])
        x_parts = (m.x_hi, m.x_lo)
        names = ["w_here_q", "w_here_k", "w_here_v", "w_split_q", "w_split_k", "made_q", "made_k", "made_v",
                 "q_out", "k_out", "v_out", "scored", "sized", "exped", "logged", "soft_done", "masked", "soft_split",
                 "summed", "weighed", "ready", "mixed", "stored", "dve_chain", "passed", "later_here"]
        with phase(nc, names) as (block, w_here_q, w_here_k, w_here_v, w_split_q, w_split_k, made_q, made_k, made_v,
                                  q_out, k_out, v_out, scored, sized, exped, logged, soft_done, masked, soft_split,
                                  summed, weighed, ready, mixed, stored, chain, passed, later_here):
            z = [c.flat[:, 1536 * e:1536 * e + PACKED] for e in range(2)]
            w_here, w_split, made = (w_here_q, w_here_k, w_here_v), (w_split_q, w_split_k), (made_q, made_k)

            @block.sync
            def _(sp):
                load_la_pair(sp, m, l, w_uq, w_ukv, 0, later_here)
                sp.dma_start(m.la_wkv[:].rearrange("p e h n -> p (e h n)"),
                             w_ukv[bass.ds(l, 1)].rearrange("o p n -> p (o n)")).then_inc(later_here, 16)
                with sp.Fori(1, PAIRS) as p:
                    for n in range(2):
                        sp.wait_ge(w_split[n], p)
                        load_sb_weights(sp, m, l, w_in, p, n, w_here[n])
                    sp.wait_ge(made_v, p)
                    load_sb_weights(sp, m, l, w_in, p, 2, w_here_v)
                sp.wait_ge(later_here, 112 + 16)

            @block.tensor
            def _(pe):
                def project(p, n):
                    pe.wait_ge(w_split[n], p + 1)
                    for k in range(ND):
                        for m_, (i, j) in enumerate(PARTS):
                            mm = nc.tensor.matmul(c.psum[:, 6 + n, :], w_parts[i][:, n, k, :], x_parts[j][:, k, :],
                                                  start=k + m_ == 0, stop=k == ND - 1 and m_ == 2)
                    mm.then_inc(made[n], 1)

                def turn(p, last):
                    pe.wait_ge(q_out, p + 1)
                    pe.wait_ge(k_out, p + 1)
                    for e in range(2):
                        for s in (0, 1, 3, 2):
                            mm = nc.tensor.matmul(cols(z[e], SB_AT[s], S - s * P),
                                                  k_[HD * e:HD * (e + 1), s * P:(s + 1) * P],
                                                  q[HD * e:HD * (e + 1), s * P:], start=s != 3, stop=False,
                                                  skip_group_check=True)
                        mm.then_inc(scored, 1)
                    pe.wait_ge(w_here_v, p * 16 + CREDIT)
                    for t in range(NT):
                        for k in range(ND):
                            mm = nc.tensor.matmul(c.psum[:, 6, t * P:(t + 1) * P],
                                                  c.xt[:, k, t * P:(t + 1) * P], w[:, 2, k, :],
                                                  start=k == 0, stop=k == ND - 1)
                    mm.then_inc(made_v, 1)
                    if not last:
                        pe.wait_ge(v_out, p + 1)
                        project(p + 1, 0)
                    for e in range(2):
                        pe.wait_ge(soft_split, p * 2 + e + 1)
                        for j in range(NT):
                            for s in range(j + 1):
                                out = cols(z[e], SB_AT[s] + (j - s) * P, S - j * P)
                                for i in range(2):
                                    mm = nc.tensor.matmul(out, (c.neg_tri_r if s == j else c.neg_ones_r)[:],
                                                          cols(soft_parts[i][:, e], SB_AT[j], S - j * P),
                                                          start=False, stop=s == j and i == 1,
                                                          skip_group_check=True)
                        mm.then_inc(summed, 1)
                    if not last:
                        pe.wait_ge(stored, p + CREDIT)
                        project(p + 1, 1)
                        pe.wait_ge(k_out, p + 2)
                    else:
                        pe.wait_ge(stored, p + CREDIT)
                    pe.wait_ge(v_out, p + 1)
                    for e in range(2):
                        pe.wait_ge(ready, p * 2 + e + 1)
                        for s in range(NT):
                            mm = nc.tensor.matmul(c.psum[HD * e:HD * (e + 1), 7, s * P:],
                                                  v[:, s, HD * e:HD * (e + 1)],
                                                  cols(wts[:, e], SB_AT[s], S - s * P),
                                                  start=s == 0, stop=s == NT - 1, skip_group_check=True)
                    mm.then_inc(mixed, 1)

                project(0, 0)
                project(0, 1)
                with pe.Fori(0, PAIRS - 1) as p:
                    turn(p, False)
                turn(PAIRS - 1, True)

            @block.scalar
            def _(act):
                def take_q(p):
                    act.wait_ge(made_q, p + 1)
                    nc.scalar.mul(q[:], c.psum[:, 6, :], HD ** -0.5).then_inc(q_out, 1)

                def take_k(p):
                    act.wait_ge(made_k, p + 1)
                    nc.scalar.copy(k_[:], c.psum[:, 7, :]).then_inc(k_out, 1)

                def turn(p, last):
                    for e in range(2):
                        act.wait_ge(scored, p * 2 + e + 1)
                        nc.scalar.activation(soft[:, e], z[e], ACT.Abs).then_inc(sized, 1)
                        act.wait_ge(sized, p * 2 + e + 1)
                        nc.scalar.activation(soft[:, e], soft[:, e], ACT.Exp, scale=-1.0).then_inc(exped, 1)
                        act.wait_ge(exped, p * 2 + e + 1)
                        nc.scalar.activation(soft[:, e], soft[:, e], ACT.Ln, bias=c.ones[:, 0:1]).then_inc(logged, 1)
                    act.wait_ge(made_v, p + 1)
                    nc.scalar.copy(v[:].rearrange("p t n -> p (t n)"), c.psum[:, 6, :]).then_inc(v_out, 1)
                    if not last:
                        take_q(p + 1)
                    for e in range(2):
                        act.wait_ge(summed, p * 2 + e + 1)
                        nc.scalar.activation(wts[:, e], z[e], ACT.Exp).then_inc(weighed, 1)
                    if not last:
                        take_k(p + 1)
                    act.wait_ge(mixed, p + 1)
                    nc.scalar.copy(m.mixed_t[:, bass.ds(p, 1), :].rearrange("p o t -> p (o t)"),
                                   c.psum[:, 7, :]).then_inc(stored, 1)

                take_q(0)
                take_k(0)
                with act.Fori(0, PAIRS - 1) as p:
                    turn(p, False)
                turn(PAIRS - 1, True)

            @block.vector
            def _(dve):
                ch = Chain(dve, chain)

                def split_w(p, n, first=False):
                    if not first:
                        dve.wait_ge(w_here[n], p * 16)
                        dve.wait_ge(made[n], p)
                    split(nc, ch, w[:, n], w_parts[0][:, n], w_parts[1][:, n]).then_inc(w_split[n], 1)

                def soften(p, e):
                    dve.wait_ge(logged, p * 2 + e + 1)
                    nc.vector.scalar_tensor_tensor(out=soft[:, e], in0=z[e], scalar=0.0, in1=soft[:, e],
                                                   op0=ALU.max, op1=ALU.add).then_inc(soft_done, 1)

                def split_soft(p, e):
                    dve.wait_ge(masked, p * 2 + e + 1)
                    split(nc, ch, soft[:, e], soft_parts[0][:, e], soft_parts[1][:, e]).then_inc(soft_split, 1)

                def turn(p, last):
                    if not last:
                        split_w(p + 1, 0)
                    soften(p, 0)
                    if not last:
                        split_w(p + 1, 1)
                    split_soft(p, 0)
                    soften(p, 1)
                    split_soft(p, 1)

                split_w(0, 0, True)
                split_w(0, 1, True)
                ch.credit = ch.n
                with dve.Fori(0, PAIRS - 1) as p:
                    ch.turn(p, 4)
                    turn(p, False)
                ch.turned(PAIRS - 1)
                turn(PAIRS - 1, True)

            @block.gpsimd
            def _(pool):
                pool.sem_inc(stored, CREDIT)
                pool.sem_inc(w_here_v, CREDIT)
                with pool.Fori(0, PAIRS) as p:
                    for sem, done, tile in ((soft_done, masked, soft), (weighed, ready, wts)):
                        for e in range(2):
                            pool.wait_ge(sem, p * 2 + e + 1)
                            pool.sem_inc(passed, 1)
                            for s in range(NT):
                                diag = cols(tile[:, e], SB_AT[s], P)
                                ins = nc.gpsimd.affine_select(out=diag, in_=diag, compare_op=ALU.is_gt, fill=0.0,
                                                              base=0, pattern=[[1, P]], channel_multiplier=-1)
                            ins.then_inc(done, 1)


def load_la_pair(sp, m, l, w_uq, w_ukv, p, here):
    uq = w_uq[bass.ds(l, 1), :, bass.ds(p * 2 * QK, 2 * QK)].rearrange("o (c p) (e n) -> p (o c) e n", p=P, e=2)
    for k in range(2):
        sp.dma_start(m.la_wq[:, k], uq[:, k]).then_inc(here, 16)
        sp.dma_start(m.la_wq_swap[:, k, :, 0:ROPE // 2], uq[:, k, :, HD + ROPE // 2:]).then_inc(here, 16)
        sp.dma_start(m.la_wq_swap[:, k, :, ROPE // 2:], uq[:, k, :, HD:HD + ROPE // 2]).then_inc(here, 16)
    sp.dma_start(m.la_wk[:], w_ukv[bass.ds(l, 1), :, bass.ds(p * 4 * HD, 4 * HD)].rearrange(
        "o p (e h n) -> p (o e) h n", e=2, h=2)[:, :, 0, :]).then_inc(here, 16)


def latent_attention(nc, c, m, l, w_uq, w_ukv, w_o, ln_g, ln_b):
    with ExitStack() as ctx:
        def sb(name, shape):
            return ctx.enter_context(nc.sbuf_tensor(name, shape, F32))
        wq, wq_swap, wk, wkv = m.la_wq, m.la_wq_swap, m.la_wk, m.la_wkv
        q = sb("la_q", [P, 2, S])
        rot = sb("la_rot", [P, 2, 2, S])
        v = sb("la_v", [P, NT, P])
        probs = sb("la_probs", [P, 2, PACKED])
        probs_t = sb("la_probs_t", [P, 2, PACKED])
        peak = sb("la_peak", [P, 2, NT])
        bias = sb("la_bias", [P, 2, NT])
        total = sb("la_total", [P, 2, NT])
        share = sb("la_share", [P, 2, NT])
        scale = QK ** -0.5
        names = ["w_here", "q_made", "k_made", "v_made", "q_out", "k_out", "v_out", "scored", "biased",
                 "exped", "scaled", "turned", "turned_out", "mixed", "stored", "dve_chain",
                 "later_here"]
        with phase(nc, names) as (block, w_here, q_made, k_made, v_made, q_out, k_out, v_out, scored,
                                  biased, exped, scaled, turned, turned_out, mixed, stored, chain,
                                  later_here):
            sc = [c.flat[:, 1536 * e:1536 * e + PACKED] for e in range(2)]
            give_credit(block, (stored, turned_out))

            @block.sync
            def _(sp):
                def load_next(p):
                    sp.wait_ge(k_made, p * 2)
                    load_la_pair(sp, m, l, w_uq, w_ukv, p, w_here)

                load_next(1)
                for k in range(0, ND, 2):
                    sp.dma_start(m.w_out[:, k:k + 2], w_o[bass.ds(l, 1), k * P:(k + 2) * P]
                                 .rearrange("o (c p) n -> p (o c) n", p=P)).then_inc(later_here, 16)
                sp.dma_start(m.ln.g[:], ln_g[bass.ds(l, 1)].broadcast_to([P, D])).then_inc(later_here, 16)
                sp.dma_start(m.ln.b[:], ln_b[bass.ds(l, 1)].broadcast_to([P, D])).then_inc(later_here, 16)
                with sp.Fori(2, PAIRS) as p:
                    load_next(p)
                sp.wait_ge(later_here, 16 * (ND // 2 + 2))

            @block.tensor
            def _(pe):
                def make_qk(p, first):
                    if not first:
                        pe.wait_ge(w_here, p * 112)
                        pe.wait_ge(v_out, p)
                        pe.wait_ge(stored, p - 1 + CREDIT)
                    for e in range(2):
                        if e == 1:
                            pe.wait_ge(q_out, p * 4 + 2)
                            pe.wait_ge(k_out, p * 2 + 1)
                        for k in range(2):
                            nc.tensor.matmul(c.psum[0:QK, 6, :], wq[:, k, e, :], m.lat_t[:, k, :],
                                             start=k == 0, stop=k == 1)
                        for k in range(2):
                            mm = nc.tensor.matmul(c.psum[HD:QK, 7, :], wq_swap[:, k, e, :], m.lat_t[:, k, :],
                                                  start=k == 0, stop=k == 1)
                        mm.then_inc(q_made, 1)
                        mm = nc.tensor.matmul(c.psum[0:HD, 7, :], wk[:, e, :], m.lat_t[:, 2, :],
                                              start=True, stop=True)
                        mm.then_inc(k_made, 1)

                def turn(p, last):
                    pe.wait_ge(turned_out, p * 2 + CREDIT)
                    pe.wait_ge(q_out, p * 4 + 4)
                    pe.wait_ge(k_out, p * 2 + 2)
                    for e in range(2):
                        for t in (3, 2, 0, 1):
                            mm = nc.tensor.matmul(cols(sc[e], LA_AT[t], (t + 1) * P),
                                                  q[0:QK, e, t * P:(t + 1) * P], m.k_full[0:QK, e, 0:(t + 1) * P],
                                                  start=True, stop=True)
                        mm.then_inc(scored, 1)
                    for t in range(NT):
                        mm = nc.tensor.matmul(c.psum[:, 6, t * P:(t + 1) * P], m.lat_t[:, 2, t * P:(t + 1) * P],
                                              wkv[:, bass.ds(p * 2, 2), 1, :], start=True, stop=True)
                    mm.then_inc(v_made, 1)
                    if not last:
                        make_qk(p + 1, False)
                    for e in range(2):
                        pe.wait_ge(scaled, p * 2 + e + 1)
                        for s in range(NT):
                            for t in range(s, NT):
                                mm = nc.tensor.transpose(cols(sc[e], SB_AT[s] + (t - s) * P, P),
                                                         cols(probs[:, e], LA_AT[t] + s * P, P), c.ident[:])
                        mm.then_inc(turned, 1)
                    pe.wait_ge(v_out, p + 1)
                    if not last:
                        pe.wait_ge(q_out, p * 4 + 8)
                        pe.wait_ge(k_out, p * 2 + 4)
                    for e in range(2):
                        pe.wait_ge(turned_out, p * 2 + e + 1 + CREDIT)
                        for s in range(NT):
                            mm = nc.tensor.matmul(c.psum[HD * e:HD * (e + 1), 7, s * P:],
                                                  v[:, s, HD * e:HD * (e + 1)],
                                                  cols(probs_t[:, e], SB_AT[s], S - s * P),
                                                  start=s == 0, stop=s == NT - 1, skip_group_check=True)
                    mm.then_inc(mixed, 1)

                make_qk(0, True)
                with pe.Fori(0, PAIRS - 1) as p:
                    turn(p, False)
                turn(PAIRS - 1, True)

            @block.scalar
            def _(act):
                def take_qk(p):
                    for e in range(2):
                        act.wait_ge(q_made, p * 2 + (e + 1))
                        nc.scalar.copy(q[0:HD, e, :], c.psum[0:HD, 6, :]).then_inc(q_out, 1)
                        act.wait_ge(k_made, p * 2 + (e + 1))
                        nc.scalar.copy(m.k_full[0:HD, e, :], c.psum[0:HD, 7, :]).then_inc(k_out, 1)

                def turn(p, last):
                    act.wait_ge(v_made, p + 1)
                    nc.scalar.copy(v[:].rearrange("p t n -> p (t n)"), c.psum[:, 6, :]).then_inc(v_out, 1)
                    for e in range(2):
                        act.wait_ge(biased, p * 2 + e + 1)
                        for t in range(NT):
                            at = cols(probs[:, e], LA_AT[t], (t + 1) * P)
                            ins = nc.scalar.activation(at, cols(sc[e], LA_AT[t], (t + 1) * P), ACT.Exp,
                                                       bias=bias[:, e, t:t + 1], scale=scale,
                                                       accum_out=total[:, e, t:t + 1])
                        ins.then_inc(exped, 1)
                    if not last:
                        take_qk(p + 1)
                    for e in range(2):
                        act.wait_ge(turned, p * 2 + e + 1)
                        nc.scalar.copy(probs_t[:, e], sc[e]).then_inc(turned_out, 1)
                    act.wait_ge(mixed, p + 1)
                    nc.scalar.copy(m.mixed_t[:, bass.ds(p + PAIRS, 1), :].rearrange("p o t -> p (o t)"),
                                   c.psum[:, 7, :]).then_inc(stored, 1)

                take_qk(0)
                with act.Fori(0, PAIRS - 1) as p:
                    turn(p, False)
                turn(PAIRS - 1, True)

            @block.vector
            def _(dve):
                ch = Chain(dve, chain)

                def rotate(p, e):
                    dve.wait_ge(q_made, p * 2 + (e + 1))
                    nc.vector.tensor_tensor(rot[HD:QK, e, 0, :], c.psum[HD:QK, 6, :], c.cos[HD:QK, :], ALU.mult)
                    ch.link(nc.vector.tensor_tensor(rot[HD:QK, e, 1, :], c.psum[HD:QK, 7, :], c.sin[HD:QK, :],
                                                    ALU.mult))
                    nc.vector.tensor_tensor(q[HD:QK, e, :], rot[HD:QK, e, 0, :], rot[HD:QK, e, 1, :],
                                            ALU.add).then_inc(q_out, 1)

                def divide(p, e):
                    dve.wait_ge(exped, p * 2 + e + 1)
                    ch.link(nc.vector.reciprocal(share[:, e, :], total[:, e, :]))
                    for t in range(NT):
                        at = cols(probs[:, e], LA_AT[t], (t + 1) * P)
                        ins = nc.vector.tensor_scalar(at, at, share[:, e, t:t + 1], None, ALU.mult)
                    ins.then_inc(scaled, 1)

                def turn(p, last):
                    for e in range(2):
                        dve.wait_ge(scored, p * 2 + e + 1)
                        for t in range(NT):
                            diag = cols(sc[e], LA_AT[t] + t * P, P)
                            ins = nc.vector.tensor_tensor(diag, diag, c.neg_mask[:], ALU.add)
                        ch.link(ins)
                        for t in range(NT):
                            ins = nc.vector.reduce_max(peak[:, e, t:t + 1], cols(sc[e], LA_AT[t], (t + 1) * P), AX_X)
                        ch.link(ins)
                        nc.vector.tensor_scalar(bias[:, e, :], peak[:, e, :], -scale, None,
                                                ALU.mult).then_inc(biased, 1)
                    if not last:
                        rotate(p + 1, 0)
                    divide(p, 0)
                    divide(p, 1)
                    if not last:
                        rotate(p + 1, 1)

                rotate(0, 0)
                rotate(0, 1)
                ch.credit = ch.n
                with dve.Fori(0, PAIRS - 1) as p:
                    ch.turn(p, 8)
                    turn(p, False)
                ch.turned(PAIRS - 1)
                turn(PAIRS - 1, True)


def layer_norm_steps(nc, dve, ch, c, ln, t):
    for h in range(2):
        ins = nc.vector.bn_stats(ln.stats[:, t, h, :], c.x[:, t, h * HALF:(h + 1) * HALF])
    ch.link(ins)
    ch.link(nc.vector.bn_aggr(ln.mv[:, t, :], ln.stats[:, t].rearrange("p h s -> p (h s)")))
    nc.vector.tensor_scalar(ln.var[:, t:t + 1], ln.mv[:, t, 1:2], LN_EPS, None, ALU.add).then_inc(ln.var_done, 1)
    dve.wait_ge(ln.rooted, t + 1)
    ch.link(nc.vector.reciprocal(ln.rstd[:, t:t + 1], ln.root[:, t:t + 1]))
    ch.link(nc.vector.tensor_scalar(c.x[:, t, :], c.x[:, t, :], ln.mv[:, t, 0:1], ln.rstd[:, t:t + 1],
                                    ALU.subtract, ALU.mult))
    ch.link(nc.vector.tensor_tensor(c.x[:, t, :], c.x[:, t, :], ln.g[:], ALU.mult))
    ch.link(nc.vector.tensor_tensor(c.x[:, t, :], c.x[:, t, :], ln.b[:], ALU.add))


class Norm:

    def __init__(self, nc, ctx, name):
        def sb(part, shape):
            return ctx.enter_context(nc.sbuf_tensor(f"{name}_{part}", shape, F32))
        self.g, self.b = sb("g", [P, D]), sb("b", [P, D])
        self.stats, self.mv = sb("stats", [P, NT, 2, 6]), sb("mv", [P, NT, 2])
        self.var, self.root, self.rstd = sb("var", [P, NT]), sb("root", [P, NT]), sb("rstd", [P, NT])


def project_out(nc, c, m):
    w, ln = m.w_out, m.ln
    with phase(nc, ["projected", "dve_chain", "var_done", "rooted"]) as (block, projected, chain, ln.var_done,
                                                                       ln.rooted):
        @block.tensor
        def _(pe):
            for t in range(NT):
                for h in range(2):
                    for k in range(ND):
                        mm = nc.tensor.matmul(c.psum[:, 2 * t + h, :], m.mixed_t[:, k, t * P:(t + 1) * P],
                                              w[:, k, h * HALF:(h + 1) * HALF], start=k == 0, stop=k == ND - 1)
                    mm.then_inc(projected, 1)

        @block.vector
        def _(dve):
            ch = Chain(dve, chain)
            for t in range(NT):
                for h in range(2):
                    dve.wait_ge(projected, 2 * t + h + 1)
                    half = c.x[:, t, h * HALF:(h + 1) * HALF]
                    ins = nc.vector.scalar_tensor_tensor(out=half, in0=half, scalar=ALPHA,
                                                         in1=c.psum[:, 2 * t + h, :], op0=ALU.mult, op1=ALU.add)
                ch.link(ins)
                layer_norm_steps(nc, dve, ch, c, ln, t)

        @block.scalar
        def _(act):
            for t in range(NT):
                act.wait_ge(ln.var_done, t + 1)
                nc.scalar.activation(ln.root[:, t:t + 1], ln.var[:, t:t + 1], ACT.Sqrt).then_inc(ln.rooted, 1)


def residual_norm(nc, c, l, ffn, ln_g, ln_b):
    with ExitStack() as ctx:
        ln = Norm(nc, ctx, "ln2")
        offset = ctx.enter_context(nc.sbuf_tensor("ln2_offset", [P, NT], F32))
        with phase(nc, ["params_here", "dve_chain", "rooted", "stood", "scaled", "pooled"]) as (
                block, params_here, chain, rooted, stood, scaled, pooled):
            @block.sync
            def _(sp):
                sp.dma_start(ln.g[:], ln_g[bass.ds(l, 1)].broadcast_to([P, D])).then_inc(params_here, 16)
                sp.dma_start(ln.b[:], ln_b[bass.ds(l, 1)].broadcast_to([P, D])).then_inc(params_here, 16)

            @block.vector
            def _(dve):
                ch = Chain(dve, chain)
                for t in range(NT):
                    ins = nc.vector.scalar_tensor_tensor(out=c.x[:, t, :], in0=c.x[:, t, :], scalar=ALPHA,
                                                         in1=ffn[:, t, :], op0=ALU.mult, op1=ALU.add)
                ch.link(ins)
                for t in range(NT):
                    for h in range(2):
                        ins = nc.vector.bn_stats(ln.stats[:, t, h, :], c.x[:, t, h * HALF:(h + 1) * HALF])
                ch.link(ins)
                for t in range(NT):
                    ins = nc.vector.bn_aggr(ln.mv[:, t, :], ln.stats[:, t].rearrange("p h s -> p (h s)"))
                ch.link(ins)
                ch.link(nc.vector.tensor_scalar(ln.var[:], ln.mv[:, :, 1], LN_EPS, None, ALU.add))
                dve.wait_ge(rooted, 1)
                ch.link(nc.vector.reciprocal(ln.rstd[:], ln.root[:]))
                nc.vector.scalar_tensor_tensor(out=offset[:], in0=ln.mv[:, :, 0], scalar=-1.0, in1=ln.rstd[:],
                                               op0=ALU.mult, op1=ALU.mult).then_inc(stood, 1)
                dve.wait_ge(params_here, 32)
                for t in range(NT):
                    dve.wait_ge(scaled, t + 1)
                    ins = nc.vector.tensor_tensor(c.x[:, t, :], c.x[:, t, :], ln.g[:], ALU.mult)
                    if t < NT - 1:
                        ins.then_inc(pooled, 1)
                    else:
                        ch.link(ins)
                nc.vector.tensor_tensor(c.x[:, NT - 1, :], c.x[:, NT - 1, :], ln.b[:], ALU.add)

            @block.scalar
            def _(act):
                act.wait_ge(chain, 4)
                nc.scalar.activation(ln.root[:], ln.var[:], ACT.Sqrt).then_inc(rooted, 1)
                act.wait_ge(stood, 1)
                for t in range(NT):
                    nc.scalar.activation(c.x[:, t, :], c.x[:, t, :], ACT.Identity, bias=offset[:, t:t + 1],
                                         scale=ln.rstd[:, t:t + 1]).then_inc(scaled, 1)

            @block.gpsimd
            def _(pool):
                pool.wait_ge(params_here, 32)
                for t in range(NT - 1):
                    pool.wait_ge(pooled, t + 1)
                    nc.gpsimd.tensor_tensor(c.x[:, t, :], c.x[:, t, :], ln.b[:], ALU.add)


def route(nc, c, r, l, w_q, keys):
    with ExitStack() as ctx:
        def sb(name, shape, dt=F32):
            return ctx.enter_context(nc.sbuf_tensor(name, shape, dt))
        w = sb("rt_w", [P, 2, ND, P])
        key = sb("rt_key", [P, 2, P])
        key_t = sb("rt_key_t", [P, 2, P])
        q = sb("rt_q", [P, 2, S])
        score = sb("rt_score", [P, NT, 2, N_KEYS])
        score2 = sb("rt_score2", [P, NT, 2, N_KEYS])
        best = sb("rt_best", [P, NT, 2, TOPK])
        best_at = sb("rt_best_at", [P, NT, 2, TOPK], U32)
        best_key = sb("rt_best_key", [P, NT, 2, TOPK])
        WIDE, NARROW = 4, 4
        assert (WIDE + 1) * (NARROW + 1) > TOPK and WIDE == NARROW
        SPLIT = WIDE * TOPK
        CAND = SPLIT + (TOPK - WIDE) * NARROW
        cand = sb("rt_cand", [P, NT, CAND])
        cand2 = sb("rt_cand2", [P, NT, CAND])
        top = sb("rt_top", [P, NT, TOPK])
        top_at = sb("rt_top_at", [P, NT, TOPK], U32)
        part = sb("rt_part", [P, 2, NT, TOPK], U32)
        part_f = sb("rt_part_f", [P, 2, NT, TOPK])
        place = sb("rt_place", [P, NT, TOPK])
        before = sb("rt_before", [P, 2, NT, TOPK])
        rank = sb("rt_rank", [P, 2, NT, TOPK], BF16)
        hit = sb("rt_hit", [P, 2, NT, TOPK, TOPK], BF16)
        names = ["w_here0", "w_here1", "key_here", "keys_turned", "q_made", "keys_out", "q_out", "scored",
                 "score_out", "hit_made", "looked_up", "dve_chain", "passed", "x_turned", "x_copied"]
        PER = 15
        with phase(nc, names) as (block, w_here0, w_here1, key_here, keys_turned, q_made, keys_out, q_out, scored,
                                  score_out, hit_made, looked_up, chain, passed, x_turned,
                                  x_copied):
            w_here = (w_here0, w_here1)

            @block.sync
            def _(sp):
                with sp.Fori(0, P_HEADS) as h:
                    sp.wait_ge(keys_turned, h + CREDIT)
                    sp.dma_start(key[:], keys[bass.ds(l, 1), bass.ds(h, 1)]
                                 .rearrange("o h c n k -> n (o h c) k")).then_inc(key_here, 16)
                    for half in range(2):
                        sp.wait_ge(q_made, h * 2 + half + 1)
                        sp.dma_start(w[:, half], w_q[bass.ds(l, 1), :, bass.ds(h * (2 * P) + half * P, P)]
                                     .rearrange("o (c p) n -> p (o c) n", p=P)).then_inc(w_here[half], 16)

            @block.gpsimd
            def _(pool):
                nc.gpsimd.memset(hit[:], 0.0).then_inc(looked_up, 2)
                for sem, n in ((keys_turned, CREDIT), (q_made, 2), (keys_out, CREDIT), (score_out, CREDIT),
                               (chain, PER)):
                    pool.sem_inc(sem, n)
                with pool.Fori(0, P_HEADS) as h:
                    for half in range(2):
                        pool.wait_ge(hit_made, h * 2 + half + 1)
                        nc.gpsimd.tensor_tensor(
                            hit[:, half], hit[:, half],
                            best_key[:, :, half, :].unsqueeze(3).broadcast_to([P, NT, TOPK, TOPK]),
                            ALU.mult).then_inc(looked_up, 1)

            @block.tensor
            def _(pe):
                turn_x(nc, c, pe, x_turned, x_copied)
                with pe.Fori(0, P_HEADS) as h:
                    pe.wait_ge(key_here, h * 16 + 16)
                    pe.wait_ge(keys_out, h + CREDIT)
                    for half in range(2):
                        mm = nc.tensor.transpose(c.psum[:, 0, half * P:(half + 1) * P], key[:, half, :], c.ident[:])
                    mm.then_inc(keys_turned, 1)
                    for half in range(2):
                        pe.wait_ge(w_here[half], h * 16 + 16)
                        for k in range(ND):
                            mm = nc.tensor.matmul(c.psum[:, 1 + half, :], w[:, half, k, :],
                                                  c.xt[:, k, :], start=k == 0, stop=k == ND - 1)
                        mm.then_inc(q_made, 1)
                    pe.wait_ge(keys_out, h + 1 + CREDIT)
                    pe.wait_ge(q_out, h * 2 + 2)
                    pe.wait_ge(score_out, h + CREDIT)
                    for t in range(NT):
                        for half in range(2):
                            mm = nc.tensor.matmul(c.flat[:, 2048 + (2 * t + half) * P:2048 + (2 * t + half + 1) * P],
                                                  q[:, half, t * P:(t + 1) * P], key_t[:, half, :],
                                                  start=True, stop=True)
                    mm.then_inc(scored, 1)

            @block.scalar
            def _(act):
                take_x(nc, c, act, x_turned, x_copied)
                with act.Fori(0, P_HEADS) as h:
                    act.wait_ge(keys_turned, h + 1 + CREDIT)
                    nc.scalar.copy(key_t[:].rearrange("p c k -> p (c k)"), c.psum[:, 0, 0:2 * P]).then_inc(keys_out, 1)
                    for half in range(2):
                        act.wait_ge(q_made, h * 2 + half + 1 + 2)
                        nc.scalar.copy(q[:, half, :], c.psum[:, 1 + half, :]).then_inc(q_out, 1)
                    act.wait_ge(scored, h + 1)
                    act.wait_ge(chain, h * PER + 2)
                    nc.scalar.copy(score[:].rearrange("p t c n -> p (t c n)"),
                                   c.flat[:, 2048:2048 + NT * 2 * N_KEYS]).then_inc(score_out, 1)

            @block.vector
            def _(dve):
                ch = Chain(dve, chain, PER, passed)

                def top16(pairs):
                    for values, spare, out, at in pairs:
                        ins = nc.vector.max(out[:, 0:8], values)
                    ch.link_plain(ins)
                    for values, spare, out, at in pairs:
                        nc.vector.max_index(at[:, 0:8], out[:, 0:8], values)
                    for values, spare, out, at in pairs:
                        ins = nc.vector.match_replace(spare, out[:, 0:8], values, NEG)
                    ch.link_plain(ins)
                    for values, spare, out, at in pairs:
                        ins = nc.vector.max(out[:, 8:16], spare)
                    ch.link_plain(ins)
                    for values, spare, out, at in pairs:
                        ins = nc.vector.max_index(at[:, 8:16], out[:, 8:16], spare)
                    ch.link_plain(ins)

                with dve.Fori(0, P_HEADS) as h:
                    ch.turn(h, PER)
                    dve.wait_ge(score_out, h + 1 + CREDIT)
                    dve.sem_inc(passed, 1)
                    top16([(score[:, t, half, :], score2[:, t, half, :], best[:, t, half, :], best_at[:, t, half, :])
                           for t in range(NT) for half in range(2)])
                    for half in range(2):
                        dve.wait_ge(looked_up, h * 2 + half + 1)
                        nc.vector.tensor_reduce(
                            r.index[:, half, :, bass.ds(h, 1), :].rearrange("p t o k -> p t (o k)"),
                            hit[:, half].rearrange("p t a k -> p t k a"), AX_X, ALU.add)
                    nc.vector.tensor_copy(best_key[:], best_at[:])
                    nc.vector.tensor_tensor(
                        cand[:, :, 0:SPLIT].rearrange("p t (a b) -> p t a b", a=WIDE),
                        best[:, :, 0, 0:WIDE].unsqueeze(3).broadcast_to([P, NT, WIDE, TOPK]),
                        best[:, :, 1, :].unsqueeze(2).broadcast_to([P, NT, WIDE, TOPK]), ALU.add)
                    ch.link_plain(nc.vector.tensor_tensor(
                        cand[:, :, SPLIT:].rearrange("p t (a b) -> p t a b", b=NARROW),
                        best[:, :, 0, WIDE:].unsqueeze(3).broadcast_to([P, NT, TOPK - WIDE, NARROW]),
                        best[:, :, 1, 0:NARROW].unsqueeze(2).broadcast_to([P, NT, TOPK - WIDE, NARROW]), ALU.add))
                    top16([(cand[:, t], cand2[:, t], top[:, t, :], top_at[:, t, :]) for t in range(NT)])
                    at_h = bass.ds(h, 1)
                    nc.vector.tensor_scalar(part[:, 0], top_at[:], 4, None, ALU.logical_shift_right)
                    ch.link(nc.vector.tensor_scalar(part[:, 1], top_at[:], 2, None, ALU.logical_shift_right))
                    nc.vector.tensor_copy(place[:], top_at[:])
                    ch.link(nc.vector.tensor_copy(part_f[:], part[:]))
                    ch.link(nc.vector.scalar_tensor_tensor(
                        out=rank[:, 0], in0=part_f[:, 1], scalar=float(WIDE - SPLIT // NARROW), in1=part_f[:, 0],
                        op0=ALU.add, op1=ALU.max))
                    ch.link(nc.vector.tensor_scalar(before[:, 0], rank[:, 0], float(NARROW),
                                                    float(SPLIT - WIDE * NARROW), ALU.mult, ALU.add))
                    nc.vector.tensor_copy(r.top[:, :, at_h, :].rearrange("p t o k -> p t (o k)"), top[:])
                    ch.link(nc.vector.scalar_tensor_tensor(out=before[:, 1], in0=rank[:, 0], scalar=float(TOPK),
                                                           in1=before[:, 0], op0=ALU.mult, op1=ALU.min))
                    for half in range(2):
                        if half == 1:
                            ch.link(nc.vector.tensor_tensor(rank[:, 1], place[:], before[:, 1], ALU.subtract))
                        nc.vector.tensor_tensor(
                            hit[:, half], rank[:, half].unsqueeze(2).broadcast_to([P, NT, TOPK, TOPK]),
                            c.count_rows[:].unsqueeze(1).broadcast_to([P, NT, TOPK, TOPK]),
                            ALU.is_equal).then_inc(hit_made, 1)
                ch.turned(P_HEADS)
                for half in range(2):
                    dve.wait_ge(looked_up, P_HEADS * 2 + half + 1)
                    nc.vector.tensor_reduce(r.index[:, half, :, P_HEADS, :],
                                            hit[:, half].rearrange("p t a k -> p t k a"), AX_X, ALU.add)


def gates(nc, c, r):
    with ExitStack() as ctx:
        def sb(name, shape):
            return ctx.enter_context(nc.sbuf_tensor(name, shape, F32))
        e = sb("gt_exp", [P, NT, P_HEADS, TOPK])
        total = sb("gt_total", [P, NT * P_HEADS])
        share = sb("gt_share", [P, NT * P_HEADS])
        with phase(nc, ["dve_chain", "exped", "turned", "evacuated"]) as (block, chain, exped, turned, evacuated):
            ef = e[:].rearrange("p t h k -> p (t h) k")
            shape = [P, NT * P_HEADS, TOPK]

            @block.vector
            def _(dve):
                ch = Chain(dve, chain)
                top = r.top[:].rearrange("p t h k -> p (t h) k")
                ch.link(nc.vector.tensor_tensor(ef, top, top[:, :, 0:1].broadcast_to(shape), ALU.subtract))
                dve.wait_ge(exped, 1)
                ch.link(nc.vector.tensor_reduce(total[:], ef, AX_X, ALU.add))
                ch.link(nc.vector.reciprocal(share[:], total[:]))
                ch.link(nc.vector.tensor_tensor(ef, ef, share[:].unsqueeze(2).broadcast_to(shape), ALU.mult))

            @block.scalar
            def _(act):
                act.wait_ge(chain, 1)
                nc.scalar.activation(e[:], e[:], ACT.Exp).then_inc(exped, 1)
                for n in range(3):
                    act.wait_ge(turned, n + 1)
                    nc.scalar.copy(r.turned[:, n, :], c.psum[:, n, :]).then_inc(evacuated, 1)

            @block.tensor
            def _(pe):
                for n, tile in enumerate((r.index[:, 0, :, 1:], r.index[:, 1, :, 1:], e)):
                    if n == 2:
                        pe.wait_ge(chain, 4)
                    for t in range(NT):
                        mm = nc.tensor.transpose(c.psum[:, n, t * P:(t + 1) * P],
                                                 tile[:, t].rearrange("p h k -> p (h k)"), c.ident[:])
                    mm.then_inc(turned, 1)


def spread_gates(nc, c, r, gate_dram):
    RING = 8
    GATE_RING = 4
    GROUPS = P // 4
    BODY = 8
    TILE_TURNS = GROUPS // BODY
    TURNS = NT * TILE_TURNS
    LAG = 3
    ONE_HOT_BY = "PADPAPAD"
    with ExitStack() as ctx:
        hot_j = ctx.enter_context(nc.sbuf_tensor("sg_hot_j", [P, RING, 4, N_KEYS], F32))
        gate_i = ctx.enter_context(nc.sbuf_tensor("sg_gate_i", [P, GATE_RING, 4, N_KEYS], F32))
        apart = ctx.enter_context(nc.sbuf_tensor("sg_apart", [P, 4, N_KEYS], F32))
        pool_j = ctx.enter_context(nc.sbuf_tensor("sg_pool_j", [P, BODY, 4], F32))
        out = [ctx.enter_context(nc.sbuf_tensor(f"sg_out{b}", [P, N_KEYS, P], F32)) for b in range(2)]
        by = {e: ONE_HOT_BY.count(e) for e in "PAD"}
        names = ["made", "hot_pool", "hot_act", "hot_dve", "staged", "apart_done", "passed", "multiplied", "evacuated",
                 "written0", "written1"]
        with phase(nc, names) as (block, made, hot_pool, hot_act, hot_dve, staged, apart_done, passed, multiplied,
                                  evacuated, *written):
            hot = {"P": hot_pool, "A": hot_act, "D": hot_dve}

            def nth(g):
                return ONE_HOT_BY[:g + 1].count(ONE_HOT_BY[g])

            @block.gpsimd
            def _(pool):
                pool.sem_inc(multiplied, RING)
                pool.sem_inc(evacuated, RING)
                pool.sem_inc(hot_pool, by["P"])
                pool.sem_inc(hot_act, by["A"])
                with pool.Fori(0, TURNS) as i:
                    for g in range(BODY):
                        if ONE_HOT_BY[g] != "P":
                            continue
                        pool.wait_ge(staged, i * by["P"] + nth(g))
                        pool.wait_ge(multiplied, i * BODY + (g + 1))
                        pool.sem_inc(passed, 1)
                        for n in range(4):
                            ins = nc.gpsimd.tensor_scalar(hot_j[:, g % RING, n, :], c.count_keys[:],
                                                          pool_j[:, g, n:n + 1], None, ALU.is_equal)
                        ins.then_inc(hot_pool, 1)

            @block.vector
            def _(dve):
                with dve.Fori(0, TURNS) as i:
                    for g in range(BODY):
                        at4 = bass.ds(i * (4 * BODY) + 4 * g, 4)
                        if ONE_HOT_BY[g] == "P":
                            dve.wait_ge(hot_pool, i * by["P"] + nth(g))
                            nc.vector.tensor_copy(pool_j[:, g, :], r.turned[:, 1, at4]).then_inc(staged, 1)
                        dve.wait_ge(multiplied, i * BODY + (g + 1 + RING - GATE_RING))
                        for n in range(4):
                            at = bass.ds(i * (4 * BODY) + (4 * g + n), 1)
                            ins = nc.vector.tensor_scalar(gate_i[:, g % GATE_RING, n, :], c.count_keys[:],
                                                          r.turned[:, 0, at], r.turned[:, 2, at],
                                                          ALU.is_equal, ALU.mult)
                        ins.then_inc(made, 1)
                        if ONE_HOT_BY[g] == "D":
                            nc.vector.tensor_tensor(
                                hot_j[:, g % RING], c.count_keys[:].unsqueeze(1).broadcast_to([P, 4, N_KEYS]),
                                r.turned[:, 1, at4].unsqueeze(2).broadcast_to([P, 4, N_KEYS]),
                                ALU.is_equal).then_inc(hot_dve, 1)

            @block.tensor
            def _(pe):
                with pe.Fori(0, TURNS) as i:
                    for g in range(BODY):
                        e = ONE_HOT_BY[g]
                        pe.wait_ge(made, i * BODY + (g + 1))
                        pe.wait_ge(hot[e], i * by[e] + (nth(g) + (0 if e == "D" else by[e])))
                        pe.wait_ge(evacuated, i * BODY + (g + 1))
                        for n in range(4):
                            mm = nc.tensor.matmul(c.psum[:, g % RING, n * P:(n + 1) * P], hot_j[:, g % RING, n, :],
                                                  gate_i[:, g % GATE_RING, n, :], start=True, stop=True)
                        mm.then_inc(multiplied, 1)

            @block.scalar
            def _(act):
                def one_hot(i, t, g):
                    done = t * by["A"] * TILE_TURNS + nth(g)
                    act.wait_ge(multiplied, i * BODY + (t * GROUPS + g + 1))
                    act.wait_ge(hot_act, i * by["A"] + (done - 1 + by["A"]))
                    for n in range(4):
                        at = bass.ds(i * (4 * BODY) + (t * P + 4 * g + n), 1)
                        ins = nc.scalar.activation(apart[:, n, :], c.count_keys[:], ACT.Abs,
                                                   bias=r.turned[:, 1, at], scale=-1.0)
                    ins.then_inc(apart_done, 1)
                    act.wait_ge(apart_done, i * by["A"] + done)
                    nc.scalar.activation(hot_j[:, g % RING], apart[:], ACT.Relu, bias=c.ones[:, 0:1],
                                         scale=-1.0).then_inc(hot_act, 1)

                def empty(i, t, g):
                    evacuate(nc, c, act, out[t % 2], i, t, g, multiplied, evacuated, GROUPS, BODY, RING)

                def turn(i, t, first):
                    for g in range(BODY):
                        if ONE_HOT_BY[g] == "A":
                            one_hot(i, t, g)
                        if g >= LAG or not first:
                            empty(i, t, g - LAG)

                for t in range(NT):
                    if t >= 2:
                        act.wait_ge(written[t % 2], 64 * (t // 2))
                    turn(0, t, True)
                    with act.Fori(1, TILE_TURNS) as i:
                        turn(i, t, False)
                    for g in range(BODY - LAG, BODY):
                        empty(TILE_TURNS - 1, t, g)

            @block.sync
            def _(sp):
                for t in range(NT):
                    sp.wait_ge(evacuated, (t + 1) * GROUPS + RING)
                    for q in range(4):
                        n = N_KEYS // 4
                        sp.dma_start(gate_dram[q * n:(q + 1) * n, :, t * P:(t + 1) * P].rearrange("i j t -> j i t"),
                                     out[t % 2][:, q * n:(q + 1) * n, :]).then_inc(written[t % 2], 16)
                for sem in written:
                    sp.wait_ge(sem, 64 * NT // 2)


def evacuate(nc, c, act, out, i, t, g, multiplied, evacuated, groups, body, ring):
    act.wait_ge(multiplied, i * body + (t * groups + g + 1 + ring))
    nc.scalar.copy(out[:, :, bass.ds(i * (4 * body) + 4 * g, 4)],
                   c.psum[:, g % ring, :].rearrange("p (n i) -> p i n", n=4)).then_inc(evacuated, 1)


def experts(nc, c, l, x_hi, x_lo, ffn, peer_u, peer_v, gate_dram):
    GB = 2
    BODY = 2 * GB
    TURNS = N_KEYS // BODY
    with ExitStack() as ctx:
        def sb(name, shape, dt=F32):
            return ctx.enter_context(nc.sbuf_tensor(name, shape, dt))
        u = sb("ex_u", [P, BODY, D])
        v = sb("ex_v", [P, BODY, D])
        gate = sb("ex_gate", [P, BODY, S])
        ut_hi, ut_lo = (sb(f"ex_ut_{n}", [P, 2, D], F32R) for n in ("hi", "lo"))
        v_hi, v_lo = (sb(f"ex_v_{n}", [P, 2, GB, D], F32R) for n in ("hi", "lo"))
        a_hi, a_lo = (sb(f"ex_a_{n}", [P, 2, GB, S], F32R) for n in ("hi", "lo"))
        act_out = sb("ex_act", [P, 2, S])
        a_full = sb("ex_a", [P, 2, S])
        names = ([f"u_here{s}" for s in range(BODY)] + [f"v_here{s}" for s in range(BODY)]
                 + [f"gate_here{s}" for s in range(BODY)]
                 + ["u_turned", "u_high", "u_low", "hidden", "gelued", "gated", "a_high", "a_low", "v_high", "v_low",
                    "summed", "added", "zeroed", "x_high", "x_low"])
        with phase(nc, names) as (block, *sems):
            u_here, v_here, gate_here = sems[0:BODY], sems[BODY:2 * BODY], sems[2 * BODY:3 * BODY]
            (u_turned, u_high, u_low, hidden, gelued, gated, a_high, a_low, v_high, v_low,
             summed, added, zeroed, x_high, x_low) = sems[3 * BODY:]


            @block.sync
            def _(sp):
                def load(i, s, first):
                    at = bass.ds(i * (BODY * P) + s * P, P) if not first else slice(s * P, (s + 1) * P)
                    key = bass.ds(i * BODY + s, 1) if not first else slice(s, s + 1)
                    if not first:
                        sp.wait_ge(u_turned, i * (2 * BODY) + (2 * (s + 1) - 2 * BODY))
                    sp.dma_start(u[:, s, :], peer_u[bass.ds(l, 1), at].rearrange("o p d -> (o p) d")
                                 ).then_inc(u_here[s], 16)
                    if not first:
                        sp.wait_ge(gated, i * BODY + (s + 1 - BODY))
                        sp.wait_ge(a_low, i * BODY + (s + 1 - BODY))
                    sp.dma_start(gate[:, s, :], gate_dram[key].rearrange("o j t -> (o j) t")
                                 ).then_inc(gate_here[s], 16)
                    if not first:
                        sp.wait_ge(v_low, i * BODY + (s + 1 - BODY))
                    sp.dma_start(v[:, s, :], peer_v[bass.ds(l, 1), at].rearrange("o p d -> (o p) d")
                                 ).then_inc(v_here[s], 16)

                for s in range(BODY):
                    load(0, s, True)
                with sp.Fori(1, TURNS) as i:
                    for s in range(BODY):
                        load(i, s, False)

            @block.tensor
            def _(pe):
                def turn_u(i, s):
                    pe.wait_ge(u_here[s], i * 16 + 16)
                    for h in range(2):
                        if not (isinstance(i, int) and s == 0):
                            pe.wait_ge(u_low, i * (2 * BODY) + (2 * s + h - 1))
                        for k in range(4):
                            mm = nc.tensor.transpose(c.psum[:, h, k * P:(k + 1) * P],
                                                     u[:, s, (4 * h + k) * P:(4 * h + k + 1) * P], c.ident[:])
                        mm.then_inc(u_turned, 1)

                def hide(i, s):
                    pe.wait_ge(u_low, i * (2 * BODY) + (2 * s + 2))
                    if not (isinstance(i, int) and s < 2):
                        pe.wait_ge(gelued, i * BODY + (s - 1))
                    for k in range(ND):
                        at = slice(k * P, (k + 1) * P)
                        for n, (left, right) in enumerate(((ut_hi, x_hi), (ut_hi, x_lo), (ut_lo, x_hi))):
                            if isinstance(i, int) and s == 0 and n == 0:
                                pe.wait_ge(x_low, k + 1)
                            mm = nc.tensor.matmul(c.psum[:, 2 + s % 2, :], left[:, s % 2, at], right[:, k, :],
                                                  start=k + n == 0, stop=k == ND - 1 and n == 2)
                    mm.then_inc(hidden, 1)

                def add_up(i, par, part):
                    if part == 0:
                        pe.wait_ge(a_low, i * BODY + GB * (par + 1))
                        pe.wait_ge(v_low, i * BODY + GB * (par + 1))
                    for t in (2 * part, 2 * part + 1):
                        tok = slice(t * P, (t + 1) * P)
                        for h in range(2):
                            n = 2 * t + h
                            if not (isinstance(i, int) and par == 0 and n < 4):
                                pe.wait_ge(added, i * 16 + (8 * par + n - 3))
                            half = slice(h * HALF, (h + 1) * HALF)
                            for b in range(GB):
                                for m, (left, right) in enumerate(((a_hi, v_hi), (a_hi, v_lo), (a_lo, v_hi))):
                                    mm = nc.tensor.matmul(c.psum[:, 4 + n % 4, :], left[:, par, b, tok],
                                                          right[:, par, b, half], start=b + m == 0,
                                                          stop=b == GB - 1 and m == 2)
                            mm.then_inc(summed, 1)

                def turn(i, first):
                    for s, (di, par, part) in enumerate(((-1, 0, 1), (-1, 1, 0), (-1, 1, 1), (0, 0, 0))):
                        turn_u(i, s)
                        if not first or di == 0:
                            add_up(i + di, par, part)
                        hide(i, s)

                turn(0, True)
                with pe.Fori(1, TURNS) as i:
                    turn(i, False)
                add_up(TURNS - 1, 0, 1)
                add_up(TURNS - 1, 1, 0)
                add_up(TURNS - 1, 1, 1)

            def free_group(eng, i, s, first):
                if not first:
                    eng.wait_ge(summed, i * 16 + (8 * (s // GB) - 8))

            @block.scalar
            def _(act):
                def turn(i, first):
                    for s in range(BODY):
                        for h in range(2):
                            act.wait_ge(u_turned, i * (2 * BODY) + (2 * s + h + 1))
                            nc.scalar.copy(ut_hi[:, s % 2, h * HALF:(h + 1) * HALF],
                                           c.psum[:, h, :]).then_inc(u_high, 1)
                        act.wait_ge(v_here[s], i * 16 + 16)
                        free_group(act, i, s, first)
                        nc.scalar.copy(v_hi[:, s // GB, s % GB, :], v[:, s, :]).then_inc(v_high, 1)
                        act.wait_ge(hidden, i * BODY + (s + 1))
                        if not (first and s < 2):
                            act.wait_ge(gated, i * BODY + (s - 1))
                            act.wait_ge(a_high, i * BODY + (s - 1))
                        nc.scalar.activation(act_out[:, s % 2, :], c.psum[:, 2 + s % 2, :],
                                             ACT.Gelu).then_inc(gelued, 1)

                for k in range(ND):
                    nc.scalar.copy(x_hi[:, k, :], c.xt[:, k, :]).then_inc(x_high, 1)
                turn(0, True)
                with act.Fori(1, TURNS) as i:
                    turn(i, False)

            @block.gpsimd
            def _(pool):
                nc.gpsimd.memset(ffn[:], 0.0).then_inc(zeroed, 1)

                def turn(i, first):
                    for s in range(BODY):
                        pool.wait_ge(gate_here[s], i * 16 + 16)
                        pool.wait_ge(gelued, i * BODY + (s + 1))
                        if not (first and s < 2):
                            pool.wait_ge(a_low, i * BODY + (s - 1))
                        nc.gpsimd.tensor_tensor(a_full[:, s % 2, :], act_out[:, s % 2, :], gate[:, s, :],
                                                ALU.mult).then_inc(gated, 1)

                turn(0, True)
                with pool.Fori(1, TURNS) as i:
                    turn(i, False)

            @block.vector
            def _(dve):
                def add(i, first_sum):
                    for n in range(first_sum, first_sum + 4):
                        dve.wait_ge(summed, i * 16 + (n + 1))
                        at = ffn[:, (n % 8) // 2, (n % 2) * HALF:(n % 2 + 1) * HALF]
                        nc.vector.tensor_tensor(at, at, c.psum[:, 4 + n % 4, :], ALU.add).then_inc(added, 1)

                def turn(i, first):
                    for s in range(BODY):
                        for h in range(2):
                            dve.wait_ge(u_high, i * (2 * BODY) + (2 * s + h + 1))
                            at = slice(h * HALF, (h + 1) * HALF)
                            nc.vector.tensor_tensor(ut_lo[:, s % 2, at], c.psum[:, h, :],
                                                    ut_hi[:, s % 2, at].bitcast(F32), ALU.subtract).then_inc(u_low, 1)
                        if not first or s == 3:
                            add(i, 4 * s - 12)
                        dve.wait_ge(v_high, i * BODY + (s + 1))
                        nc.vector.tensor_tensor(v_lo[:, s // GB, s % GB, :], v[:, s, :],
                                                v_hi[:, s // GB, s % GB, :].bitcast(F32),
                                                ALU.subtract).then_inc(v_low, 1)
                        dve.wait_ge(gate_here[s], i * 16 + 16)
                        dve.wait_ge(gelued, i * BODY + (s + 1))
                        nc.vector.tensor_tensor(a_hi[:, s // GB, s % GB, :], act_out[:, s % 2, :], gate[:, s, :],
                                                ALU.mult).then_inc(a_high, 1)
                        dve.wait_ge(a_high, i * BODY + (s + 1))
                        dve.wait_ge(gated, i * BODY + (s + 1))
                        nc.vector.tensor_tensor(a_lo[:, s // GB, s % GB, :], a_full[:, s % 2, :],
                                                a_hi[:, s // GB, s % GB, :].bitcast(F32),
                                                ALU.subtract).then_inc(a_low, 1)

                for k in range(ND):
                    dve.wait_ge(x_high, k + 1)
                    nc.vector.tensor_tensor(x_lo[:, k, :], c.xt[:, k, :], x_hi[:, k, :].bitcast(F32),
                                            ALU.subtract).then_inc(x_low, 1)
                dve.wait_ge(zeroed, 1)
                turn(0, True)
                with dve.Fori(1, TURNS) as i:
                    turn(i, False)
                for first_sum in (4, 8, 12):
                    add(TURNS - 1, first_sum)


class Tiles:
    pass


def build(nc, x, w_in, g_cq, w_uq, g_ckv, w_ukv, w_o, ln1_g, ln1_b, peer_wq, peer_keys, peer_u, peer_v,
          ln2_g, ln2_b, rope_cos, rope_sin, out, gate_dram):
    with ExitStack() as whole:
        def tile(ctx, name, shape, dt=F32):
            return ctx.enter_context(nc.sbuf_tensor(name, shape, dt))

        c = Tiles()
        c.x = tile(whole, "x", [P, NT, D])
        c.xt = tile(whole, "xt", [P, ND, S])
        c.ident = tile(whole, "ident", [P, P])
        c.neg_ones = tile(whole, "neg_ones", [P, P])
        c.neg_tri = tile(whole, "neg_tri", [P, P])
        c.neg_ones_r = tile(whole, "neg_ones_r", [P, P], F32R)
        c.neg_tri_r = tile(whole, "neg_tri_r", [P, P], F32R)
        c.neg_mask = tile(whole, "neg_mask", [P, P])
        c.count_keys = tile(whole, "count_keys", [P, N_KEYS])
        c.count_rows = tile(whole, "count_rows", [P, TOPK, TOPK], BF16)
        c.ones = tile(whole, "ones", [P, 1])
        c.cos = tile(whole, "cos", [P, S])
        c.sin = tile(whole, "sin", [P, S])
        c.psum = whole.enter_context(nc.psum_tensor("banks", [P, 8, 512], F32))
        c.flat = c.psum[:].rearrange("p b n -> p (b n)")

        make_constants(nc, c, x, rope_cos, rope_sin)
        with nc.Fori(0, DEPTH) as l:
            with ExitStack() as ctx:
                m = Tiles()
                m.mixed_t = tile(ctx, "mixed_t", [P, ND, S])
                m.lat_t = tile(ctx, "lat_t", [P, 3, S])
                m.k_full = tile(ctx, "k_full", [P, 2, S])
                m.la_wq = tile(ctx, "la_wq", [P, 2, 2, QK])
                m.la_wq_swap = tile(ctx, "la_wq_swap", [P, 2, 2, ROPE])
                m.la_wk = tile(ctx, "la_wk", [P, 2, HD])
                m.la_wkv = tile(ctx, "la_wkv", [P, 2 * PAIRS, 2, HD])
                with ExitStack() as until_latent:
                    m.sb_w = tile(until_latent, "sb_w", [P, 3, ND, P])
                    m.x_hi, m.x_lo = (tile(until_latent, f"mix_x_{n}", [P, ND, S], F32R) for n in ("hi", "lo"))
                    latents(nc, c, m, l, w_in, g_cq, g_ckv)
                    stick_breaking(nc, c, m, l, w_in, w_uq, w_ukv)
                m.w_out = tile(ctx, "w_out", [P, ND, D])
                m.ln = Norm(nc, ctx, "ln1")
                latent_attention(nc, c, m, l, w_uq, w_ukv, w_o, ln1_g, ln1_b)
                project_out(nc, c, m)
            with ExitStack() as ctx:
                r = Tiles()
                r.top = tile(ctx, "top", [P, NT, P_HEADS, TOPK])
                r.index = tile(ctx, "index", [P, 2, NT, 1 + P_HEADS, TOPK])
                r.turned = tile(ctx, "picks_t", [P, 3, S])
                route(nc, c, r, l, peer_wq, peer_keys)
                gates(nc, c, r)
                spread_gates(nc, c, r, gate_dram)
            with ExitStack() as ctx:
                ffn = tile(ctx, "ffn", [P, NT, D])
                x_hi, x_lo = (tile(ctx, f"x_{n}", [P, ND, S], F32R) for n in ("hi", "lo"))
                experts(nc, c, l, x_hi, x_lo, ffn, peer_u, peer_v, gate_dram)
                residual_norm(nc, c, l, ffn, ln2_g, ln2_b)
        store_x(nc, c, out)


_INS = ["x", "w_in", "g_cq", "w_uq", "g_ckv", "w_ukv", "w_o", "ln1_g", "ln1_b", "peer_wq", "peer_keys",
        "peer_u", "peer_v", "ln2_g", "ln2_b"]


def rope_tables():
    inv = (np.float32(10000.0) ** (-np.arange(0, ROPE, 2, dtype=np.float32) / np.float32(ROPE))).astype(np.float32)
    angle = inv[:, None] * np.arange(S, dtype=np.float32)[None, :]
    cos, sin = np.cos(angle, dtype=np.float32), np.sin(angle, dtype=np.float32)
    return np.concatenate([cos, cos]), np.concatenate([-sin, sin])


def kernel(**inputs):
    import concourse.bacc as bacc
    from concourse.bass_utils import run_bass_kernel_spmd

    nc = bacc.Bacc("TRN2", target_bir_lowering=False, num_devices=1)
    arrays, args = {}, []
    for name in _INS:
        arrays[f"in_{name}_dram"] = np.ascontiguousarray(inputs[name])
    arrays["rope_cos_dram"], arrays["rope_sin_dram"] = rope_tables()
    for name, a in arrays.items():
        args.append(nc.dram_tensor(name, a.shape, mybir.dt.from_np(a.dtype), kind="ExternalInput").ap())
    args.append(nc.dram_tensor("out_0_dram", (1, S, D), F32, kind="ExternalOutput").ap())
    args.append(nc.dram_tensor("gates_dram", (N_KEYS, N_KEYS, S), F32).ap())
    build(nc, *args)
    return run_bass_kernel_spmd(nc, [arrays], core_ids=[0]).results[0]["out_0_dram"]
```

```python
from contextlib import ExitStack, contextmanager

import numpy as np

import concourse.bass as bass
from concourse import mybir

F32 = mybir.dt.float32
BF16 = mybir.dt.bfloat16
F32R = mybir.dt.float32r
U32 = mybir.dt.uint32
ALU = mybir.AluOpType
ACT = mybir.ActivationFunctionType
AX_X = mybir.AxisListType.X

P = 128
DEPTH = 2
S = 512
D = 1024
NT = S // P
ND = D // P
HALF = D // 2
HD = 64
PAIRS = 4
D_SB = 512
Q_RANK = 256
KV_RANK = 128
ROPE = 32
QK = HD + ROPE
LATENT0 = 3 * D_SB
LATENT = Q_RANK + KV_RANK
N_KEYS = 128
P_HEADS = 8
TOPK = 16
HALF_TILE = P // 2
HALF_TILES = S // HALF_TILE
EXPERT_SLOTS = 4
ALPHA = (2.0 * DEPTH) ** 0.25
LN_EPS = 1e-5
RMS_EPS = 1e-6
NEG = -3.0e38

PACK = {4: 0, 3: 512, 1: 896, 2: 1024}
PACKED = 1280
SB_AT = {s: PACK[NT - s] for s in range(NT)}
LA_AT = {t: PACK[t + 1] for t in range(NT)}


class Chain:

    def __init__(self, eng, sem, credit=0, passed=None):
        self.passed = passed
        self.eng, self.sem, self.credit, self.base, self.n = eng, sem, credit, credit, 0

    def link(self, instruction):
        instruction.then_inc(self.sem, 1)
        self.n += 1
        self.eng.wait_ge(self.sem, self.base + self.n)

    def mark(self, instruction):
        instruction.then_inc(self.sem, 1)
        self.n += 1
        return self.base + self.n

    def after(self, mark, plain=False):
        self.eng.wait_ge(self.sem, mark)
        if plain:
            self.eng.sem_inc(self.passed, 1)

    def turn(self, i, per):
        self.base, self.n, self.per = i * per + self.credit, 0, per

    def turned(self, count):
        assert self.n == self.per, (self.n, self.per)
        self.base, self.n = count * self.per + self.credit, 0


@contextmanager
def phase(nc, names):
    with ExitStack() as ctx:
        sems = [ctx.enter_context(nc.semaphore(n)) for n in names]
        with nc.Block(no_gpsimd_drain=True) as block:
            yield (block, *sems)
        nums = sorted(s.num for s in sems)
        assert nums == list(range(nums[0], nums[0] + len(nums)))
        nc.all_engine_barrier(sems_to_clear=range(nums[0], nums[-1] + 1))


CREDIT = 1


def give_credit(block, sems):
    @block.gpsimd
    def _(pool):
        for sem in sems:
            pool.sem_inc(sem, CREDIT)


def cols(ap, start, n):
    return ap[:, start:start + n]


def make_constants(nc, c, x, rope_cos, rope_sin):
    with phase(nc, ["filled", "selected", "tables_in"]) as (block, filled, selected, tables_in):
        @block.vector
        def _(dve):
            dve.wait_ge(selected, 1)
            nc.vector.tensor_copy(c.neg_tri_r[:], c.neg_tri[:])
            nc.vector.tensor_copy(c.neg_ones_r[:], c.neg_ones[:])

        @block.gpsimd
        def _(pool):
            nc.gpsimd.memset(c.ident[:], 0.0).then_inc(filled, 1)
            nc.gpsimd.memset(c.neg_ones[:], -1.0).then_inc(filled, 1)
            nc.gpsimd.memset(c.neg_mask[:], 0.0).then_inc(filled, 1)
            nc.gpsimd.iota(c.count_keys[:], [[1, N_KEYS]], base=0, channel_multiplier=0,
                           allow_small_or_imprecise_dtypes=True)
            nc.gpsimd.iota(c.count_rows[:], [[1, TOPK], [0, TOPK]], base=0, channel_multiplier=0,
                           allow_small_or_imprecise_dtypes=True)
            nc.gpsimd.memset(c.ones[:], 1.0)
            pool.wait_ge(filled, 3)
            nc.gpsimd.affine_select(out=c.ident[:], in_=c.ident[:], compare_op=ALU.not_equal, fill=1.0,
                                    base=0, pattern=[[-1, P]], channel_multiplier=1)
            nc.gpsimd.affine_select(out=c.neg_tri[:], in_=c.neg_ones[:], compare_op=ALU.is_ge, fill=0.0,
                                    base=0, pattern=[[-1, P]], channel_multiplier=1)
            nc.gpsimd.affine_select(out=c.neg_mask[:], in_=c.neg_mask[:], compare_op=ALU.is_ge, fill=NEG,
                                    base=0, pattern=[[-1, P]], channel_multiplier=1).then_inc(selected, 1)

        @block.sync
        def _(sp):
            sp.dma_start(c.x[:], x[0].rearrange("(t p) d -> p t d", p=P)).then_inc(tables_in, 16)
            sp.dma_start(c.cos[HD:QK, :], rope_cos).then_inc(tables_in, 16)
            sp.dma_start(c.sin[HD:QK, :], rope_sin).then_inc(tables_in, 16)
            sp.wait_ge(tables_in, 48)


def store_x(nc, c, out):
    with phase(nc, ["x_out"]) as (block, x_out):
        @block.sync
        def _(sp):
            sp.dma_start(out[0].rearrange("(t p) d -> p t d", p=P), c.x[:]).then_inc(x_out, 16)
            sp.wait_ge(x_out, 16)


def split(nc, ch, full, high, low):
    ch.link(nc.vector.tensor_copy(high, full))
    return nc.vector.tensor_tensor(low, full, high.bitcast(F32), ALU.subtract)


PARTS = ((0, 0), (0, 1), (1, 0))


def turn_x(nc, c, pe, x_turned, x_copied):
    for k in range(ND):
        if k >= 4:
            pe.wait_ge(x_copied, k - 3)
        for t in range(NT):
            mm = nc.tensor.transpose(c.psum[:, k % 4, t * P:(t + 1) * P], c.x[:, t, k * P:(k + 1) * P], c.ident[:])
        mm.then_inc(x_turned, 1)
    pe.wait_ge(x_copied, ND)


def take_x(nc, c, act, x_turned, x_copied):
    for k in range(ND):
        act.wait_ge(x_turned, k + 1)
        nc.scalar.copy(c.xt[:, k, :], c.psum[:, k % 4, :]).then_inc(x_copied, 1)


def latents(nc, c, m, l, w_in, g_cq, g_ckv):
    with ExitStack() as ctx:
        w = ctx.enter_context(nc.sbuf_tensor("w_lat", [P, ND, LATENT + ROPE], F32))
        w_swap = ctx.enter_context(nc.sbuf_tensor("w_lat_swap", [P, ND, ROPE], F32))
        g = ctx.enter_context(nc.sbuf_tensor("g_lat", [P, 3], F32))
        squares = ctx.enter_context(nc.sbuf_tensor("lat_squares", [P, NT, Q_RANK], F32))
        stat = ctx.enter_context(nc.sbuf_tensor("lat_stat", [P, 2, 2 * NT], F32))
        normed = ctx.enter_context(nc.sbuf_tensor("lat_normed", [P, NT, LATENT], F32))
        rot = ctx.enter_context(nc.sbuf_tensor("lat_rot", [P, 2, S], F32))
        names = ["w_here", "g_here", "first_pair_here", "x_turned", "x_copied", "projected", "roped", "squared",
                 "rooted", "dve_chain", "norm_done", "turned"]
        with phase(nc, names) as (block, loaded, g_here, first_pair_here, x_turned, x_copied, projected, roped,
                                  squared, rooted, chain, norm_done, turned):
            wl = w_in[bass.ds(l, 1)].rearrange("o (c p) n -> p (o c) n", p=P)
            rope0 = LATENT0 + LATENT

            @block.sync
            def _(sp):
                sp.dma_start(w[:], wl[:, :, LATENT0:]).then_inc(loaded, 16)
                sp.dma_start(w_swap[:, :, 0:ROPE // 2], wl[:, :, rope0 + ROPE // 2:]).then_inc(loaded, 16)
                sp.dma_start(w_swap[:, :, ROPE // 2:], wl[:, :, rope0:rope0 + ROPE // 2]).then_inc(loaded, 16)
                sp.dma_start(g[:, 0:2], g_cq[bass.ds(l, 1)].rearrange("o (c p) -> p (o c)", p=P),
                             allow_slow_non_contiguous=True).then_inc(g_here, 16)
                sp.dma_start(g[:, 2:3], g_ckv[bass.ds(l, 1)].rearrange("o (c p) -> p (o c)", p=P),
                             allow_slow_non_contiguous=True).then_inc(g_here, 16)

                for n in range(3):
                    load_sb_weights(sp, m, l, w_in, 0, n, first_pair_here)
                sp.wait_ge(first_pair_here, 48)

            @block.tensor
            def _(pe):
                turn_x(nc, c, pe, x_turned, x_copied)
                pe.wait_ge(loaded, 48)
                for t in range(NT):
                    for k in range(ND):
                        mm = nc.tensor.matmul(c.psum[:, t, 0:LATENT], c.xt[:, k, t * P:(t + 1) * P],
                                              w[:, k, 0:LATENT], start=k == 0, stop=k == ND - 1)
                    mm.then_inc(projected, 1)
                for bank, wr in ((4, w[:, :, LATENT:]), (5, w_swap[:])):
                    for k in range(ND):
                        mm = nc.tensor.matmul(c.psum[HD:QK, bank, :], wr[:, k, :], c.xt[:, k, :],
                                              start=k == 0, stop=k == ND - 1)
                    mm.then_inc(roped, 1)
                pe.wait_ge(norm_done, NT)
                for k in range(3):
                    for t in range(NT):
                        mm = nc.tensor.transpose(c.psum[:, k, t * P:(t + 1) * P],
                                                 normed[:, t, k * P:(k + 1) * P], c.ident[:])
                    mm.then_inc(turned, 1)

            @block.scalar
            def _(act):
                take_x(nc, c, act, x_turned, x_copied)
                for t in range(NT):
                    act.wait_ge(projected, t + 1)
                    nc.scalar.activation(squares[:, t, :], c.psum[:, t, 0:Q_RANK], ACT.Square,
                                         accum_out=stat[:, 0, t:t + 1]).then_inc(squared, 1)
                    act.wait_ge(squared, 2 * t + 1)
                    nc.scalar.activation(squares[:, t, 0:KV_RANK], c.psum[:, t, Q_RANK:LATENT], ACT.Square,
                                         accum_out=stat[:, 0, NT + t:NT + t + 1]).then_inc(squared, 1)
                act.wait_ge(chain, ND + 2)
                nc.scalar.activation(stat[:, 0, :], stat[:, 1, :], ACT.Sqrt).then_inc(rooted, 1)

            @block.vector
            def _(dve):
                ch = Chain(dve, chain)
                for k in range(ND):
                    dve.wait_ge(x_copied, k + 1)
                    split(nc, ch, c.xt[:, k, :], m.x_hi[:, k, :], m.x_lo[:, k, :])
                dve.wait_ge(squared, 2 * NT)
                ch.link(nc.vector.tensor_scalar(stat[:, 1, 0:NT], stat[:, 0, 0:NT], 1.0 / Q_RANK, RMS_EPS,
                                                ALU.mult, ALU.add))
                ch.link(nc.vector.tensor_scalar(stat[:, 1, NT:], stat[:, 0, NT:], 1.0 / KV_RANK, RMS_EPS,
                                                ALU.mult, ALU.add))
                dve.wait_ge(rooted, 1)
                ch.link(nc.vector.reciprocal(stat[:, 1, :], stat[:, 0, :]))
                for t in range(NT):
                    nc.vector.tensor_scalar(normed[:, t, 0:Q_RANK], c.psum[:, t, 0:Q_RANK],
                                            stat[:, 1, t:t + 1], None, ALU.mult)
                    nc.vector.tensor_scalar(normed[:, t, Q_RANK:], c.psum[:, t, Q_RANK:LATENT],
                                            stat[:, 1, NT + t:NT + t + 1], None, ALU.mult).then_inc(norm_done, 1)
                dve.wait_ge(roped, 2)
                nc.vector.tensor_tensor(rot[HD:QK, 0, :], c.psum[HD:QK, 4, :], c.cos[HD:QK, :], ALU.mult)
                ch.link(nc.vector.tensor_tensor(rot[HD:QK, 1, :], c.psum[HD:QK, 5, :], c.sin[HD:QK, :], ALU.mult))
                for e in range(2):
                    nc.vector.tensor_tensor(m.k_full[HD:QK, e, :], rot[HD:QK, 0, :], rot[HD:QK, 1, :], ALU.add)
                dve.wait_ge(g_here, 32)
                for k in range(3):
                    dve.wait_ge(turned, k + 1)
                    ins = nc.vector.tensor_scalar(m.lat_t[:, k, :], c.psum[:, k, :], g[:, k:k + 1], None, ALU.mult)
                ch.link(ins)


def load_sb_weights(sp, m, l, w_in, p, n, here):
    sp.dma_start(m.sb_w[:, n], w_in[bass.ds(l, 1), :, bass.ds(p * P + n * D_SB, P)]
                 .rearrange("o (c p) n -> p (o c) n", p=P)).then_inc(here, 16)


def stick_breaking(nc, c, m, l, w_in, w_uq, w_ukv):
    with ExitStack() as ctx:
        def sb(name, shape, dt=F32):
            return ctx.enter_context(nc.sbuf_tensor(name, shape, dt))
        w = m.sb_w
        w_parts = [sb(f"sb_w_{n}", [P, 2, ND, P], F32R) for n in ("hi", "lo")]
        q, k_ = sb("sb_q", [P, S]), sb("sb_k", [P, S])
        v = sb("sb_v", [P, NT, P])
        soft = sb("sb_soft", [P, 2, PACKED])
        soft_parts = [sb(f"sb_soft_{n}", [P, 2, PACKED], F32R) for n in ("hi", "lo")]
        wts = sb("sb_wts", [P, 2, PACKED])
        x_parts = (m.x_hi, m.x_lo)
        names = ["w_here_q", "w_here_k", "w_here_v", "w_split_q", "w_split_k", "made_q", "made_k", "made_v",
                 "q_out", "k_out", "v_out", "scored", "sized", "exped", "logged", "soft_done", "masked", "soft_split",
                 "summed", "weighed", "ready", "mixed", "stored", "dve_chain", "passed", "later_here",
                 "v_weights"]
        with phase(nc, names) as (block, w_here_q, w_here_k, w_here_v, w_split_q, w_split_k, made_q, made_k, made_v,
                                  q_out, k_out, v_out, scored, sized, exped, logged, soft_done, masked, soft_split,
                                  summed, weighed, ready, mixed, stored, chain, passed, later_here,
                                  v_weights):
            z = [c.flat[:, 1536 * e:1536 * e + PACKED] for e in range(2)]
            w_here, w_split, made = (w_here_q, w_here_k, w_here_v), (w_split_q, w_split_k), (made_q, made_k)

            @block.sync
            def _(sp):
                load_la_pair(sp, m, l, w_uq, w_ukv, 0, later_here)
                sp.dma_start(m.la_wkv[:].rearrange("p e h n -> p (e h n)"),
                             w_ukv[bass.ds(l, 1)].rearrange("o p n -> p (o n)")).then_inc(later_here, 16)
                with sp.Fori(1, PAIRS) as p:
                    for n in range(2):
                        sp.wait_ge(w_split[n], p)
                        load_sb_weights(sp, m, l, w_in, p, n, w_here[n])
                    sp.wait_ge(made_v, p)
                    load_sb_weights(sp, m, l, w_in, p, 2, w_here_v)
                    sp.wait_ge(w_here_v, p * 16)
                    sp.sem_inc(v_weights, 1)
                sp.wait_ge(later_here, 112 + 16)

            @block.tensor
            def _(pe):
                def project(p, n):
                    pe.wait_ge(w_split[n], p + 1)
                    for k in range(ND):
                        for m_, (i, j) in enumerate(PARTS):
                            mm = nc.tensor.matmul(c.psum[:, 6 + n, :], w_parts[i][:, n, k, :], x_parts[j][:, k, :],
                                                  start=k + m_ == 0, stop=k == ND - 1 and m_ == 2)
                    mm.then_inc(made[n], 1)

                def turn(p, last):
                    pe.wait_ge(q_out, p + 1)
                    pe.wait_ge(k_out, p + 1)
                    for e in range(2):
                        for s in (0, 1, 3, 2):
                            mm = nc.tensor.matmul(cols(z[e], SB_AT[s], S - s * P),
                                                  k_[HD * e:HD * (e + 1), s * P:(s + 1) * P],
                                                  q[HD * e:HD * (e + 1), s * P:], start=s != 3, stop=False,
                                                  skip_group_check=True)
                        mm.then_inc(scored, 1)
                    pe.wait_ge(v_weights, p + CREDIT)
                    for t in range(NT):
                        for k in range(ND):
                            mm = nc.tensor.matmul(c.psum[:, 6, t * P:(t + 1) * P],
                                                  c.xt[:, k, t * P:(t + 1) * P], w[:, 2, k, :],
                                                  start=k == 0, stop=k == ND - 1)
                    mm.then_inc(made_v, 1)
                    if not last:
                        pe.wait_ge(v_out, p + 1)
                        project(p + 1, 0)
                    for e in range(2):
                        pe.wait_ge(soft_split, p * 2 + e + 1)
                        for j in range(NT):
                            for s in range(j + 1):
                                out = cols(z[e], SB_AT[s] + (j - s) * P, S - j * P)
                                for i in range(2):
                                    mm = nc.tensor.matmul(out, (c.neg_tri_r if s == j else c.neg_ones_r)[:],
                                                          cols(soft_parts[i][:, e], SB_AT[j], S - j * P),
                                                          start=False, stop=s == j and i == 1,
                                                          skip_group_check=True)
                        mm.then_inc(summed, 1)
                    pe.wait_ge(stored, p + CREDIT)
                    if not last:
                        project(p + 1, 1)
                        pe.wait_ge(k_out, p + 2)
                    pe.wait_ge(v_out, p + 1)
                    for e in range(2):
                        pe.wait_ge(ready, p * 2 + e + 1)
                        for s in range(NT):
                            mm = nc.tensor.matmul(c.psum[HD * e:HD * (e + 1), 7, s * P:],
                                                  v[:, s, HD * e:HD * (e + 1)],
                                                  cols(wts[:, e], SB_AT[s], S - s * P),
                                                  start=s == 0, stop=s == NT - 1, skip_group_check=True)
                    mm.then_inc(mixed, 1)

                project(0, 0)
                project(0, 1)
                with pe.Fori(0, PAIRS - 1) as p:
                    turn(p, False)
                turn(PAIRS - 1, True)

            @block.scalar
            def _(act):
                def take_q(p):
                    act.wait_ge(made_q, p + 1)
                    nc.scalar.mul(q[:], c.psum[:, 6, :], HD ** -0.5).then_inc(q_out, 1)

                def take_k(p):
                    act.wait_ge(made_k, p + 1)
                    nc.scalar.copy(k_[:], c.psum[:, 7, :]).then_inc(k_out, 1)

                def turn(p, last):
                    for e in range(2):
                        act.wait_ge(scored, p * 2 + e + 1)
                        nc.scalar.activation(soft[:, e], z[e], ACT.Abs).then_inc(sized, 1)
                        act.wait_ge(sized, p * 2 + e + 1)
                        nc.scalar.activation(soft[:, e], soft[:, e], ACT.Exp, scale=-1.0).then_inc(exped, 1)
                    for e in range(2):
                        act.wait_ge(exped, p * 2 + e + 1)
                        nc.scalar.activation(soft[:, e], soft[:, e], ACT.Ln, bias=c.ones[:, 0:1]).then_inc(logged, 1)
                    act.wait_ge(made_v, p + 1)
                    nc.scalar.copy(v[:].rearrange("p t n -> p (t n)"), c.psum[:, 6, :]).then_inc(v_out, 1)
                    if not last:
                        take_q(p + 1)
                    for e in range(2):
                        act.wait_ge(summed, p * 2 + e + 1)
                        nc.scalar.activation(wts[:, e], z[e], ACT.Exp).then_inc(weighed, 1)
                    if not last:
                        take_k(p + 1)
                    act.wait_ge(mixed, p + 1)
                    nc.scalar.copy(m.mixed_t[:, bass.ds(p, 1), :].rearrange("p o t -> p (o t)"),
                                   c.psum[:, 7, :]).then_inc(stored, 1)

                take_q(0)
                take_k(0)
                with act.Fori(0, PAIRS - 1) as p:
                    turn(p, False)
                turn(PAIRS - 1, True)

            @block.vector
            def _(dve):
                ch = Chain(dve, chain)

                def split_w(p, n, first=False):
                    if not first:
                        dve.wait_ge(w_here[n], p * 16)
                        dve.wait_ge(made[n], p)
                    split(nc, ch, w[:, n], w_parts[0][:, n], w_parts[1][:, n]).then_inc(w_split[n], 1)

                def soften(p, e):
                    dve.wait_ge(logged, p * 2 + e + 1)
                    nc.vector.scalar_tensor_tensor(out=soft[:, e], in0=z[e], scalar=0.0, in1=soft[:, e],
                                                   op0=ALU.max, op1=ALU.add).then_inc(soft_done, 1)

                def split_soft(p, e):
                    dve.wait_ge(masked, p * 2 + e + 1)
                    split(nc, ch, soft[:, e], soft_parts[0][:, e], soft_parts[1][:, e]).then_inc(soft_split, 1)

                def turn(p, last):
                    if not last:
                        split_w(p + 1, 0)
                    soften(p, 0)
                    if not last:
                        split_w(p + 1, 1)
                    split_soft(p, 0)
                    soften(p, 1)
                    split_soft(p, 1)

                split_w(0, 0, True)
                split_w(0, 1, True)
                ch.credit = ch.n
                with dve.Fori(0, PAIRS - 1) as p:
                    ch.turn(p, 4)
                    turn(p, False)
                ch.turned(PAIRS - 1)
                turn(PAIRS - 1, True)

            @block.gpsimd
            def _(pool):
                pool.sem_inc(stored, CREDIT)
                pool.sem_inc(v_weights, CREDIT)
                with pool.Fori(0, PAIRS) as p:
                    for sem, done, tile in ((soft_done, masked, soft), (weighed, ready, wts)):
                        for e in range(2):
                            pool.wait_ge(sem, p * 2 + e + 1)
                            pool.sem_inc(passed, 1)
                            for s in range(NT):
                                diag = cols(tile[:, e], SB_AT[s], P)
                                ins = nc.gpsimd.affine_select(out=diag, in_=diag, compare_op=ALU.is_gt, fill=0.0,
                                                              base=0, pattern=[[1, P]], channel_multiplier=-1)
                            ins.then_inc(done, 1)


def load_la_pair(sp, m, l, w_uq, w_ukv, p, here):
    uq = w_uq[bass.ds(l, 1), :, bass.ds(p * 2 * QK, 2 * QK)].rearrange("o (c p) (e n) -> p (o c) e n", p=P, e=2)
    for k in range(2):
        sp.dma_start(m.la_wq[:, k], uq[:, k]).then_inc(here, 16)
        sp.dma_start(m.la_wq_swap[:, k, :, 0:ROPE // 2], uq[:, k, :, HD + ROPE // 2:]).then_inc(here, 16)
        sp.dma_start(m.la_wq_swap[:, k, :, ROPE // 2:], uq[:, k, :, HD:HD + ROPE // 2]).then_inc(here, 16)
    sp.dma_start(m.la_wk[:], w_ukv[bass.ds(l, 1), :, bass.ds(p * 4 * HD, 4 * HD)].rearrange(
        "o p (e h n) -> p (o e) h n", e=2, h=2)[:, :, 0, :]).then_inc(here, 16)


def latent_attention(nc, c, m, l, w_uq, w_ukv, w_o, ln_g, ln_b):
    with ExitStack() as ctx:
        def sb(name, shape):
            return ctx.enter_context(nc.sbuf_tensor(name, shape, F32))
        wq, wq_swap, wk, wkv = m.la_wq, m.la_wq_swap, m.la_wk, m.la_wkv
        q = sb("la_q", [P, 2, S])
        rot = sb("la_rot", [P, 2, 2, S])
        v = sb("la_v", [P, NT, P])
        probs = sb("la_probs", [P, 2, PACKED])
        probs_t = sb("la_probs_t", [P, 2, PACKED])
        peak = sb("la_peak", [P, 2, NT])
        bias = sb("la_bias", [P, 2, NT])
        total = sb("la_total", [P, 2, NT])
        share = sb("la_share", [P, 2, NT])
        scale = QK ** -0.5
        names = ["w_here", "q_made", "k_made", "v_made", "q_out", "k_out", "v_out", "scored", "biased",
                 "exped", "scaled", "turned", "turned_out", "mixed", "stored", "dve_chain",
                 "later_here"]
        with phase(nc, names) as (block, w_here, q_made, k_made, v_made, q_out, k_out, v_out, scored,
                                  biased, exped, scaled, turned, turned_out, mixed, stored, chain,
                                  later_here):
            sc = [c.flat[:, 1536 * e:1536 * e + PACKED] for e in range(2)]
            give_credit(block, (stored, turned_out))

            @block.sync
            def _(sp):
                def load_next(p):
                    sp.wait_ge(k_made, p * 2)
                    load_la_pair(sp, m, l, w_uq, w_ukv, p, w_here)

                load_next(1)
                for k in range(0, ND, 2):
                    sp.dma_start(m.w_out[:, k:k + 2], w_o[bass.ds(l, 1), k * P:(k + 2) * P]
                                 .rearrange("o (c p) n -> p (o c) n", p=P)).then_inc(later_here, 16)
                sp.dma_start(m.ln.g[:], ln_g[bass.ds(l, 1)].broadcast_to([P, D])).then_inc(later_here, 16)
                sp.dma_start(m.ln.b[:], ln_b[bass.ds(l, 1)].broadcast_to([P, D])).then_inc(later_here, 16)
                with sp.Fori(2, PAIRS) as p:
                    load_next(p)
                sp.wait_ge(later_here, 16 * (ND // 2 + 2))

            @block.tensor
            def _(pe):
                def make_qk(p, first):
                    if not first:
                        pe.wait_ge(w_here, p * 112)
                        pe.wait_ge(v_out, p)
                        pe.wait_ge(stored, p - 1 + CREDIT)
                    for e in range(2):
                        if e == 1:
                            pe.wait_ge(q_out, p * 4 + 2)
                            pe.wait_ge(k_out, p * 2 + 1)
                        for k in range(2):
                            nc.tensor.matmul(c.psum[0:QK, 6, :], wq[:, k, e, :], m.lat_t[:, k, :],
                                             start=k == 0, stop=k == 1)
                        for k in range(2):
                            mm = nc.tensor.matmul(c.psum[HD:QK, 7, :], wq_swap[:, k, e, :], m.lat_t[:, k, :],
                                                  start=k == 0, stop=k == 1)
                        mm.then_inc(q_made, 1)
                        mm = nc.tensor.matmul(c.psum[0:HD, 7, :], wk[:, e, :], m.lat_t[:, 2, :],
                                              start=True, stop=True)
                        mm.then_inc(k_made, 1)

                def turn(p, last):
                    pe.wait_ge(turned_out, p * 2 + CREDIT)
                    pe.wait_ge(q_out, p * 4 + 4)
                    pe.wait_ge(k_out, p * 2 + 2)
                    for e in range(2):
                        for t in (3, 2, 0, 1):
                            mm = nc.tensor.matmul(cols(sc[e], LA_AT[t], (t + 1) * P),
                                                  q[0:QK, e, t * P:(t + 1) * P], m.k_full[0:QK, e, 0:(t + 1) * P],
                                                  start=True, stop=True)
                        mm.then_inc(scored, 1)
                    for t in range(NT):
                        mm = nc.tensor.matmul(c.psum[:, 6, t * P:(t + 1) * P], m.lat_t[:, 2, t * P:(t + 1) * P],
                                              wkv[:, bass.ds(p * 2, 2), 1, :], start=True, stop=True)
                    mm.then_inc(v_made, 1)
                    if not last:
                        make_qk(p + 1, False)
                    for e in range(2):
                        pe.wait_ge(scaled, p * 2 + e + 1)
                        for s in range(NT):
                            for t in range(s, NT):
                                mm = nc.tensor.transpose(cols(sc[e], SB_AT[s] + (t - s) * P, P),
                                                         cols(probs[:, e], LA_AT[t] + s * P, P), c.ident[:])
                        mm.then_inc(turned, 1)
                    pe.wait_ge(v_out, p + 1)
                    if not last:
                        pe.wait_ge(q_out, p * 4 + 8)
                        pe.wait_ge(k_out, p * 2 + 4)
                    for e in range(2):
                        pe.wait_ge(turned_out, p * 2 + e + 1 + CREDIT)
                        for s in range(NT):
                            mm = nc.tensor.matmul(c.psum[HD * e:HD * (e + 1), 7, s * P:],
                                                  v[:, s, HD * e:HD * (e + 1)],
                                                  cols(probs_t[:, e], SB_AT[s], S - s * P),
                                                  start=s == 0, stop=s == NT - 1, skip_group_check=True)
                    mm.then_inc(mixed, 1)

                make_qk(0, True)
                with pe.Fori(0, PAIRS - 1) as p:
                    turn(p, False)
                turn(PAIRS - 1, True)

            @block.scalar
            def _(act):
                def take_qk(p, e):
                    act.wait_ge(q_made, p * 2 + (e + 1))
                    nc.scalar.copy(q[0:HD, e, :], c.psum[0:HD, 6, :]).then_inc(q_out, 1)
                    act.wait_ge(k_made, p * 2 + (e + 1))
                    nc.scalar.copy(m.k_full[0:HD, e, :], c.psum[0:HD, 7, :]).then_inc(k_out, 1)

                def turn(p, last):
                    act.wait_ge(v_made, p + 1)
                    nc.scalar.copy(v[:].rearrange("p t n -> p (t n)"), c.psum[:, 6, :]).then_inc(v_out, 1)
                    for e in range(2):
                        act.wait_ge(biased, p * 2 + e + 1)
                        for t in range(NT):
                            at = cols(probs[:, e], LA_AT[t], (t + 1) * P)
                            ins = nc.scalar.activation(at, cols(sc[e], LA_AT[t], (t + 1) * P), ACT.Exp,
                                                       bias=bias[:, e, t:t + 1], scale=scale,
                                                       accum_out=total[:, e, t:t + 1])
                        ins.then_inc(exped, 1)
                        if not last:
                            take_qk(p + 1, e)
                    for e in range(2):
                        act.wait_ge(turned, p * 2 + e + 1)
                        nc.scalar.copy(probs_t[:, e], sc[e]).then_inc(turned_out, 1)
                    act.wait_ge(mixed, p + 1)
                    nc.scalar.copy(m.mixed_t[:, bass.ds(p + PAIRS, 1), :].rearrange("p o t -> p (o t)"),
                                   c.psum[:, 7, :]).then_inc(stored, 1)

                take_qk(0, 0)
                take_qk(0, 1)
                with act.Fori(0, PAIRS - 1) as p:
                    turn(p, False)
                turn(PAIRS - 1, True)

            @block.vector
            def _(dve):
                ch = Chain(dve, chain)

                def rotate(p, e):
                    dve.wait_ge(q_made, p * 2 + (e + 1))
                    nc.vector.tensor_tensor(rot[HD:QK, e, 0, :], c.psum[HD:QK, 6, :], c.cos[HD:QK, :], ALU.mult)
                    ch.link(nc.vector.tensor_tensor(rot[HD:QK, e, 1, :], c.psum[HD:QK, 7, :], c.sin[HD:QK, :],
                                                    ALU.mult))
                    nc.vector.tensor_tensor(q[HD:QK, e, :], rot[HD:QK, e, 0, :], rot[HD:QK, e, 1, :],
                                            ALU.add).then_inc(q_out, 1)

                def divide(p, e):
                    dve.wait_ge(exped, p * 2 + e + 1)
                    ch.link(nc.vector.reciprocal(share[:, e, :], total[:, e, :]))
                    for t in range(NT):
                        at = cols(probs[:, e], LA_AT[t], (t + 1) * P)
                        ins = nc.vector.tensor_scalar(at, at, share[:, e, t:t + 1], None, ALU.mult)
                    ins.then_inc(scaled, 1)

                def turn(p, last):
                    for e in range(2):
                        dve.wait_ge(scored, p * 2 + e + 1)
                        for t in range(NT):
                            diag = cols(sc[e], LA_AT[t] + t * P, P)
                            ins = nc.vector.tensor_tensor(diag, diag, c.neg_mask[:], ALU.add)
                        ch.link(ins)
                        for t in range(NT):
                            ins = nc.vector.reduce_max(peak[:, e, t:t + 1], cols(sc[e], LA_AT[t], (t + 1) * P), AX_X)
                        ch.link(ins)
                        nc.vector.tensor_scalar(bias[:, e, :], peak[:, e, :], -scale, None,
                                                ALU.mult).then_inc(biased, 1)
                    if not last:
                        rotate(p + 1, 0)
                    divide(p, 0)
                    divide(p, 1)
                    if not last:
                        rotate(p + 1, 1)

                rotate(0, 0)
                rotate(0, 1)
                ch.credit = ch.n
                with dve.Fori(0, PAIRS - 1) as p:
                    ch.turn(p, 8)
                    turn(p, False)
                ch.turned(PAIRS - 1)
                turn(PAIRS - 1, True)


def layer_norm_steps(nc, dve, ch, c, ln, t):
    for h in range(2):
        ins = nc.vector.bn_stats(ln.stats[:, t, h, :], c.x[:, t, h * HALF:(h + 1) * HALF])
    ch.link(ins)
    ch.link(nc.vector.bn_aggr(ln.mv[:, t, :], ln.stats[:, t].rearrange("p h s -> p (h s)")))
    nc.vector.tensor_scalar(ln.var[:, t:t + 1], ln.mv[:, t, 1:2], LN_EPS, None, ALU.add).then_inc(ln.var_done, 1)
    dve.wait_ge(ln.rooted, t + 1)
    ch.link(nc.vector.reciprocal(ln.rstd[:, t:t + 1], ln.root[:, t:t + 1]))
    ch.link(nc.vector.tensor_scalar(c.x[:, t, :], c.x[:, t, :], ln.mv[:, t, 0:1], ln.rstd[:, t:t + 1],
                                    ALU.subtract, ALU.mult))
    ch.link(nc.vector.tensor_tensor(c.x[:, t, :], c.x[:, t, :], ln.g[:], ALU.mult))
    ch.link(nc.vector.tensor_tensor(c.x[:, t, :], c.x[:, t, :], ln.b[:], ALU.add))


class Norm:

    def __init__(self, nc, ctx, name):
        def sb(part, shape):
            return ctx.enter_context(nc.sbuf_tensor(f"{name}_{part}", shape, F32))
        self.g, self.b = sb("g", [P, D]), sb("b", [P, D])
        self.stats, self.mv = sb("stats", [P, NT, 2, 6]), sb("mv", [P, NT, 2])
        self.var, self.root, self.rstd = sb("var", [P, NT]), sb("root", [P, NT]), sb("rstd", [P, NT])


def project_out(nc, c, m):
    w, ln = m.w_out, m.ln
    with phase(nc, ["projected", "dve_chain", "var_done", "rooted"]) as (block, projected, chain, ln.var_done,
                                                                       ln.rooted):
        @block.tensor
        def _(pe):
            for t in range(NT):
                for h in range(2):
                    for k in range(ND):
                        mm = nc.tensor.matmul(c.psum[:, 2 * t + h, :], m.mixed_t[:, k, t * P:(t + 1) * P],
                                              w[:, k, h * HALF:(h + 1) * HALF], start=k == 0, stop=k == ND - 1)
                    mm.then_inc(projected, 1)

        @block.vector
        def _(dve):
            ch = Chain(dve, chain)
            for t in range(NT):
                for h in range(2):
                    dve.wait_ge(projected, 2 * t + h + 1)
                    half = c.x[:, t, h * HALF:(h + 1) * HALF]
                    ins = nc.vector.scalar_tensor_tensor(out=half, in0=half, scalar=ALPHA,
                                                         in1=c.psum[:, 2 * t + h, :], op0=ALU.mult, op1=ALU.add)
                ch.link(ins)
                layer_norm_steps(nc, dve, ch, c, ln, t)

        @block.scalar
        def _(act):
            for t in range(NT):
                act.wait_ge(ln.var_done, t + 1)
                nc.scalar.activation(ln.root[:, t:t + 1], ln.var[:, t:t + 1], ACT.Sqrt).then_inc(ln.rooted, 1)


def residual_norm(nc, c, l, ffn, ln_g, ln_b):
    with ExitStack() as ctx:
        ln = Norm(nc, ctx, "ln2")
        offset = ctx.enter_context(nc.sbuf_tensor("ln2_offset", [P, NT], F32))
        with phase(nc, ["params_here", "dve_chain", "rooted", "stood", "scaled", "pooled"]) as (
                block, params_here, chain, rooted, stood, scaled, pooled):
            @block.sync
            def _(sp):
                sp.dma_start(ln.g[:], ln_g[bass.ds(l, 1)].broadcast_to([P, D])).then_inc(params_here, 16)
                sp.dma_start(ln.b[:], ln_b[bass.ds(l, 1)].broadcast_to([P, D])).then_inc(params_here, 16)

            @block.vector
            def _(dve):
                ch = Chain(dve, chain)
                for t in range(NT):
                    for h in range(2):
                        ins = nc.vector.bn_stats(ln.stats[:, t, h, :], ffn[:, t, h * HALF:(h + 1) * HALF])
                ch.link(ins)
                for t in range(NT):
                    ins = nc.vector.bn_aggr(ln.mv[:, t, :], ln.stats[:, t].rearrange("p h s -> p (h s)"))
                ch.link(ins)
                ch.link(nc.vector.tensor_scalar(ln.var[:], ln.mv[:, :, 1], LN_EPS, None, ALU.add))
                dve.wait_ge(rooted, 1)
                ch.link(nc.vector.reciprocal(ln.rstd[:], ln.root[:]))
                nc.vector.scalar_tensor_tensor(out=offset[:], in0=ln.mv[:, :, 0], scalar=-1.0, in1=ln.rstd[:],
                                               op0=ALU.mult, op1=ALU.mult).then_inc(stood, 1)
                dve.wait_ge(params_here, 32)
                for t in range(NT):
                    dve.wait_ge(scaled, t + 1)
                    ins = nc.vector.tensor_tensor(c.x[:, t, :], c.x[:, t, :], ln.g[:], ALU.mult)
                    if t < NT - 1:
                        ins.then_inc(pooled, 1)
                    else:
                        ch.link(ins)
                nc.vector.tensor_tensor(c.x[:, NT - 1, :], c.x[:, NT - 1, :], ln.b[:], ALU.add)

            @block.scalar
            def _(act):
                act.wait_ge(chain, 3)
                nc.scalar.activation(ln.root[:], ln.var[:], ACT.Sqrt).then_inc(rooted, 1)
                act.wait_ge(stood, 1)
                for t in range(NT):
                    nc.scalar.activation(c.x[:, t, :], ffn[:, t, :], ACT.Identity, bias=offset[:, t:t + 1],
                                         scale=ln.rstd[:, t:t + 1]).then_inc(scaled, 1)

            @block.gpsimd
            def _(pool):
                pool.wait_ge(params_here, 32)
                for t in range(NT - 1):
                    pool.wait_ge(pooled, t + 1)
                    nc.gpsimd.tensor_tensor(c.x[:, t, :], c.x[:, t, :], ln.b[:], ALU.add)


def route(nc, c, r, l, w_q, keys, x_hi, x_lo):
    with ExitStack() as ctx:
        def sb(name, shape, dt=F32):
            return ctx.enter_context(nc.sbuf_tensor(name, shape, dt))
        w = sb("rt_w", [P, 2, ND, P])
        key = sb("rt_key", [P, 2, P])
        key_t = sb("rt_key_t", [P, 2, P])
        q = sb("rt_q", [P, 2, S])
        score = sb("rt_score", [P, NT, 2, N_KEYS])
        score2 = sb("rt_score2", [P, NT, 2, N_KEYS])
        best = sb("rt_best", [P, NT, 2, TOPK])
        best_at = sb("rt_best_at", [P, NT, 2, TOPK], U32)
        best_key = sb("rt_best_key", [P, NT, 2, TOPK])
        WIDE, NARROW = 4, 4
        assert (WIDE + 1) * (NARROW + 1) > TOPK and WIDE == NARROW
        SPLIT = WIDE * TOPK
        CAND = SPLIT + (TOPK - WIDE) * NARROW
        cand = sb("rt_cand", [P, NT, CAND])
        cand2 = sb("rt_cand2", [P, NT, CAND])
        top = sb("rt_top", [P, NT, TOPK])
        top_at = sb("rt_top_at", [P, NT, TOPK], U32)
        part = sb("rt_part", [P, 2, NT, TOPK], U32)
        part_f = sb("rt_part_f", [P, 2, NT, TOPK])
        place = sb("rt_place", [P, NT, TOPK])
        before = sb("rt_before", [P, 2, NT, TOPK])
        rank = sb("rt_rank", [P, 2, NT, TOPK], BF16)
        hit = sb("rt_hit", [P, 2, NT, TOPK, TOPK], BF16)
        names = ["w_here0", "w_here1", "key_here", "keys_turned", "q_made", "keys_out", "q_out", "scored",
                 "score_out", "hit_made", "looked_up", "dve_chain", "passed", "x_turned", "x_copied",
                 "x_high"]
        PER = 21
        with phase(nc, names) as (block, w_here0, w_here1, key_here, keys_turned, q_made, keys_out, q_out, scored,
                                  score_out, hit_made, looked_up, chain, passed, x_turned,
                                  x_copied, x_high):
            w_here = (w_here0, w_here1)

            @block.sync
            def _(sp):
                with sp.Fori(0, P_HEADS) as h:
                    sp.wait_ge(keys_turned, h + CREDIT)
                    sp.dma_start(key[:], keys[bass.ds(l, 1), bass.ds(h, 1)]
                                 .rearrange("o h c n k -> n (o h c) k")).then_inc(key_here, 16)
                    for half in range(2):
                        sp.wait_ge(q_made, h * 2 + half + 1)
                        sp.dma_start(w[:, half], w_q[bass.ds(l, 1), :, bass.ds(h * (2 * P) + half * P, P)]
                                     .rearrange("o (c p) n -> p (o c) n", p=P)).then_inc(w_here[half], 16)

            @block.gpsimd
            def _(pool):
                nc.gpsimd.memset(hit[:], 0.0).then_inc(looked_up, 2)
                for sem, n in ((keys_turned, CREDIT), (q_made, 2), (keys_out, CREDIT), (score_out, CREDIT),
                               (chain, PER)):
                    pool.sem_inc(sem, n)
                with pool.Fori(0, P_HEADS) as h:
                    for half in range(2):
                        pool.wait_ge(hit_made, h * 2 + half + 1)
                        nc.gpsimd.tensor_tensor(
                            hit[:, half], hit[:, half],
                            best_key[:, :, half, :].unsqueeze(3).broadcast_to([P, NT, TOPK, TOPK]),
                            ALU.mult).then_inc(looked_up, 1)

            @block.tensor
            def _(pe):
                turn_x(nc, c, pe, x_turned, x_copied)
                with pe.Fori(0, P_HEADS) as h:
                    pe.wait_ge(key_here, h * 16 + 16)
                    pe.wait_ge(keys_out, h + CREDIT)
                    for half in range(2):
                        mm = nc.tensor.transpose(c.psum[:, 0, half * P:(half + 1) * P], key[:, half, :], c.ident[:])
                    mm.then_inc(keys_turned, 1)
                    for half in range(2):
                        pe.wait_ge(w_here[half], h * 16 + 16)
                        for k in range(ND):
                            mm = nc.tensor.matmul(c.psum[:, 1 + half, :], w[:, half, k, :],
                                                  c.xt[:, k, :], start=k == 0, stop=k == ND - 1)
                        mm.then_inc(q_made, 1)
                    pe.wait_ge(keys_out, h + 1 + CREDIT)
                    pe.wait_ge(q_out, h * 2 + 2)
                    pe.wait_ge(score_out, h + CREDIT)
                    for t in range(NT):
                        for half in range(2):
                            mm = nc.tensor.matmul(c.flat[:, 2048 + (2 * t + half) * P:2048 + (2 * t + half + 1) * P],
                                                  q[:, half, t * P:(t + 1) * P], key_t[:, half, :],
                                                  start=True, stop=True)
                    mm.then_inc(scored, 1)

            @block.scalar
            def _(act):
                take_x(nc, c, act, x_turned, x_copied)
                with act.Fori(0, P_HEADS) as h:
                    act.wait_ge(keys_turned, h + 1 + CREDIT)
                    nc.scalar.copy(key_t[:].rearrange("p c k -> p (c k)"), c.psum[:, 0, 0:2 * P]).then_inc(keys_out, 1)
                    for half in range(2):
                        act.wait_ge(q_made, h * 2 + half + 1 + 2)
                        nc.scalar.copy(q[:, half, :], c.psum[:, 1 + half, :]).then_inc(q_out, 1)
                    act.wait_ge(scored, h + 1)
                    act.wait_ge(chain, h * PER + 6)
                    nc.scalar.copy(score[:].rearrange("p t c n -> p (t c n)"),
                                   c.flat[:, 2048:2048 + NT * 2 * N_KEYS]).then_inc(score_out, 1)

            @block.vector
            def _(dve):
                ch = Chain(dve, chain, PER, passed)
                for k in range(ND):
                    dve.wait_ge(x_copied, k + 1)
                    nc.vector.tensor_copy(x_hi[:, k, :], c.xt[:, k, :]).then_inc(x_high, 1)
                    dve.wait_ge(x_high, k + 1)
                    nc.vector.tensor_tensor(x_lo[:, k, :], c.xt[:, k, :], x_hi[:, k, :].bitcast(F32), ALU.subtract)

                def top16(tiles):
                    groups = tiles[:len(tiles) // 2], tiles[len(tiles) // 2:]

                    def first_max(group):
                        for values, spare, out, at in group:
                            ins = nc.vector.max(out[:, 0:8], values)
                        return ch.mark(ins)

                    def first_places(group):
                        for values, spare, out, at in group:
                            nc.vector.max_index(at[:, 0:8], out[:, 0:8], values)

                    def take_out(group):
                        for values, spare, out, at in group:
                            ins = nc.vector.match_replace(spare, out[:, 0:8], values, NEG)
                        return ch.mark(ins)

                    def second_max(group):
                        for values, spare, out, at in group:
                            ins = nc.vector.max(out[:, 8:16], spare)
                        return ch.mark(ins)

                    def second_places(group):
                        for values, spare, out, at in group:
                            ins = nc.vector.max_index(at[:, 8:16], out[:, 8:16], spare)
                        return ins

                    maxed = [first_max(group) for group in groups]
                    taken = []
                    for group, done in zip(groups, maxed):
                        ch.after(done, True)
                        taken.append(take_out(group))
                    first_places(groups[0])
                    ch.after(taken[0], True)
                    maxed = [second_max(groups[0])]
                    first_places(groups[1])
                    ch.after(taken[1], True)
                    maxed.append(second_max(groups[1]))
                    for group, done in zip(groups, maxed):
                        ch.after(done, True)
                        ins = second_places(group)
                    return ch.mark(ins)

                def look_up(h, half):
                    dve.wait_ge(looked_up, h * 2 + half + 1)
                    nc.vector.tensor_reduce(
                        r.index[:, half, :, bass.ds(h, 1), :].rearrange("p t o k -> p t (o k)"),
                        hit[:, half].rearrange("p t a k -> p t k a"), AX_X, ALU.add)

                def make_hits(half):
                    nc.vector.tensor_tensor(
                        hit[:, half], rank[:, half].unsqueeze(2).broadcast_to([P, NT, TOPK, TOPK]),
                        c.count_rows[:].unsqueeze(1).broadcast_to([P, NT, TOPK, TOPK]),
                        ALU.is_equal).then_inc(hit_made, 1)

                with dve.Fori(0, P_HEADS) as h:
                    ch.turn(h, PER)
                    dve.wait_ge(score_out, h + 1 + CREDIT)
                    dve.sem_inc(passed, 1)
                    found = top16([(score[:, t, half, :], score2[:, t, half, :], best[:, t, half, :],
                                    best_at[:, t, half, :]) for t in range(NT) for half in range(2)])
                    nc.vector.tensor_tensor(
                        cand[:, :, 0:SPLIT].rearrange("p t (a b) -> p t a b", a=WIDE),
                        best[:, :, 0, 0:WIDE].unsqueeze(3).broadcast_to([P, NT, WIDE, TOPK]),
                        best[:, :, 1, :].unsqueeze(2).broadcast_to([P, NT, WIDE, TOPK]), ALU.add)
                    added = ch.mark(nc.vector.tensor_tensor(
                        cand[:, :, SPLIT:].rearrange("p t (a b) -> p t a b", b=NARROW),
                        best[:, :, 0, WIDE:].unsqueeze(3).broadcast_to([P, NT, TOPK - WIDE, NARROW]),
                        best[:, :, 1, 0:NARROW].unsqueeze(2).broadcast_to([P, NT, TOPK - WIDE, NARROW]), ALU.add))
                    ch.after(added, True)
                    chosen = top16([(cand[:, t], cand2[:, t], top[:, t, :], top_at[:, t, :]) for t in range(NT)])
                    ch.after(chosen)
                    nc.vector.tensor_scalar(part[:, 0], top_at[:], 4, None, ALU.logical_shift_right)
                    parted = ch.mark(nc.vector.tensor_scalar(part[:, 1], top_at[:], 2, None,
                                                             ALU.logical_shift_right))
                    nc.vector.tensor_copy(place[:], top_at[:])
                    look_up(h, 0)
                    ch.after(parted)
                    as_float = ch.mark(nc.vector.tensor_copy(part_f[:], part[:]))
                    look_up(h, 1)
                    ch.after(as_float)
                    ranked = ch.mark(nc.vector.scalar_tensor_tensor(
                        out=rank[:, 0], in0=part_f[:, 1], scalar=float(WIDE - SPLIT // NARROW), in1=part_f[:, 0],
                        op0=ALU.add, op1=ALU.max))
                    ch.after(found)
                    nc.vector.tensor_copy(best_key[:], best_at[:])
                    ch.after(ranked)
                    narrow = ch.mark(nc.vector.tensor_scalar(before[:, 0], rank[:, 0], float(NARROW),
                                                             float(SPLIT - WIDE * NARROW), ALU.mult, ALU.add))
                    make_hits(0)
                    ch.after(narrow)
                    smaller = ch.mark(nc.vector.scalar_tensor_tensor(
                        out=before[:, 1], in0=rank[:, 0], scalar=float(TOPK), in1=before[:, 0], op0=ALU.mult,
                        op1=ALU.min))
                    nc.vector.tensor_copy(r.top[:, :, bass.ds(h, 1), :].rearrange("p t o k -> p t (o k)"), top[:])
                    ch.after(smaller)
                    ch.after(ch.mark(nc.vector.tensor_tensor(rank[:, 1], place[:], before[:, 1], ALU.subtract)))
                    make_hits(1)
                ch.turned(P_HEADS)
                for half in range(2):
                    dve.wait_ge(looked_up, P_HEADS * 2 + half + 1)
                    nc.vector.tensor_reduce(r.index[:, half, :, P_HEADS, :],
                                            hit[:, half].rearrange("p t a k -> p t k a"), AX_X, ALU.add)


def gates(nc, c, r):
    with ExitStack() as ctx:
        def sb(name, shape):
            return ctx.enter_context(nc.sbuf_tensor(name, shape, F32))
        e = sb("gt_exp", [P, NT, P_HEADS, TOPK])
        total = sb("gt_total", [P, NT * P_HEADS])
        share = sb("gt_share", [P, NT * P_HEADS])
        with phase(nc, ["dve_chain", "exped", "turned", "evacuated"]) as (block, chain, exped, turned, evacuated):
            ef = e[:].rearrange("p t h k -> p (t h) k")
            shape = [P, NT * P_HEADS, TOPK]

            @block.vector
            def _(dve):
                ch = Chain(dve, chain)
                top = r.top[:].rearrange("p t h k -> p (t h) k")
                ch.link(nc.vector.tensor_tensor(ef, top, top[:, :, 0:1].broadcast_to(shape), ALU.subtract))
                dve.wait_ge(exped, 1)
                ch.link(nc.vector.tensor_reduce(total[:], ef, AX_X, ALU.add))
                ch.link(nc.vector.reciprocal(share[:], total[:]))
                ch.link(nc.vector.tensor_tensor(ef, ef, share[:].unsqueeze(2).broadcast_to(shape), ALU.mult))

            @block.scalar
            def _(act):
                act.wait_ge(chain, 1)
                nc.scalar.activation(e[:], e[:], ACT.Exp).then_inc(exped, 1)
                for n in range(3):
                    act.wait_ge(turned, n + 1)
                    nc.scalar.copy(r.turned[:, n, :], c.psum[:, n, :]).then_inc(evacuated, 1)

            @block.tensor
            def _(pe):
                for n, tile in enumerate((r.index[:, 0, :, 1:], r.index[:, 1, :, 1:], e)):
                    if n == 2:
                        pe.wait_ge(chain, 4)
                    for t in range(NT):
                        mm = nc.tensor.transpose(c.psum[:, n, t * P:(t + 1) * P],
                                                 tile[:, t].rearrange("p h k -> p (h k)"), c.ident[:])
                    mm.then_inc(turned, 1)


def spread_gates(nc, c, r, l, gate_dram, u, v, peer_u, peer_v):
    RING = 8
    GATE_RING = 4
    GROUPS = HALF_TILE // 4
    BODY = 8
    TURNS = S // 4 // BODY
    LAG = 3
    ONE_HOT_BY = "PADPAPAD"
    with ExitStack() as ctx:
        hot_j = ctx.enter_context(nc.sbuf_tensor("sg_hot_j", [P, RING, 4, N_KEYS], F32))
        gate_i = ctx.enter_context(nc.sbuf_tensor("sg_gate_i", [P, GATE_RING, 4, N_KEYS], F32))
        apart = ctx.enter_context(nc.sbuf_tensor("sg_apart", [P, 4, N_KEYS], F32))
        pool_j = ctx.enter_context(nc.sbuf_tensor("sg_pool_j", [P, BODY, 4], F32))
        out = [ctx.enter_context(nc.sbuf_tensor(f"sg_out{b}", [P, N_KEYS, HALF_TILE], F32)) for b in range(2)]
        by = {e: ONE_HOT_BY.count(e) for e in "PAD"}
        names = ["made", "hot_pool", "hot_act", "hot_dve", "staged", "apart_done", "passed", "multiplied", "evacuated",
                 "written", "out_free", "experts_here"]
        with phase(nc, names) as (block, made, hot_pool, hot_act, hot_dve, staged, apart_done, passed, multiplied,
                                  evacuated, written, out_free, experts_here):
            hot = {"P": hot_pool, "A": hot_act, "D": hot_dve}

            def nth(g):
                return ONE_HOT_BY[:g + 1].count(ONE_HOT_BY[g])

            @block.gpsimd
            def _(pool):
                pool.sem_inc(multiplied, RING)
                pool.sem_inc(evacuated, RING)
                pool.sem_inc(hot_pool, by["P"])
                pool.sem_inc(hot_act, by["A"])
                pool.sem_inc(out_free, 2)
                with pool.Fori(0, TURNS) as i:
                    for g in range(BODY):
                        if ONE_HOT_BY[g] != "P":
                            continue
                        pool.wait_ge(staged, i * by["P"] + nth(g))
                        pool.wait_ge(multiplied, i * BODY + (g + 1))
                        pool.sem_inc(passed, 1)
                        for n in range(4):
                            ins = nc.gpsimd.tensor_scalar(hot_j[:, g % RING, n, :], c.count_keys[:],
                                                          pool_j[:, g, n:n + 1], None, ALU.is_equal)
                        ins.then_inc(hot_pool, 1)

            @block.vector
            def _(dve):
                with dve.Fori(0, TURNS) as i:
                    for g in range(BODY):
                        at4 = bass.ds(i * (4 * BODY) + 4 * g, 4)
                        if ONE_HOT_BY[g] == "P":
                            dve.wait_ge(hot_pool, i * by["P"] + nth(g))
                            nc.vector.tensor_copy(pool_j[:, g, :], r.turned[:, 1, at4]).then_inc(staged, 1)
                        dve.wait_ge(multiplied, i * BODY + (g + 1 + RING - GATE_RING))
                        for n in range(4):
                            at = bass.ds(i * (4 * BODY) + (4 * g + n), 1)
                            ins = nc.vector.tensor_scalar(gate_i[:, g % GATE_RING, n, :], c.count_keys[:],
                                                          r.turned[:, 0, at], r.turned[:, 2, at],
                                                          ALU.is_equal, ALU.mult)
                        ins.then_inc(made, 1)
                        if ONE_HOT_BY[g] == "D":
                            nc.vector.tensor_tensor(
                                hot_j[:, g % RING], c.count_keys[:].unsqueeze(1).broadcast_to([P, 4, N_KEYS]),
                                r.turned[:, 1, at4].unsqueeze(2).broadcast_to([P, 4, N_KEYS]),
                                ALU.is_equal).then_inc(hot_dve, 1)

            @block.tensor
            def _(pe):
                with pe.Fori(0, TURNS) as i:
                    for g in range(BODY):
                        e = ONE_HOT_BY[g]
                        pe.wait_ge(made, i * BODY + (g + 1))
                        pe.wait_ge(hot[e], i * by[e] + (nth(g) + (0 if e == "D" else by[e])))
                        pe.wait_ge(evacuated, i * BODY + (g + 1))
                        for n in range(4):
                            mm = nc.tensor.matmul(c.psum[:, g % RING, n * P:(n + 1) * P], hot_j[:, g % RING, n, :],
                                                  gate_i[:, g % GATE_RING, n, :], start=True, stop=True)
                        mm.then_inc(multiplied, 1)

            @block.scalar
            def _(act):
                def one_hot(r2, n8, g):
                    done = n8 * by["A"] + nth(g)
                    act.wait_ge(multiplied, r2 * (2 * GROUPS) + (n8 * BODY + g + 1))
                    act.wait_ge(hot_act, r2 * PER + (done - 1 + by["A"]))
                    for n in range(4):
                        at = bass.ds(r2 * (2 * HALF_TILE) + (n8 * 4 * BODY + 4 * g + n), 1)
                        ins = nc.scalar.activation(apart[:, n, :], c.count_keys[:], ACT.Abs,
                                                   bias=r.turned[:, 1, at], scale=-1.0)
                    ins.then_inc(apart_done, 1)
                    act.wait_ge(apart_done, r2 * PER + done)
                    nc.scalar.activation(hot_j[:, g % RING], apart[:], ACT.Relu, bias=c.ones[:, 0:1],
                                         scale=-1.0).then_inc(hot_act, 1)

                def empty(r2, n):
                    act.wait_ge(multiplied, r2 * (2 * GROUPS) + (n + 1 + RING))
                    if n % GROUPS == 0:
                        act.wait_ge(out_free, r2 * 2 + (n // GROUPS + 1))
                    at = n % GROUPS * 4
                    nc.scalar.copy(out[n // GROUPS][:, :, at:at + 4],
                                   c.psum[:, n % RING, :].rearrange("p (n i) -> p i n", n=4)).then_inc(evacuated, 1)

                PER = 2 * GROUPS // BODY * by["A"]
                with act.Fori(0, HALF_TILES // 2) as r2:
                    for n in range(2 * GROUPS):
                        if ONE_HOT_BY[n % BODY] == "A":
                            one_hot(r2, n // BODY, n % BODY)
                        if n >= LAG:
                            empty(r2, n - LAG)
                    for n in range(2 * GROUPS - LAG, 2 * GROUPS):
                        empty(r2, n)

            @block.sync
            def _(sp):
                for s in range(EXPERT_SLOTS):
                    load_block(sp, peer_u, l, s, u, s, experts_here)
                    load_block(sp, peer_v, l, s, v, s, experts_here)
                with sp.Fori(0, HALF_TILES // 2) as r2:
                    for b in range(2):
                        sp.wait_ge(evacuated, r2 * (2 * GROUPS) + ((b + 1) * GROUPS + RING))
                        sp.dma_start(gate_dram[bass.ds(r2 * 2 + b, 1)].rearrange("o j i t -> (o j) (i t)"),
                                     out[b][:].rearrange("p i t -> p (i t)")).then_inc(written, 16)
                        sp.wait_ge(written, r2 * 32 + (16 * b + 16))
                        sp.sem_inc(out_free, 1)
                sp.wait_ge(experts_here, 2 * EXPERT_SLOTS * 16)


def load_block(sp, table, l, b, into, s, here):
    at = slice(b * P, (b + 1) * P) if isinstance(b, int) else bass.ds(b * P, P)
    sp.dma_start(into[:, s, :], table[bass.ds(l, 1), at].rearrange("o p d -> (o p) d")).then_inc(here, 16)


def experts(nc, c, l, x_hi, x_lo, u, v, ffn, peer_u, peer_v, gate_dram):
    GB = 2
    BODY = EXPERT_SLOTS
    TURNS = N_KEYS // BODY
    with ExitStack() as ctx:
        def sb(name, shape, dt=F32):
            return ctx.enter_context(nc.sbuf_tensor(name, shape, dt))
        gate = sb("ex_gate", [P, BODY, S])
        ut_hi, ut_lo = (sb(f"ex_ut_{n}", [P, 2, D], F32R) for n in ("hi", "lo"))
        v_hi, v_lo = (sb(f"ex_v_{n}", [P, 2, GB, D], F32R) for n in ("hi", "lo"))
        a_hi, a_lo = (sb(f"ex_a_{n}", [P, 2, GB, S], F32R) for n in ("hi", "lo"))
        act_out = sb("ex_act", [P, 2, S])
        a_full = sb("ex_a", [P, 2, S])
        names = ([f"u_here{s}" for s in range(BODY)] + [f"v_here{s}" for s in range(BODY)]
                 + [f"gate_here{s}" for s in range(BODY)]
                 + ["u_turned", "u_high", "u_low", "hidden", "gelued", "gated", "a_high", "a_low", "v_high", "v_low",
                    "summed", "added", "started"])
        with phase(nc, names) as (block, *sems):
            u_here, v_here, gate_here = sems[0:BODY], sems[BODY:2 * BODY], sems[2 * BODY:3 * BODY]
            (u_turned, u_high, u_low, hidden, gelued, gated, a_high, a_low, v_high, v_low,
             summed, added, started) = sems[3 * BODY:]


            @block.sync
            def _(sp):
                def load(i, s, first):
                    key = bass.ds(i * BODY + s, 1) if not first else slice(s, s + 1)
                    if not first:
                        sp.wait_ge(u_turned, i * (2 * BODY) + (2 * (s + 1) - 2 * BODY))
                        load_block(sp, peer_u, l, i * BODY + s, u, s, u_here[s])
                        sp.wait_ge(gated, i * BODY + (s + 1 - BODY))
                        sp.wait_ge(a_low, i * BODY + (s + 1 - BODY))
                    sp.dma_start(gate[:, s, :].rearrange("j (h t) -> j h t", h=HALF_TILES),
                                 gate_dram[:, :, key, :].rearrange("h j o t -> j h (o t)")).then_inc(gate_here[s], 16)
                    if not first:
                        sp.wait_ge(v_low, i * BODY + (s + 1 - BODY))
                        load_block(sp, peer_v, l, i * BODY + s, v, s, v_here[s])

                for s in range(BODY):
                    load(0, s, True)
                with sp.Fori(1, TURNS) as i:
                    for s in range(BODY):
                        load(i, s, False)

            @block.tensor
            def _(pe):
                def turn_u(i, s):
                    if not isinstance(i, int):
                        pe.wait_ge(u_here[s], i * 16)
                    for h in range(2):
                        if not (isinstance(i, int) and s == 0):
                            pe.wait_ge(u_low, i * (2 * BODY) + (2 * s + h - 1))
                        for k in range(4):
                            mm = nc.tensor.transpose(c.psum[:, h, k * P:(k + 1) * P],
                                                     u[:, s, (4 * h + k) * P:(4 * h + k + 1) * P], c.ident[:])
                        mm.then_inc(u_turned, 1)

                def hide(i, s):
                    pe.wait_ge(u_low, i * (2 * BODY) + (2 * s + 2))
                    if not (isinstance(i, int) and s < 2):
                        pe.wait_ge(gelued, i * BODY + (s - 1))
                    for k in range(ND):
                        at = slice(k * P, (k + 1) * P)
                        for n, (left, right) in enumerate(((ut_hi, x_hi), (ut_hi, x_lo), (ut_lo, x_hi))):
                            mm = nc.tensor.matmul(c.psum[:, 2 + s % 2, :], left[:, s % 2, at], right[:, k, :],
                                                  start=k + n == 0, stop=k == ND - 1 and n == 2)
                    mm.then_inc(hidden, 1)

                def add_up(i, par, part):
                    if part == 0:
                        pe.wait_ge(a_low, i * BODY + GB * (par + 1))
                        pe.wait_ge(v_low, i * BODY + GB * (par + 1))
                    for t in (2 * part, 2 * part + 1):
                        tok = slice(t * P, (t + 1) * P)
                        for h in range(2):
                            n = 2 * t + h
                            if not (isinstance(i, int) and par == 0 and n < 4):
                                pe.wait_ge(added, i * 16 + (8 * par + n - 3))
                            half = slice(h * HALF, (h + 1) * HALF)
                            for b in range(GB):
                                for m, (left, right) in enumerate(((a_hi, v_hi), (a_hi, v_lo), (a_lo, v_hi))):
                                    mm = nc.tensor.matmul(c.psum[:, 4 + n % 4, :], left[:, par, b, tok],
                                                          right[:, par, b, half], start=b + m == 0,
                                                          stop=b == GB - 1 and m == 2)
                            mm.then_inc(summed, 1)

                def turn(i, first):
                    if first:
                        turn_u(i, 0)
                    for s, (di, par, part) in enumerate(((-1, 0, 1), (-1, 1, 0), (-1, 1, 1), (0, 0, 0))):
                        if not first:
                            turn_u(i, s)
                        elif s + 1 < BODY:
                            turn_u(i, s + 1)
                        if not first or di == 0:
                            add_up(i + di, par, part)
                        hide(i, s)

                turn(0, True)
                with pe.Fori(1, TURNS) as i:
                    turn(i, False)
                add_up(TURNS - 1, 0, 1)
                add_up(TURNS - 1, 1, 0)
                add_up(TURNS - 1, 1, 1)

            def free_group(eng, i, s, first):
                if not first:
                    eng.wait_ge(summed, i * 16 + (8 * (s // GB) - 8))

            @block.scalar
            def _(act):
                def high_u(i, s):
                    for h in range(2):
                        act.wait_ge(u_turned, i * (2 * BODY) + (2 * s + h + 1))
                        nc.scalar.copy(ut_hi[:, s % 2, h * HALF:(h + 1) * HALF],
                                       c.psum[:, h, :]).then_inc(u_high, 1)

                def turn(i, first):
                    if first:
                        high_u(i, 0)
                    for s in range(BODY):
                        if not first:
                            high_u(i, s)
                        elif s + 1 < BODY:
                            high_u(i, s + 1)
                        if not first:
                            act.wait_ge(v_here[s], i * 16)
                        free_group(act, i, s, first)
                        nc.scalar.copy(v_hi[:, s // GB, s % GB, :], v[:, s, :]).then_inc(v_high, 1)
                        act.wait_ge(hidden, i * BODY + (s + 1))
                        if not (first and s < 2):
                            act.wait_ge(gated, i * BODY + (s - 1))
                            act.wait_ge(a_high, i * BODY + (s - 1))
                        nc.scalar.activation(act_out[:, s % 2, :], c.psum[:, 2 + s % 2, :],
                                             ACT.Gelu).then_inc(gelued, 1)

                turn(0, True)
                with act.Fori(1, TURNS) as i:
                    turn(i, False)

            @block.gpsimd
            def _(pool):
                def turn(i, first):
                    for s in range(BODY):
                        pool.wait_ge(gate_here[s], i * 16 + 16)
                        pool.wait_ge(gelued, i * BODY + (s + 1))
                        if not (first and s < 2):
                            pool.wait_ge(a_low, i * BODY + (s - 1))
                        nc.gpsimd.tensor_tensor(a_full[:, s % 2, :], act_out[:, s % 2, :], gate[:, s, :],
                                                ALU.mult).then_inc(gated, 1)

                turn(0, True)
                with pool.Fori(1, TURNS) as i:
                    turn(i, False)

            @block.vector
            def _(dve):
                def add(i, first_sum):
                    for n in range(first_sum, first_sum + 4):
                        dve.wait_ge(summed, i * 16 + (n + 1))
                        at = ffn[:, (n % 8) // 2, (n % 2) * HALF:(n % 2 + 1) * HALF]
                        nc.vector.tensor_tensor(at, at, c.psum[:, 4 + n % 4, :], ALU.add).then_inc(added, 1)

                def low_u(i, s):
                    for h in range(2):
                        dve.wait_ge(u_high, i * (2 * BODY) + (2 * s + h + 1))
                        at = slice(h * HALF, (h + 1) * HALF)
                        nc.vector.tensor_tensor(ut_lo[:, s % 2, at], c.psum[:, h, :],
                                                ut_hi[:, s % 2, at].bitcast(F32), ALU.subtract).then_inc(u_low, 1)

                def turn(i, first):
                    if first:
                        low_u(i, 0)
                    for s in range(BODY):
                        if not first:
                            low_u(i, s)
                        elif s + 1 < BODY:
                            low_u(i, s + 1)
                            if s == 0:
                                nc.vector.tensor_scalar(ffn[:].rearrange("p t d -> p (t d)"),
                                                        c.x[:].rearrange("p t d -> p (t d)"), ALPHA, None,
                                                        ALU.mult).then_inc(started, 1)
                        if first and s == 3:
                            dve.wait_ge(started, 1)
                        if not first or s == 3:
                            add(i, 4 * s - 12)
                        dve.wait_ge(v_high, i * BODY + (s + 1))
                        nc.vector.tensor_tensor(v_lo[:, s // GB, s % GB, :], v[:, s, :],
                                                v_hi[:, s // GB, s % GB, :].bitcast(F32),
                                                ALU.subtract).then_inc(v_low, 1)
                        dve.wait_ge(gate_here[s], i * 16 + 16)
                        dve.wait_ge(gelued, i * BODY + (s + 1))
                        nc.vector.tensor_tensor(a_hi[:, s // GB, s % GB, :], act_out[:, s % 2, :], gate[:, s, :],
                                                ALU.mult).then_inc(a_high, 1)
                        dve.wait_ge(a_high, i * BODY + (s + 1))
                        dve.wait_ge(gated, i * BODY + (s + 1))
                        nc.vector.tensor_tensor(a_lo[:, s // GB, s % GB, :], a_full[:, s % 2, :],
                                                a_hi[:, s // GB, s % GB, :].bitcast(F32),
                                                ALU.subtract).then_inc(a_low, 1)

                turn(0, True)
                with dve.Fori(1, TURNS) as i:
                    turn(i, False)
                for first_sum in (4, 8, 12):
                    add(TURNS - 1, first_sum)


class Tiles:
    pass


def build(nc, x, w_in, g_cq, w_uq, g_ckv, w_ukv, w_o, ln1_g, ln1_b, peer_wq, peer_keys, peer_u, peer_v,
          ln2_g, ln2_b, rope_cos, rope_sin, out, gate_dram):
    with ExitStack() as whole:
        def tile(ctx, name, shape, dt=F32):
            return ctx.enter_context(nc.sbuf_tensor(name, shape, dt))

        c = Tiles()
        c.x = tile(whole, "x", [P, NT, D])
        c.xt = tile(whole, "xt", [P, ND, S])
        c.ident = tile(whole, "ident", [P, P])
        c.neg_ones = tile(whole, "neg_ones", [P, P])
        c.neg_tri = tile(whole, "neg_tri", [P, P])
        c.neg_ones_r = tile(whole, "neg_ones_r", [P, P], F32R)
        c.neg_tri_r = tile(whole, "neg_tri_r", [P, P], F32R)
        c.neg_mask = tile(whole, "neg_mask", [P, P])
        c.count_keys = tile(whole, "count_keys", [P, N_KEYS])
        c.count_rows = tile(whole, "count_rows", [P, TOPK, TOPK], BF16)
        c.ones = tile(whole, "ones", [P, 1])
        c.cos = tile(whole, "cos", [P, S])
        c.sin = tile(whole, "sin", [P, S])
        c.psum = whole.enter_context(nc.psum_tensor("banks", [P, 8, 512], F32))
        c.flat = c.psum[:].rearrange("p b n -> p (b n)")

        make_constants(nc, c, x, rope_cos, rope_sin)
        with nc.Fori(0, DEPTH) as l:
            with ExitStack() as ctx:
                m = Tiles()
                m.mixed_t = tile(ctx, "mixed_t", [P, ND, S])
                m.lat_t = tile(ctx, "lat_t", [P, 3, S])
                m.k_full = tile(ctx, "k_full", [P, 2, S])
                m.la_wq = tile(ctx, "la_wq", [P, 2, 2, QK])
                m.la_wq_swap = tile(ctx, "la_wq_swap", [P, 2, 2, ROPE])
                m.la_wk = tile(ctx, "la_wk", [P, 2, HD])
                m.la_wkv = tile(ctx, "la_wkv", [P, 2 * PAIRS, 2, HD])
                with ExitStack() as until_latent:
                    m.sb_w = tile(until_latent, "sb_w", [P, 3, ND, P])
                    m.x_hi, m.x_lo = (tile(until_latent, f"mix_x_{n}", [P, ND, S], F32R) for n in ("hi", "lo"))
                    latents(nc, c, m, l, w_in, g_cq, g_ckv)
                    stick_breaking(nc, c, m, l, w_in, w_uq, w_ukv)
                m.w_out = tile(ctx, "w_out", [P, ND, D])
                m.ln = Norm(nc, ctx, "ln1")
                latent_attention(nc, c, m, l, w_uq, w_ukv, w_o, ln1_g, ln1_b)
                project_out(nc, c, m)
            with ExitStack() as ctx:
                x_hi, x_lo = (tile(ctx, f"x_{n}", [P, ND, S], F32R) for n in ("hi", "lo"))
                u = tile(ctx, "ex_u", [P, EXPERT_SLOTS, D])
                v = tile(ctx, "ex_v", [P, EXPERT_SLOTS, D])
                with ExitStack() as until_experts:
                    r = Tiles()
                    r.top = tile(until_experts, "top", [P, NT, P_HEADS, TOPK])
                    r.index = tile(until_experts, "index", [P, 2, NT, 1 + P_HEADS, TOPK])
                    r.turned = tile(until_experts, "picks_t", [P, 3, S])
                    route(nc, c, r, l, peer_wq, peer_keys, x_hi, x_lo)
                    gates(nc, c, r)
                    spread_gates(nc, c, r, l, gate_dram, u, v, peer_u, peer_v)
                ffn = tile(ctx, "ffn", [P, NT, D])
                experts(nc, c, l, x_hi, x_lo, u, v, ffn, peer_u, peer_v, gate_dram)
                residual_norm(nc, c, l, ffn, ln2_g, ln2_b)
        store_x(nc, c, out)


_INS = ["x", "w_in", "g_cq", "w_uq", "g_ckv", "w_ukv", "w_o", "ln1_g", "ln1_b", "peer_wq", "peer_keys",
        "peer_u", "peer_v", "ln2_g", "ln2_b"]


def rope_tables():
    inv = (np.float32(10000.0) ** (-np.arange(0, ROPE, 2, dtype=np.float32) / np.float32(ROPE))).astype(np.float32)
    angle = inv[:, None] * np.arange(S, dtype=np.float32)[None, :]
    cos, sin = np.cos(angle, dtype=np.float32), np.sin(angle, dtype=np.float32)
    return np.concatenate([cos, cos]), np.concatenate([-sin, sin])


def kernel(**inputs):
    import concourse.bacc as bacc
    from concourse.bass_utils import run_bass_kernel_spmd

    nc = bacc.Bacc("TRN2", target_bir_lowering=False, num_devices=1)
    arrays, args = {}, []
    for name in _INS:
        arrays[f"in_{name}_dram"] = np.ascontiguousarray(inputs[name])
    arrays["rope_cos_dram"], arrays["rope_sin_dram"] = rope_tables()
    for name, a in arrays.items():
        args.append(nc.dram_tensor(name, a.shape, mybir.dt.from_np(a.dtype), kind="ExternalInput").ap())
    args.append(nc.dram_tensor("out_0_dram", (1, S, D), F32, kind="ExternalOutput").ap())
    args.append(nc.dram_tensor("gates_dram", (HALF_TILES, N_KEYS, N_KEYS, HALF_TILE), F32).ap())
    build(nc, *args)
    return run_bass_kernel_spmd(nc, [arrays], core_ids=[0]).results[0]["out_0_dram"]
```
